# Optimizing a Trainium2 kernel written in Bass

```python
import math
import jax
import jax.numpy as jnp
from jax import lax
import numpy as np

D_MODEL = 1024
BATCH = 1
SEQ = 512
DEPTH = 2

F32 = jnp.float32
NORM_EPS = 1e-6
ROPE_THETA = 10000.0
HEAD_DIM = 64
ATTN_BLOCK = 128
A_HEADS = 8
A_KV_HEADS = 2
IDX_HEADS = 8
IDX_DIM = 64
A_TOPK_MAX = 256
B_WIDTH = 512
B_GROUP = 16
B_GROUPS = B_WIDTH // B_GROUP
B_STATE = 64
C_HEADS = 8
C_KV_HEADS = 2
CMP_LEN = 32
CMP_STRIDE = 16
CMP_HIDDEN = 256
SLC_LEN = 64
SLC_TOPN = 16
WIN = 512
C_BLOCK = 64
FORCE_SCORE = 1e9
D_HEADS = 4
D_KDIM = 64
D_VDIM = 128
GATE_RANK = 16
GATE_TAU = 16.0
GLA_CHUNK = 32
PEER_HEADS = 8
PEER_KEYS = 128
PEER_EXPERTS = PEER_KEYS * PEER_KEYS
PEER_QDIM = 256
PEER_TOPK = 16
PEER_BLOCK = 128

MIX_WIDTH = A_HEADS * HEAD_DIM + B_WIDTH
EVEN_COLS = (A_HEADS * HEAD_DIM, A_KV_HEADS * HEAD_DIM, A_KV_HEADS * HEAD_DIM,
             IDX_HEADS * IDX_DIM, IDX_DIM, IDX_HEADS, B_WIDTH)
ODD_COLS = (C_HEADS * HEAD_DIM,) + (C_KV_HEADS * HEAD_DIM,) * 6 + (
    C_HEADS * 3, D_HEADS * D_KDIM, D_HEADS * D_KDIM, D_HEADS * D_VDIM, GATE_RANK, D_HEADS * D_VDIM)

kernel_name = 'hybrid_dsa_s5_nsa_gla_peer'

def rms_norm(x, gain):
    xf = x.astype(F32)
    y = xf * lax.rsqrt(jnp.mean(xf * xf, axis=-1, keepdims=True) + NORM_EPS)
    return (y * gain.astype(F32)).astype(x.dtype)

def rope(x, pos):
    half = x.shape[-1] // 2
    inv_freq = ROPE_THETA ** (-jnp.arange(half, dtype=F32) / half)
    ang = pos.astype(F32)[:, None] * inv_freq[None, :]
    cos = jnp.cos(ang)[:, None, :]
    sin = jnp.sin(ang)[:, None, :]
    xf = x.astype(F32)
    x1, x2 = xf[..., :half], xf[..., half:]
    return jnp.concatenate([x1 * cos - x2 * sin, x1 * sin + x2 * cos], axis=-1).astype(x.dtype)

def masked_softmax(s, mask):
    s = jnp.where(mask, s.astype(F32), -1e30)
    m = jnp.max(s, axis=-1, keepdims=True)
    p = jnp.exp(s - m) * mask
    return p / jnp.maximum(jnp.sum(p, axis=-1, keepdims=True), 1e-30)

def split_cols(h, sizes):
    return jnp.split(h, np.cumsum(sizes)[:-1].tolist(), axis=-1)

def to_blocks(t, blk):
    return t.reshape(t.shape[0], t.shape[1] // blk, blk, *t.shape[2:]).swapaxes(0, 1)

def dsa_attention(q, k, v, iq, ik, iw, q_gain, k_gain, pos):
    bsz, seq = q.shape[:2]
    topk = min(A_TOPK_MAX, seq // 4)
    rep = A_HEADS // A_KV_HEADS
    q = rope(rms_norm(q, q_gain), pos).astype(F32) * HEAD_DIM ** -0.5
    k = rope(rms_norm(k, k_gain), pos).astype(F32)
    v = v.astype(F32)
    iq = rope(iq, pos).astype(F32) * IDX_DIM ** -0.5
    ik = rope(ik[:, :, None, :], pos)[:, :, 0, :].astype(F32)
    iw = iw.astype(F32) * IDX_HEADS ** -0.5
    key_pos = jnp.arange(seq)
    gather = jax.vmap(lambda t, idx: t[idx])

    def block(args):
        qb, iqb, iwb, start = args
        tq = start + jnp.arange(ATTN_BLOCK)
        rel = jax.nn.relu(jnp.einsum('bqhd,bsd->bqhs', iqb, ik))
        score = jnp.einsum('bqh,bqhs->bqs', iwb, rel)
        causal = key_pos[None, :] <= tq[:, None]
        score = jnp.where(causal[None], score, -jnp.inf)
        _, sel = lax.top_k(score, topk)
        valid = sel <= tq[None, :, None]
        k_sel = gather(k, sel)
        v_sel = gather(v, sel)
        qg = qb.reshape(bsz, ATTN_BLOCK, A_KV_HEADS, rep, HEAD_DIM)
        s = jnp.einsum('bqgrd,bqkgd->bqgrk', qg, k_sel)
        p = masked_softmax(s, valid[:, :, None, None, :])
        o = jnp.einsum('bqgrk,bqkgd->bqgrd', p, v_sel)
        return o.reshape(bsz, ATTN_BLOCK, A_HEADS * HEAD_DIM)

    starts = jnp.arange(seq // ATTN_BLOCK) * ATTN_BLOCK
    out = lax.map(block, (to_blocks(q, ATTN_BLOCK), to_blocks(iq, ATTN_BLOCK),
                          to_blocks(iw, ATTN_BLOCK), starts))
    return out.swapaxes(0, 1).reshape(bsz, seq, A_HEADS * HEAD_DIM)

def s5_ssm(u, log_dt, a_re, a_im, b_re, b_im, c_re, c_im, d_skip, w_glu, b_glu):
    bsz, seq = u.shape[:2]
    uf = u.astype(F32).reshape(bsz, seq, B_GROUPS, B_GROUP)
    dt = jnp.exp(log_dt.astype(F32))[:, None]
    lr, li = a_re.astype(F32), a_im.astype(F32)
    mag = jnp.exp(dt * lr)
    ab_re = mag * jnp.cos(dt * li)
    ab_im = mag * jnp.sin(dt * li)
    den = lr * lr + li * li
    f_re = ((ab_re - 1.0) * lr + ab_im * li) / den
    f_im = (ab_im * lr - (ab_re - 1.0) * li) / den
    br, bi = b_re.astype(F32), b_im.astype(F32)
    bb_re = f_re[..., None] * br - f_im[..., None] * bi
    bb_im = f_re[..., None] * bi + f_im[..., None] * br
    x_re = jnp.einsum('gpc,bsgc->bsgp', bb_re, uf)
    x_im = jnp.einsum('gpc,bsgc->bsgp', bb_im, uf)
    a_re_t = jnp.broadcast_to(ab_re, x_re.shape)
    a_im_t = jnp.broadcast_to(ab_im, x_im.shape)

    def combine(e1, e2):
        a1r, a1i, b1r, b1i = e1
        a2r, a2i, b2r, b2i = e2
        return (a1r * a2r - a1i * a2i, a1r * a2i + a1i * a2r,
                a2r * b1r - a2i * b1i + b2r, a2r * b1i + a2i * b1r + b2i)

    _, _, h_re, h_im = lax.associative_scan(combine, (a_re_t, a_im_t, x_re, x_im), axis=1)
    y = (jnp.einsum('gcp,bsgp->bsgc', c_re.astype(F32), h_re)
         - jnp.einsum('gcp,bsgp->bsgc', c_im.astype(F32), h_im)
         + d_skip.astype(F32) * uf)
    y = jax.nn.gelu(y.reshape(bsz, seq, B_WIDTH))
    return y * jax.nn.sigmoid(y @ w_glu.astype(F32) + b_glu.astype(F32))

def compress_blocks(t, cmp_pos, w1, w2):
    bsz, seq, groups, dh = t.shape
    n_cmp = (seq - CMP_LEN) // CMP_STRIDE + 1
    idx = jnp.arange(n_cmp)[:, None] * CMP_STRIDE + jnp.arange(CMP_LEN)[None, :]
    blocks = t.astype(F32)[:, idx] + cmp_pos.astype(F32)[:, None, :]
    blocks = blocks.transpose(0, 1, 3, 2, 4).reshape(bsz, n_cmp, groups, CMP_LEN * dh)
    return jax.nn.gelu(blocks @ w1.astype(F32)) @ w2.astype(F32)

def nsa_attention(q, k_cmp, v_cmp, k_slc, v_slc, k_win, v_win, gate_logits,
                  q_gain, k_gain, cmp_pos, k_w1, k_w2, v_w1, v_w2, pos):
    bsz, seq = q.shape[:2]
    rep = C_HEADS // C_KV_HEADS
    n_cmp = (seq - CMP_LEN) // CMP_STRIDE + 1
    n_slc = seq // SLC_LEN
    top_n = min(SLC_TOPN, n_slc)
    q = rope(rms_norm(q, q_gain), pos).astype(F32) * HEAD_DIM ** -0.5
    cmp_end = jnp.arange(n_cmp) * CMP_STRIDE + (CMP_LEN - 1)
    kc = rope(rms_norm(compress_blocks(k_cmp, cmp_pos, k_w1, k_w2), k_gain), cmp_end)
    vc = compress_blocks(v_cmp, cmp_pos, v_w1, v_w2)
    ks = rope(rms_norm(k_slc, k_gain), pos).astype(F32)
    ks = ks.reshape(bsz, n_slc, SLC_LEN, C_KV_HEADS, HEAD_DIM).transpose(0, 3, 1, 2, 4)
    vs = v_slc.astype(F32).reshape(bsz, n_slc, SLC_LEN, C_KV_HEADS, HEAD_DIM).transpose(0, 3, 1, 2, 4)
    pad = ((0, 0), (WIN, 0), (0, 0), (0, 0))
    kw = jnp.pad(rope(rms_norm(k_win, k_gain), pos).astype(F32), pad)
    vw = jnp.pad(v_win.astype(F32), pad)
    gates = jax.nn.sigmoid(gate_logits.astype(F32))
    ratio = SLC_LEN // CMP_STRIDE
    span = CMP_LEN // CMP_STRIDE
    off = jnp.arange(n_cmp)[:, None] - ratio * jnp.arange(n_slc)[None, :]
    cmp_to_slc = jnp.maximum(
        jnp.minimum(ratio - 1, off) - jnp.maximum(0, off - span + 1) + 1, 0).astype(F32)
    slc_ids = jnp.arange(n_slc)
    tok_off = jnp.arange(SLC_LEN)
    win_off = jnp.arange(WIN + C_BLOCK)
    gather = jax.vmap(jax.vmap(lambda t, idx: t[idx]))

    def block(args):
        qb, gb, start = args
        tq = start + jnp.arange(C_BLOCK)
        qg = qb.reshape(bsz, C_BLOCK, C_KV_HEADS, rep, HEAD_DIM)
        gb = gb.reshape(bsz, C_BLOCK, C_KV_HEADS, rep, 3)
        s_c = jnp.einsum('bqgrd,bcgd->bqgrc', qg, kc)
        p_c = masked_softmax(s_c, (cmp_end[None, :] <= tq[:, None])[None, :, None, None, :])
        o_c = jnp.einsum('bqgrc,bcgd->bqgrd', p_c, vc)
        imp = jnp.einsum('bqgrc,cj->bqgj', p_c, cmp_to_slc)
        cur = tq // SLC_LEN
        forced = (slc_ids[None, :] == cur[:, None]) | (slc_ids[None, :] == 0)
        admissible = slc_ids[None, :] <= cur[:, None]
        imp = jnp.where(forced[None, :, None, :], FORCE_SCORE, imp)
        imp = jnp.where(admissible[None, :, None, :], imp, -jnp.inf)
        _, sel = lax.top_k(imp, top_n)
        sel_g = sel.transpose(0, 2, 1, 3)
        k_sel = gather(ks, sel_g)
        v_sel = gather(vs, sel_g)
        s_s = jnp.einsum('bqgrd,bgqnld->bqgrnl', qg, k_sel)
        kpos = sel[..., None] * SLC_LEN + tok_off
        smask = (kpos <= tq[None, :, None, None, None]).reshape(bsz, C_BLOCK, C_KV_HEADS, 1, -1)
        p_s = masked_softmax(s_s.reshape(bsz, C_BLOCK, C_KV_HEADS, rep, -1), smask)
        o_s = jnp.einsum('bqgrnl,bgqnld->bqgrd', p_s.reshape(s_s.shape), v_sel)
        kwb = lax.dynamic_slice_in_dim(kw, start, WIN + C_BLOCK, axis=1)
        vwb = lax.dynamic_slice_in_dim(vw, start, WIN + C_BLOCK, axis=1)
        wpos = start - WIN + win_off
        wmask = ((wpos[None, :] <= tq[:, None]) & (wpos[None, :] > tq[:, None] - WIN)
                 & (wpos[None, :] >= 0))
        s_w = jnp.einsum('bqgrd,bkgd->bqgrk', qg, kwb)
        p_w = masked_softmax(s_w, wmask[None, :, None, None, :])
        o_w = jnp.einsum('bqgrk,bkgd->bqgrd', p_w, vwb)
        o = gb[..., 0:1] * o_c + gb[..., 1:2] * o_s + gb[..., 2:3] * o_w
        return o.reshape(bsz, C_BLOCK, C_HEADS * HEAD_DIM)

    starts = jnp.arange(seq // C_BLOCK) * C_BLOCK
    out = lax.map(block, (to_blocks(q, C_BLOCK), to_blocks(gates, C_BLOCK), starts))
    return out.swapaxes(0, 1).reshape(bsz, seq, C_HEADS * HEAD_DIM)

def gla_attention(q, k, v, g_low, r, w_gate, b_gate, o_gain):
    bsz, seq = q.shape[:2]
    n_chunk = seq // GLA_CHUNK
    logit = g_low.astype(F32) @ w_gate.astype(F32) + b_gate.astype(F32)
    log_a = jax.nn.log_sigmoid(logit) / GATE_TAU

    def chunks(t):
        return t.astype(F32).reshape(bsz, n_chunk, GLA_CHUNK, D_HEADS, -1).transpose(0, 3, 1, 2, 4)

    qc = chunks(q) * D_KDIM ** -0.5
    kc, vc, gc = chunks(k), chunks(v), chunks(log_a)
    bcum = jnp.cumsum(gc, axis=3)
    blast = bcum[:, :, :, -1:, :]
    q_dec = qc * jnp.exp(bcum)
    k_inv = kc * jnp.exp(-bcum)
    causal = jnp.tril(jnp.ones((GLA_CHUNK, GLA_CHUNK), dtype=bool))
    att = jnp.where(causal, jnp.einsum('bhncd,bhnsd->bhncs', q_dec, k_inv), 0.0)
    o_intra = jnp.einsum('bhncs,bhnse->bhnce', att, vc)
    upd = jnp.einsum('bhncd,bhnce->bhnde', kc * jnp.exp(blast - bcum), vc)
    decay = jnp.exp(blast[:, :, :, 0, :])

    def step(state, inp):
        dec, u = inp
        return dec[..., None] * state + u, state

    init = jnp.zeros((bsz, D_HEADS, D_KDIM, D_VDIM), F32)
    _, prev = lax.scan(step, init, (jnp.moveaxis(decay, 2, 0), jnp.moveaxis(upd, 2, 0)))
    o_inter = jnp.einsum('bhncd,nbhde->bhnce', q_dec, prev)
    o = (o_intra + o_inter).transpose(0, 2, 3, 1, 4).reshape(bsz, seq, D_HEADS, D_VDIM)
    o = rms_norm(o, o_gain).reshape(bsz, seq, D_HEADS * D_VDIM)
    return o * jax.nn.silu(r.astype(F32))

def peer_ffn(x, wq, subkeys, u_tab, v_tab):
    bsz, seq, dm = x.shape
    xt = x.reshape(bsz * seq // PEER_BLOCK, PEER_BLOCK, dm)
    half = PEER_QDIM // 2

    def block(xb):
        q = (xb @ wq).reshape(PEER_BLOCK, PEER_HEADS, 2, half)
        s = jnp.einsum('thpc,hpkc->thpk', q, subkeys).astype(F32)
        s1, i1 = lax.top_k(s[:, :, 0], PEER_TOPK)
        s2, i2 = lax.top_k(s[:, :, 1], PEER_TOPK)
        cand = (s1[..., :, None] + s2[..., None, :]).reshape(PEER_BLOCK, PEER_HEADS, -1)
        cand_id = (i1[..., :, None] * PEER_KEYS + i2[..., None, :]).reshape(PEER_BLOCK, PEER_HEADS, -1)
        top_s, top_pos = lax.top_k(cand, PEER_TOPK)
        expert = jnp.take_along_axis(cand_id, top_pos, axis=-1).reshape(PEER_BLOCK, -1)
        gate = jax.nn.softmax(top_s, axis=-1).reshape(PEER_BLOCK, -1)
        h = jax.nn.gelu(jnp.einsum('td,ted->te', xb, u_tab[expert]).astype(F32))
        return jnp.einsum('te,ted->td', gate * h, v_tab[expert].astype(F32))

    return lax.map(block, xt).reshape(bsz, seq, dm)

def even_mixer(h, pos, w_in, q_gain, k_gain, log_dt, a_re, a_im, b_re, b_im,
               c_re, c_im, d_skip, w_glu, b_glu, w_out):
    bsz, seq = h.shape[:2]
    q, k, v, iq, ik, iw, u = split_cols(h @ w_in, EVEN_COLS)
    heads = lambda t, n: t.reshape(bsz, seq, n, -1)
    o_a = dsa_attention(heads(q, A_HEADS), heads(k, A_KV_HEADS), heads(v, A_KV_HEADS),
                        heads(iq, IDX_HEADS), ik, iw, q_gain, k_gain, pos)
    o_b = s5_ssm(u, log_dt, a_re, a_im, b_re, b_im, c_re, c_im, d_skip, w_glu, b_glu)
    return jnp.concatenate([o_a, o_b], axis=-1) @ w_out.astype(F32)

def odd_mixer(h, pos, w_in, q_gain, k_gain, cmp_pos, k_w1, k_w2, v_w1, v_w2,
              w_gate, b_gate, o_gain, w_out):
    bsz, seq = h.shape[:2]
    (q, kc, vc, ks, vs, kw, vw, gl, gq, gk, gv, glow, gr) = split_cols(h @ w_in, ODD_COLS)
    heads = lambda t, n: t.reshape(bsz, seq, n, -1)
    o_c = nsa_attention(heads(q, C_HEADS), heads(kc, C_KV_HEADS), heads(vc, C_KV_HEADS),
                        heads(ks, C_KV_HEADS), heads(vs, C_KV_HEADS), heads(kw, C_KV_HEADS),
                        heads(vw, C_KV_HEADS), heads(gl, C_HEADS), q_gain, k_gain,
                        cmp_pos, k_w1, k_w2, v_w1, v_w2, pos)
    o_d = gla_attention(gq, gk, gv, glow, gr, w_gate, b_gate, o_gain)
    return jnp.concatenate([o_c, o_d], axis=-1) @ w_out.astype(F32)

def setup_inputs(seed: int = 0) -> dict:
    key = jax.random.key(seed)
    keys = iter(list(jax.random.split(key, 64)))

    def normal(shape, scale):
        return jax.random.normal(next(keys), shape, F32) * scale

    def gain(n):
        return 1.0 + normal((n,), 0.02)

    def peer_params():
        return (normal((D_MODEL, PEER_HEADS * PEER_QDIM), D_MODEL ** -0.5),
                normal((PEER_HEADS, 2, PEER_KEYS, PEER_QDIM // 2), (PEER_QDIM // 2) ** -0.5),
                normal((PEER_EXPERTS, D_MODEL), D_MODEL ** -0.5),
                normal((PEER_EXPERTS, D_MODEL), PEER_TOPK ** -0.5))

    x = normal((BATCH, SEQ, D_MODEL), 1.0)
    l0_mix_norm = gain(D_MODEL)
    l0_w_in = normal((D_MODEL, sum(EVEN_COLS)), D_MODEL ** -0.5)
    l0_a_q_gain = gain(HEAD_DIM)
    l0_a_k_gain = gain(HEAD_DIM)
    l0_s5_log_dt = jax.random.uniform(next(keys), (B_GROUPS,), F32, math.log(1e-3), math.log(1e-1))
    l0_s5_a_re = -0.5 + normal((B_GROUPS, B_STATE), 0.01)
    l0_s5_a_im = math.pi * jnp.arange(B_STATE, dtype=F32)[None, :] + normal((B_GROUPS, B_STATE), 0.01)
    l0_s5_b_re = normal((B_GROUPS, B_STATE, B_GROUP), (2 * B_GROUP) ** -0.5)
    l0_s5_b_im = normal((B_GROUPS, B_STATE, B_GROUP), (2 * B_GROUP) ** -0.5)
    l0_s5_c_re = normal((B_GROUPS, B_GROUP, B_STATE), 0.5)
    l0_s5_c_im = normal((B_GROUPS, B_GROUP, B_STATE), 0.5)
    l0_s5_d = normal((B_GROUPS, B_GROUP), 0.5)
    l0_s5_w_glu = normal((B_WIDTH, B_WIDTH), B_WIDTH ** -0.5)
    l0_s5_b_glu = normal((B_WIDTH,), 0.01)
    l0_w_out = normal((MIX_WIDTH, D_MODEL), MIX_WIDTH ** -0.5)
    l0_ffn_norm = gain(D_MODEL)
    l0_peer_wq, l0_peer_subkeys, l0_peer_u, l0_peer_v = peer_params()
    l1_mix_norm = gain(D_MODEL)
    l1_w_in = normal((D_MODEL, sum(ODD_COLS)), D_MODEL ** -0.5)
    l1_c_q_gain = gain(HEAD_DIM)
    l1_c_k_gain = gain(HEAD_DIM)
    l1_nsa_cmp_pos = normal((CMP_LEN, HEAD_DIM), 0.02)
    l1_nsa_k_w1 = normal((CMP_LEN * HEAD_DIM, CMP_HIDDEN), (CMP_LEN * HEAD_DIM) ** -0.5)
    l1_nsa_k_w2 = normal((CMP_HIDDEN, HEAD_DIM), CMP_HIDDEN ** -0.5)
    l1_nsa_v_w1 = normal((CMP_LEN * HEAD_DIM, CMP_HIDDEN), (CMP_LEN * HEAD_DIM) ** -0.5)
    l1_nsa_v_w2 = normal((CMP_HIDDEN, HEAD_DIM), CMP_HIDDEN ** -0.5)
    l1_gla_w_gate = normal((GATE_RANK, D_HEADS * D_KDIM), GATE_RANK ** -0.5)
    l1_gla_b_gate = normal((D_HEADS * D_KDIM,), 0.01)
    l1_gla_o_gain = gain(D_VDIM)
    l1_w_out = normal((MIX_WIDTH, D_MODEL), MIX_WIDTH ** -0.5)
    l1_ffn_norm = gain(D_MODEL)
    l1_peer_wq, l1_peer_subkeys, l1_peer_u, l1_peer_v = peer_params()
    return {
        'x': x,
        'l0_mix_norm': l0_mix_norm, 'l0_w_in': l0_w_in,
        'l0_a_q_gain': l0_a_q_gain, 'l0_a_k_gain': l0_a_k_gain,
        'l0_s5_log_dt': l0_s5_log_dt, 'l0_s5_a_re': l0_s5_a_re, 'l0_s5_a_im': l0_s5_a_im,
        'l0_s5_b_re': l0_s5_b_re, 'l0_s5_b_im': l0_s5_b_im,
        'l0_s5_c_re': l0_s5_c_re, 'l0_s5_c_im': l0_s5_c_im, 'l0_s5_d': l0_s5_d,
        'l0_s5_w_glu': l0_s5_w_glu, 'l0_s5_b_glu': l0_s5_b_glu, 'l0_w_out': l0_w_out,
        'l0_ffn_norm': l0_ffn_norm, 'l0_peer_wq': l0_peer_wq, 'l0_peer_subkeys': l0_peer_subkeys,
        'l0_peer_u': l0_peer_u, 'l0_peer_v': l0_peer_v,
        'l1_mix_norm': l1_mix_norm, 'l1_w_in': l1_w_in,
        'l1_c_q_gain': l1_c_q_gain, 'l1_c_k_gain': l1_c_k_gain,
        'l1_nsa_cmp_pos': l1_nsa_cmp_pos, 'l1_nsa_k_w1': l1_nsa_k_w1, 'l1_nsa_k_w2': l1_nsa_k_w2,
        'l1_nsa_v_w1': l1_nsa_v_w1, 'l1_nsa_v_w2': l1_nsa_v_w2,
        'l1_gla_w_gate': l1_gla_w_gate, 'l1_gla_b_gate': l1_gla_b_gate, 'l1_gla_o_gain': l1_gla_o_gain,
        'l1_w_out': l1_w_out,
        'l1_ffn_norm': l1_ffn_norm, 'l1_peer_wq': l1_peer_wq, 'l1_peer_subkeys': l1_peer_subkeys,
        'l1_peer_u': l1_peer_u, 'l1_peer_v': l1_peer_v,
    }

def reference(x, l0_mix_norm, l0_w_in, l0_a_q_gain, l0_a_k_gain, l0_s5_log_dt, l0_s5_a_re,
              l0_s5_a_im, l0_s5_b_re, l0_s5_b_im, l0_s5_c_re, l0_s5_c_im, l0_s5_d, l0_s5_w_glu,
              l0_s5_b_glu, l0_w_out, l0_ffn_norm, l0_peer_wq, l0_peer_subkeys, l0_peer_u, l0_peer_v,
              l1_mix_norm, l1_w_in, l1_c_q_gain, l1_c_k_gain, l1_nsa_cmp_pos, l1_nsa_k_w1,
              l1_nsa_k_w2, l1_nsa_v_w1, l1_nsa_v_w2, l1_gla_w_gate, l1_gla_b_gate, l1_gla_o_gain,
              l1_w_out, l1_ffn_norm, l1_peer_wq, l1_peer_subkeys, l1_peer_u, l1_peer_v):
    seq = x.shape[1]
    pos = jnp.arange(seq, dtype=jnp.int32)
    mix_norms = (l0_mix_norm, l1_mix_norm)
    mix_params = (
        (l0_w_in, l0_a_q_gain, l0_a_k_gain, l0_s5_log_dt, l0_s5_a_re, l0_s5_a_im, l0_s5_b_re,
         l0_s5_b_im, l0_s5_c_re, l0_s5_c_im, l0_s5_d, l0_s5_w_glu, l0_s5_b_glu, l0_w_out),
        (l1_w_in, l1_c_q_gain, l1_c_k_gain, l1_nsa_cmp_pos, l1_nsa_k_w1, l1_nsa_k_w2,
         l1_nsa_v_w1, l1_nsa_v_w2, l1_gla_w_gate, l1_gla_b_gate, l1_gla_o_gain, l1_w_out),
    )
    ffn_params = (
        (l0_ffn_norm, l0_peer_wq, l0_peer_subkeys, l0_peer_u, l0_peer_v),
        (l1_ffn_norm, l1_peer_wq, l1_peer_subkeys, l1_peer_u, l1_peer_v),
    )
    for layer in range(DEPTH):
        mixer = even_mixer if layer % 2 == 0 else odd_mixer
        x = x + mixer(rms_norm(x, mix_norms[layer]), pos, *mix_params[layer]).astype(x.dtype)
        g_ffn, wq, subkeys, u_tab, v_tab = ffn_params[layer]
        x = x + peer_ffn(rms_norm(x, g_ffn), wq, subkeys, u_tab, v_tab).astype(x.dtype)
    return x


_drawn_inputs = setup_inputs


def setup_inputs(seed=0):
    import zlib

    import numpy as np

    out = dict(_drawn_inputs(seed))
    spreads = {}
    factors = {'l0_a_q_gain': 4.061,
     'l0_a_k_gain': 4.755,
     'l0_s5_a_re': 30.975,
     'l0_s5_b_glu': 7.733,
     'l1_c_q_gain': 8.0,
     'l1_c_k_gain': 8.0,
     'l1_nsa_cmp_pos': 6.801,
     'l1_gla_b_gate': 8.0,
     'l1_gla_o_gain': 4.439,
     'l1_ffn_norm': 9.175}
    for name, (base, spread) in spreads.items():
        noise = np.random.default_rng([zlib.crc32(name.encode()), seed]).standard_normal(out[name].shape)
        drawn = base * np.exp(spread * noise) if base else spread * noise
        out[name] = jnp.asarray(drawn.astype(out[name].dtype))
    for name, factor in factors.items():
        out[name] = (out[name] * factor).astype(out[name].dtype)
    return out
```

```python
from contextlib import ExitStack

import numpy as np

import concourse.bass as bass
from concourse import mybir

F32 = mybir.dt.float32
U32 = mybir.dt.uint32
ALU = mybir.AluOpType
ACT = mybir.ActivationFunctionType
AX = mybir.AxisListType
ds = bass.ds

P = 128
D = 1024
KD = D // P
SEQ = 512
NT = SEQ // P
HD = 64
NH = 8
EPS = 1e-6
NEG = -1e30
TAKEN = -3e38
LEAD = 1

S5_G, S5_C, S5_P = 32, 16, 64
S5_L = 8
S5_NC = SEQ // S5_L
S5_GP = S5_G // 2
WIDTH_B = S5_G * S5_C

L0_COLS = dict(q=(0, 512), k=(512, 128), v=(640, 128), iq=(768, 512), ik=(1280, 64), iw=(1344, 8), u=(1352, 512))
L1_COLS = dict(q=(0, 512), kc=(512, 128), vc=(640, 128), ks=(768, 128), vs=(896, 128), kw=(1024, 128),
               vw=(1152, 128), gl=(1280, 24), gq=(1304, 256), gk=(1560, 256), gv=(1816, 512),
               glow=(2328, 16), gr=(2344, 512))
L0_WIDTH = 1352
L1_WIDTH = 2856
TOPK_ATT = 128
CMP_LEN, CMP_STRIDE, CMP_HID = 32, 16, 256
NCMP = (SEQ - CMP_LEN) // CMP_STRIDE + 1
GLA_H, GLA_K, GLA_V, GLA_C = 4, 64, 128, 32
GLA_N = SEQ // GLA_C
PEER_H, PEER_K, PEER_TOP = 8, 128, 16
NLIST = 2 * PEER_H


class Tiles:

    opened = []

    def __init__(self, nc, tag):
        self.nc, self.tag, self.stack = nc, tag, ExitStack()

    def __enter__(self):
        self.stack.__enter__()
        return self

    def __exit__(self, *a):
        return self.stack.__exit__(*a)

    def sb(self, name, shape, dt=F32):
        return self.stack.enter_context(self.nc.sbuf_tensor(f"{self.tag}_{name}", shape, dt))

    def banks(self, name, n=1):
        return [self.stack.enter_context(self.nc.psum_tensor(f"{self.tag}_{name}{i}", [P, 512], F32))
                for i in range(n)]

    def sem(self, name):
        Tiles.opened.append(self.nc.alloc_semaphore(f"{self.tag}_{name}"))
        return Tiles.opened[-1]

    def sems(self, name, n):
        return [self.sem(f"{name}{i}") for i in range(n)]

    def lead(self, name, by=LEAD):
        sem = self.sem(name)
        self.nc.sync.sem_inc(sem, by)
        return sem

    def leads(self, name, n):
        return [self.lead(f"{name}{i}") for i in range(n)]

    def block(self):
        return self.stack.enter_context(self.nc.Block())


def end_half(nc):
    nc.all_engine_barrier()
    nc.clear_and_free_semaphores(Tiles.opened)
    Tiles.opened.clear()
    nc.all_engine_barrier()


class Chain:

    def __init__(self, eng, sem):
        self.eng, self.sem, self.n, self.off = eng, sem, 0, 0

    def put(self, ins):
        self.n += 1
        ins.then_inc(self.sem, 1)

    def link(self, ins):
        self.put(ins)
        self.eng.wait_ge(self.sem, self.n + self.off)

    def enter(self, i, per):
        self.off, self.per, self.first = i * per, per, self.n

    def leave(self, trips):
        assert self.n == self.first + self.per, (self.n - self.first, self.per)
        self.n, self.off = self.first + trips * self.per, 0


class Consts:

    def __init__(self, nc, t, tables):
        self.loaded = t.stack.enter_context(nc.semaphore("constants_loaded"))
        self.n = 16 * len(tables)
        self.tile, self.src = {}, tables
        for name, ap in tables.items():
            self.tile[name] = t.sb(name, list(ap.shape))

    def __getitem__(self, name):
        return self.tile[name]

    def there(self, eng):
        eng.wait_ge(self.loaded, self.n)


def bc(ap, axis, n):
    a = ap.unsqueeze(axis)
    shape = list(a.shape)
    shape[axis] = n
    return a.broadcast_to(shape)


def load_all(nc, t, c, x_in, x):
    x_loaded = t.sem("x_loaded")
    with nc.Block() as block:
        @block.sync
        def _(sp):
            sp.dma_start(x[:], x_in.rearrange("(t p) d -> p t d", p=P)).then_inc(x_loaded, 16)
            for name, ap in c.src.items():
                sp.dma_start(c[name][:], ap).then_inc(c.loaded, 16)
            sp.wait_ge(x_loaded, 16)
            sp.wait_ge(c.loaded, c.n)


def rstd_steps(v, ch, ms, root, r, root_ready, count):
    v.wait_ge(root_ready, count)
    ch.link(v.reciprocal(r, root))
    ch.link(v.tensor_tensor(root, r, r, ALU.mult))
    ch.link(v.tensor_tensor(root, root, ms, ALU.mult))
    ch.link(v.tensor_scalar(root, root, -0.5, 1.5, ALU.mult, ALU.add))
    ch.link(v.tensor_tensor(r, r, root, ALU.mult))


def normed_transpose(nc, c, tag, x, gain_dram, hT):
    with Tiles(nc, tag) as t:
        gain = t.sb("gain", [P, D])
        xn = t.sb("xn", [P, NT, D])
        ms, root, r = t.sb("ms", [P, NT]), t.sb("root", [P, NT]), t.sb("r", [P, NT])
        bank = t.banks("turned", 2)
        gain_in, ms_ready, root_ready = t.sem("gain_in"), t.sem("ms_ready"), t.sem("root_ready")
        dve, turned, taken, normed = t.sem("dve"), t.sem("turned"), t.sems("taken", 2), t.sem("normed")
        block = t.block()

        @block.sync
        def _(sp):
            sp.dma_start(gain[:], gain_dram.partition_broadcast(P)).then_inc(gain_in, 16)

        @block.vector
        def _(v):
            ch = Chain(v, dve)
            for i in range(NT):
                ch.put(v.tensor_tensor_reduce(out=xn[:, i, :], in0=x[:, i, :], in1=x[:, i, :], scale=1.0 / D,
                                              scalar=0.0, op0=ALU.mult, op1=ALU.add, accum_out=ms[:, i:i + 1]))
            v.wait_ge(dve, ch.n)
            v.tensor_scalar(ms[:], ms[:], EPS, None, ALU.add).then_inc(ms_ready, 1)
            rstd_steps(v, ch, ms[:], root[:], r[:], root_ready, 1)
            v.wait_ge(gain_in, 16)
            for i in range(NT):
                v.scalar_tensor_tensor(out=xn[:, i, :], in0=x[:, i, :], scalar=r[:, i:i + 1], in1=gain[:],
                                       op0=ALU.mult, op1=ALU.mult).then_inc(normed, 1)
            for k in range(1, KD, 2):
                v.wait_ge(turned, k + 1)
                v.tensor_copy(hT[:, k, :], bank[1][:]).then_inc(taken[1], 1)

        @block.scalar
        def _(act):
            act.wait_ge(ms_ready, 1)
            act.activation(root[:], ms[:], ACT.Sqrt).then_inc(root_ready, 1)
            for k in range(0, KD, 2):
                act.wait_ge(turned, k + 1)
                act.copy(hT[:, k, :], bank[0][:]).then_inc(taken[0], 1)

        @block.tensor
        def _(pe):
            c.there(pe)
            pe.wait_ge(normed, NT)
            for k in range(KD):
                if k >= 2:
                    pe.wait_ge(taken[k % 2], k // 2)
                for i in range(NT):
                    mm = pe.transpose(bank[k % 2][:, i * P:(i + 1) * P], xn[:, i, k * P:(k + 1) * P], c["ident"][:])
                mm.then_inc(turned, 1)


def project(nc, c, tag, lhsT, w, width, step, dst, add=False):
    w_view = w.rearrange("(k p) n -> p k n", p=P)
    kk = w_view.shape[1]
    trips = width // (2 * step)
    assert trips * 2 * step == width
    with Tiles(nc, tag) as t:
        wb = [t.sb(f"w{s}", [P, kk, step]) for s in range(2)]
        bank = t.banks("out", 8)
        w_in = t.sems("w_in", 2)
        ready, taken = t.leads("ready", 2), t.leads("taken", 2)
        block = t.block()

        @block.sync
        def _(sp):
            with sp.Fori(0, trips) as i:
                for s in range(2):
                    sp.wait_ge(ready[s], LEAD + i * NT)
                    sp.dma_start(wb[s][:], w_view[:, :, ds((i * 2 + s) * step, step)]).then_inc(w_in[s], 16)

        @block.tensor
        def _(pe):
            with pe.Fori(0, trips) as i:
                for s in range(2):
                    pe.wait_ge(w_in[s], i * 16 + 16)
                    pe.wait_ge(taken[s], LEAD + i * NT)
                    for m in range(NT):
                        for k in range(kk):
                            mm = pe.matmul(bank[s * 4 + m][:, 0:step], lhsT[:, k, m * P:(m + 1) * P], wb[s][:, k, :],
                                           start=k == 0, stop=k == kk - 1)
                        mm.then_inc(ready[s], 1)

        def take(eng, s):
            with eng.Fori(0, trips) as i:
                for m in range(NT):
                    out = dst[:, m, ds((i * 2 + s) * step, step)]
                    eng.wait_ge(ready[s], LEAD + i * NT + m + 1)
                    if add:
                        ins = nc.vector.tensor_tensor(out, bank[s * 4 + m][:, 0:step], out, ALU.add)
                    elif s:
                        ins = nc.scalar.copy(out, bank[s * 4 + m][:, 0:step])
                    else:
                        ins = nc.vector.tensor_copy(out, bank[s * 4 + m][:, 0:step])
                    ins.then_inc(taken[s], 1)

        @block.vector
        def _(v):
            take(v, 0)
            if add:
                take(v, 1)

        if not add:
            @block.scalar
            def _(act):
                take(act, 1)


def prepare_heads(nc, c, tag, jobs, cos, sin):
    with Tiles(nc, tag) as t:
        rows, nt = jobs[0][0].shape[0], jobs[0][0].shape[1]
        widest = max(a.shape[2] for a, _ in jobs)
        ta, tb = t.sb("ta", [rows, nt, widest, HD]), t.sb("tb", [rows, nt, widest, HD])
        ms, root, r = [t.sb(n, [rows, nt, widest]) for n in ("ms", "root", "r")]
        gains = [g for _, g in jobs if g is not None]
        gain = t.sb("gain", [rows, max(len(gains), 1), HD])
        dve, ms_ready, root_ready, gain_in = t.sem("dve"), t.sem("ms_ready"), t.sem("root_ready"), t.sem("gain_in")
        block = t.block()

        @block.sync
        def _(sp):
            for n, g in enumerate(gains):
                sp.dma_start(gain[:, n, :], g.partition_broadcast(rows)).then_inc(gain_in, 16)

        @block.vector
        def _(v):
            ch = Chain(v, dve)
            n = 0
            for a, g in jobs:
                heads = a.shape[2]
                if g is not None:
                    full, few = [rows, nt, heads, HD], slice(0, heads)
                    ch.link(v.tensor_tensor(ta[:, :, few, :], a, a, ALU.mult))
                    ch.link(v.tensor_reduce(ms[:, :, few], ta[:, :, few, :], AX.X, ALU.add))
                    v.tensor_scalar(ms[:, :, few], ms[:, :, few], 1.0 / HD, EPS, ALU.mult,
                                    ALU.add).then_inc(ms_ready, 1)
                    n += 1
                    rstd_steps(v, ch, ms[:, :, few], root[:, :, few], r[:, :, few], root_ready, n)
                    v.wait_ge(gain_in, 16 * len(gains))
                    ch.link(v.tensor_tensor(a, a, r[:, :, few].unsqueeze(3).broadcast_to(full), ALU.mult))
                    ch.link(v.tensor_tensor(a, a, gain[:, n - 1, :].unsqueeze(1).unsqueeze(1).broadcast_to(full),
                                            ALU.mult))
                x1, x2 = a[:, :, :, 0:HD // 2], a[:, :, :, HD // 2:HD]
                cs, sn = [bc(m, 2, heads) for m in (cos, sin)]
                a1, a2 = ta[:, :, 0:heads, 0:HD // 2], ta[:, :, 0:heads, HD // 2:HD]
                b1, b2 = tb[:, :, 0:heads, 0:HD // 2], tb[:, :, 0:heads, HD // 2:HD]
                ch.put(v.tensor_tensor(a1, x1, cs, ALU.mult))
                ch.put(v.tensor_tensor(a2, x2, sn, ALU.mult))
                ch.put(v.tensor_tensor(b1, x1, sn, ALU.mult))
                ch.link(v.tensor_tensor(b2, x2, cs, ALU.mult))
                ch.put(v.tensor_tensor(x1, a1, a2, ALU.subtract))
                ch.link(v.tensor_tensor(x2, b1, b2, ALU.add))

        @block.scalar
        def _(act):
            n = 0
            for a, g in jobs:
                if g is not None:
                    few = slice(0, a.shape[2])
                    n += 1
                    act.wait_ge(ms_ready, n)
                    act.activation(root[:, :, few], ms[:, :, few], ACT.Sqrt).then_inc(root_ready, 1)


def turn(nc, c, tag, blocks, zero=()):
    with Tiles(nc, tag) as t:
        bank = t.banks("turned", 4)
        turned, taken = t.sem("turned"), t.sems("taken", 4)
        block = t.block()

        @block.tensor
        def _(pe):
            c.there(pe)
            for n, (dst, srcs, rows) in enumerate(blocks):
                if n >= 4:
                    pe.wait_ge(taken[n % 4], n // 4)
                at = 0
                for src in srcs:
                    k = src.shape[0]
                    mm = pe.transpose(bank[n % 4][0:rows, at:at + k], src, c["ident"][0:k, 0:k])
                    at += k
                mm.then_inc(turned, 1)

        def take(eng, par, copy):
            for n, (dst, srcs, rows) in enumerate(blocks):
                if n % 2 == par:
                    w = sum(s.shape[0] for s in srcs)
                    eng.wait_ge(turned, n + 1)
                    copy(dst, bank[n % 4][0:rows, 0:w]).then_inc(taken[n % 4], 1)

        @block.gpsimd
        def _(pool):
            for z in zero:
                pool.memset(z, 0.0)

        @block.vector
        def _(v):
            take(v, 0, nc.vector.tensor_copy)

        @block.scalar
        def _(act):
            take(act, 1, nc.scalar.copy)


def index_scores(nc, c, tag, iq, iw, ikT, score):
    with Tiles(nc, tag) as t:
        staged = t.sb("staged", [P, NT, P])
        qT = t.sb("qT", [P, SEQ])
        rel = [t.sb(f"rel{m}", [P, (m + 1) * P]) for m in range(1, NT)]
        bank_q = t.banks("q")[0]
        bank = t.banks("s", NT - 1)
        q_staged, q_turned, q_there = t.sem("q_staged"), t.lead("q_turned"), t.sem("q_there")
        s_ready, rel_ready, rel_used, cleared = t.lead("s_ready"), t.lead("rel_ready"), t.lead("rel_used"), t.sem("clr")
        block = t.block()
        M = NT - 1

        @block.gpsimd
        def _(pool):
            pool.memset(score[:], 0.0).then_inc(cleared, 1)
            pool.memset(staged[:], 0.0).then_inc(cleared, 1)
            pool.wait_ge(cleared, 2)
            with pool.Fori(0, NH) as h:
                pool.wait_ge(q_turned, LEAD + h)
                pool.tensor_copy(staged[:, :, 0:HD], iq[:, :, ds(h * HD, HD)]).then_inc(q_staged, 1)

        @block.tensor
        def _(pe):
            c.there(pe)
            with pe.Fori(0, NH) as h:
                pe.wait_ge(q_staged, h + 1)
                for m in range(NT):
                    mm = pe.transpose(bank_q[:, m * P:(m + 1) * P], staged[:, m, :], c["ident"][:])
                mm.then_inc(q_turned, 1)
                pe.wait_ge(q_there, h + 1)
                pe.wait_ge(rel_ready, LEAD + h * M)
                for m in range(1, NT):
                    n = (m + 1) * P
                    pe.matmul(bank[m - 1][:, 0:n], qT[:, m * P:(m + 1) * P], ikT[:, 0:n],
                              start=True, stop=True).then_inc(s_ready, 1)

        @block.scalar
        def _(act):
            with act.Fori(0, NH) as h:
                act.wait_ge(q_turned, LEAD + h + 1)
                act.wait_ge(s_ready, LEAD + h * M)
                act.copy(qT[:], bank_q[:]).then_inc(q_there, 1)
                for m in range(1, NT):
                    act.wait_ge(s_ready, LEAD + h * M + m)
                    act.wait_ge(rel_used, LEAD + h * M)
                    act.activation(rel[m - 1][:], bank[m - 1][:, 0:(m + 1) * P], ACT.Relu,
                                   scale=HD ** -0.5).then_inc(rel_ready, 1)

        @block.vector
        def _(v):
            v.wait_ge(cleared, 2)
            with v.Fori(0, NH) as h:
                for m in range(1, NT):
                    s = score[:, m, 0:(m + 1) * P]
                    v.wait_ge(rel_ready, LEAD + h * M + m)
                    v.wait_ge(rel_used, LEAD + h * M)
                    v.scalar_tensor_tensor(out=s, in0=rel[m - 1][:], scalar=iw[:, m, ds(h, 1)], in1=s,
                                           op0=ALU.mult, op1=ALU.add).then_inc(rel_used, 1)


def select_keys(nc, c, tag, score, bias):
    with Tiles(nc, tag) as t:
        best = [t.sb(f"best{m}", [P, 8]) for m in range(NT)]
        dve = t.sem("dve")
        block = t.block()

        @block.vector
        def _(v):
            ch = Chain(v, dve)
            c.there(v)
            for m in range(1, NT):
                diag = score[:, m, m * P:(m + 1) * P]
                ch.put(v.tensor_tensor(diag, diag, c["causal"][:], ALU.add))
            ch.link(v.tensor_copy(bias[:, 0, 0:P], c["causal"][:]))
            for _ in range(TOPK_ATT // 8):
                for m in range(1, NT):
                    ch.put(v.max(best[m][:], score[:, m, 0:(m + 1) * P]))
                v.wait_ge(dve, ch.n)
                for m in range(1, NT):
                    s = score[:, m, 0:(m + 1) * P]
                    ch.put(v.match_replace(s, best[m][:], s, TAKEN))
                v.wait_ge(dve, ch.n)
            for m in range(1, NT):
                n = (m + 1) * P
                ch.put(v.tensor_scalar(bias[:, m, 0:n], score[:, m, 0:n], TAKEN / 2, -NEG, ALU.is_lt, ALU.mult))
            v.wait_ge(dve, ch.n)
            for m in range(1, NT):
                n = (m + 1) * P
                ch.put(v.tensor_scalar(bias[:, m, 0:n], bias[:, m, 0:n], NEG, None, ALU.add))
            v.wait_ge(dve, ch.n)


def causal_bias(nc, c, tag, bias):
    with Tiles(nc, tag) as t:
        dve = t.sem("dve")
        block = t.block()

        @block.vector
        def _(v):
            ch = Chain(v, dve)
            c.there(v)
            ch.link(v.memset(bias[:], 0.0))
            for m in range(NT):
                ch.link(v.tensor_copy(bias[:, m, m * P:(m + 1) * P], c["causal"][:]))


def attention(nc, c, tag, q, kT, vals, bias, out, gate=None, add=False):
    with Tiles(nc, tag) as t:
        staged = t.sb("staged", [P, NT, P])
        qT = t.sb("qT", [P, SEQ])
        sm = [t.sb(f"sm{m}", [P, (m + 1) * P]) for m in range(NT)]
        pT = [t.sb(f"pT{b}", [P, SEQ]) for b in range(2)]
        mx, nmx, den, rden = [t.sb(n, [P, NT]) for n in ("mx", "nmx", "den", "rden")]
        bank_q = t.banks("q")[0]
        bank_s, bank_t, bank_o = t.banks("s", 2), t.banks("t", 2), t.banks("o", 2)
        q_staged, q_turned, q_there = t.sem("q_staged"), t.lead("q_turned"), t.sem("q_there")
        s_ready, s_taken = t.lead("s_ready"), t.leads("s_taken", 2)
        m_ready, p_ready = t.sem("m_ready"), t.sem("p_ready")
        t_ready, t_taken = t.lead("t_ready"), t.leads("t_taken", 2)
        o_ready, o_taken, dve = t.sem("o_ready"), t.leads("o_taken", 2), t.sem("dve")
        cleared, wait_taker = t.sem("cleared"), t.sb("wait_taker", [P, 1])
        block = t.block()

        @block.gpsimd
        def _(pool):
            pool.memset(staged[:], 0.0).then_inc(cleared, 1)
            pool.wait_ge(cleared, 1)
            with pool.Fori(0, NH) as h:
                pool.wait_ge(q_turned, LEAD + h)
                pool.tensor_copy(staged[:, :, 0:HD], q[:, :, ds(h * HD, HD)]).then_inc(q_staged, 1)

        @block.tensor
        def _(pe):
            def scores(h, g, m):
                b = m % 2
                pe.wait_ge(s_taken[b], LEAD + h * 2 + m // 2)
                n = (m + 1) * P
                pe.matmul(bank_s[b][:, 0:n], qT[:, m * P:(m + 1) * P],
                          kT[:, ds(g, 1), 0:n].rearrange("p a n -> p (a n)"),
                          start=True, stop=True).then_inc(s_ready, 1)

            def turn_probs(h, m):
                pe.wait_ge(p_ready, h * NT + m + 1)
                pe.wait_ge(t_taken[m % 2], LEAD + h * 2 + m // 2)
                for s in range(m + 1):
                    mm = pe.transpose(bank_t[m % 2][:, s * P:(s + 1) * P], sm[m][:, s * P:(s + 1) * P], c["ident"][:])
                mm.then_inc(t_ready, 1)

            def weigh(h, g, m):
                pe.wait_ge(t_taken[m % 2], LEAD + h * 2 + m // 2 + 1)
                pe.wait_ge(o_taken[m % 2], LEAD + h * 2 + m // 2)
                for s in range(m + 1):
                    mm = pe.matmul(bank_o[m % 2][:, 0:HD], pT[m % 2][:, s * P:(s + 1) * P],
                                   vals[:, s, ds(g * HD, HD)], start=s == 0, stop=s == m)
                mm.then_inc(o_ready, 1)

            c.there(pe)
            with pe.Fori(0, 2) as g:
                with pe.Fori(0, NH // 2) as r:
                    h = g * (NH // 2) + r
                    pe.wait_ge(q_staged, h + 1)
                    for m in range(NT):
                        mm = pe.transpose(bank_q[:, m * P:(m + 1) * P], staged[:, m, :], c["ident"][:])
                    mm.then_inc(q_turned, 1)
                    pe.wait_ge(q_there, h + 1)
                    scores(h, g, 0)
                    scores(h, g, 1)
                    for m in range(NT):
                        turn_probs(h, m)
                        if m + 2 < NT:
                            scores(h, g, m + 2)
                        weigh(h, g, m)

        @block.scalar
        def _(act):
            with act.Fori(0, NH) as h:
                act.wait_ge(q_turned, LEAD + h + 1)
                act.wait_ge(s_ready, LEAD + h * NT)
                act.copy(qT[:], bank_q[:]).then_inc(q_there, 1)
                for m in range(NT):
                    act.wait_ge(m_ready, h * NT + m + 1)
                    act.activation(sm[m][:], sm[m][:], ACT.Exp, bias=nmx[:, m:m + 1],
                                   accum_out=den[:, m:m + 1]).then_inc(p_ready, 1)

        @block.vector
        def _(v):
            ch = Chain(v, dve)

            def add_bias(h, m):
                n = (m + 1) * P
                v.wait_ge(s_ready, LEAD + h * NT + m + 1)
                v.wait_ge(t_ready, LEAD + h * NT)
                v.memset(wait_taker[:], 0.0)
                ins = v.tensor_tensor_reduce(out=sm[m][:], in0=bank_s[m % 2][:, 0:n], in1=bias[:, m, 0:n],
                                             scale=HD ** -0.5, scalar=TAKEN, op0=ALU.add, op1=ALU.max,
                                             accum_out=mx[:, m:m + 1])
                ins.then_inc(s_taken[m % 2], 1)
                v.wait_ge(s_taken[m % 2], LEAD + h * 2 + m // 2 + 1)
                v.tensor_scalar(nmx[:, m:m + 1], mx[:, m:m + 1], -1.0, None, ALU.mult).then_inc(m_ready, 1)

            with v.Fori(0, NH) as h:
                ch.enter(h, NT * (2 if gate is None else 3))
                add_bias(h, 0)
                add_bias(h, 1)
                for m in range(NT):
                    n = (m + 1) * P
                    v.wait_ge(t_ready, LEAD + h * NT + m + 1)
                    ins = v.tensor_copy(pT[m % 2][:, 0:n], bank_t[m % 2][:, 0:n])
                    ins.then_inc(t_taken[m % 2], 1)
                    if m + 2 < NT:
                        add_bias(h, m + 2)
                    v.wait_ge(p_ready, h * NT + m + 1)
                    ch.link(v.tensor_scalar(rden[:, m:m + 1], den[:, m:m + 1], 1e-30, None, ALU.max))
                    ch.link(v.reciprocal(rden[:, m:m + 1], rden[:, m:m + 1]))
                    if gate is not None:
                        ch.link(v.tensor_tensor(rden[:, m:m + 1], rden[:, m:m + 1], gate[:, m, ds(h, 1)], ALU.mult))
                    o = out[:, m, ds(h * HD, HD)]
                    v.wait_ge(o_ready, h * NT + m + 1)
                    if add:
                        ins = v.scalar_tensor_tensor(out=o, in0=bank_o[m % 2][:, 0:HD], scalar=rden[:, m:m + 1],
                                                     in1=o, op0=ALU.mult, op1=ALU.add)
                    else:
                        ins = v.tensor_scalar(o, bank_o[m % 2][:, 0:HD], rden[:, m:m + 1], None, ALU.mult)
                    ins.then_inc(o_taken[m % 2], 1)
                ch.leave(NH)


def s5_inputs(nc, c, tag, hT, w, u_sb):
    off = L0_COLS["u"][0]
    w_view = w.rearrange("(k p) n -> p k n", p=P)[:, :, off:off + WIDTH_B]
    with Tiles(nc, tag) as t:
        wb = t.sb("w", [P, KD, WIDTH_B])
        bank = t.banks("out", S5_L)
        w_in, ready = t.sem("w_in"), t.sem("ready")
        block = t.block()

        @block.sync
        def _(sp):
            sp.dma_start(wb[:], w_view).then_inc(w_in, 16)

        @block.tensor
        def _(pe):
            pe.wait_ge(w_in, 16)
            for l in range(S5_L):
                for k in range(KD):
                    mm = pe.matmul(bank[l][0:S5_NC, :], hT[:, k, l:SEQ:S5_L], wb[:, k, :], start=k == 0,
                                   stop=k == KD - 1)
                mm.then_inc(ready, 1)

        def take(eng, par, copy):
            for l in range(par, S5_L, 2):
                eng.wait_ge(ready, l + 1)
                copy(u_sb[:, :, l, :], bank[l][0:S5_NC, :].rearrange("p (g c) -> p g c", c=S5_C))

        @block.vector
        def _(v):
            take(v, 0, nc.vector.tensor_copy)

        @block.scalar
        def _(act):
            take(act, 1, nc.scalar.copy)


def s5_tables(nc, c, tag, ins, vr, vi, car, cai, pw8, bb):
    with Tiles(nc, tag) as t:
        raw = {n: t.sb(n, [P, S5_GP]) for n in ("log_dt", "a_re", "a_im")}
        raw3 = {n: t.sb(n, [P, S5_GP, S5_C]) for n in ("b_re", "b_im", "c_re", "c_im")}
        dt, dlr, mag, th, nn, red, half, sin_t, sin_h, cos_t, den, u1, u2, fr, fi = [
            t.sb(n, [P, S5_GP]) for n in ("dt", "dlr", "mag", "th", "nn", "red", "half", "sin_t", "sin_h", "cos_t",
                                          "den", "u1", "u2", "fr", "fi")]
        pr, pi = t.sb("pr", [P, S5_GP, S5_L + 1]), t.sb("pi", [P, S5_GP, S5_L + 1])
        qr, qi = t.sb("qr", [P, S5_GP, S5_L]), t.sb("qi", [P, S5_GP, S5_L])
        tmp = t.sb("tmp", [P, S5_GP, S5_L + 1, S5_C])
        t3 = t.sb("t3", [P, S5_GP, S5_C])
        loaded, dve, act_in, act_out = t.sem("loaded"), t.sem("dve"), t.sem("act_in"), t.sem("act_out")
        block = t.block()
        every = {**raw, **raw3}

        @block.sync
        def _(sp):
            for n, tile in every.items():
                sp.dma_start(tile[:], ins[n]).then_inc(loaded, 16)

        @block.scalar
        def _(act):
            act.wait_ge(loaded, 16 * len(every))
            act.activation(dt[:], raw["log_dt"][:], ACT.Exp).then_inc(act_out, 1)
            act.wait_ge(act_in, 1)
            act.activation(mag[:], dlr[:], ACT.Exp).then_inc(act_out, 1)
            act.wait_ge(act_in, 2)
            act.activation(sin_t[:], red[:], ACT.Sin).then_inc(act_out, 1)
            act.activation(sin_h[:], half[:], ACT.Sin).then_inc(act_out, 1)

        @block.vector
        def _(v):
            ch = Chain(v, dve)

            def tt(out, a, b, op):
                ch.link(v.tensor_tensor(out, a, b, op))

            lr, li = raw["a_re"][:], raw["a_im"][:]
            v.wait_ge(loaded, 16 * len(every))
            v.wait_ge(act_out, 1)
            v.tensor_tensor(dlr[:], dt[:], lr, ALU.mult).then_inc(act_in, 1)
            tt(th[:], dt[:], li, ALU.mult)
            rnd = 1.5 * 2 ** 23
            ch.link(v.tensor_scalar(nn[:], th[:], 0.15915494309189535, rnd, ALU.mult, ALU.add))
            ch.link(v.tensor_scalar(nn[:], nn[:], -rnd, None, ALU.add))
            c1 = 6.28125
            c2 = 0.0019350051879882812
            c3 = 2 * np.pi - c1 - c2
            src = th
            for cc in (c1, c2, c3):
                ch.link(v.scalar_tensor_tensor(out=red[:], in0=nn[:], scalar=-float(cc), in1=src[:], op0=ALU.mult,
                                               op1=ALU.add))
                src = red
            ch.link(v.tensor_scalar(red[:], red[:], 3.1415925, -3.1415925, ALU.min, ALU.max))
            v.tensor_scalar(half[:], red[:], 0.5, None, ALU.mult).then_inc(act_in, 1)
            v.wait_ge(act_out, 4)
            tt(cos_t[:], sin_h[:], sin_h[:], ALU.mult)
            ch.link(v.tensor_scalar(cos_t[:], cos_t[:], -2.0, 1.0, ALU.mult, ALU.add))
            ch.put(v.memset(pr[:, :, 0], 1.0))
            ch.put(v.memset(pi[:, :, 0], 0.0))
            ch.put(v.tensor_tensor(pr[:, :, 1], mag[:], cos_t[:], ALU.mult))
            ch.link(v.tensor_tensor(pi[:, :, 1], mag[:], sin_t[:], ALU.mult))
            ar, ai = pr[:, :, 1], pi[:, :, 1]
            for l in range(2, S5_L + 1):
                ch.put(v.tensor_tensor(u1[:], pr[:, :, l - 1], ar, ALU.mult))
                ch.put(v.tensor_tensor(u2[:], pi[:, :, l - 1], ai, ALU.mult))
                ch.put(v.tensor_tensor(fr[:], pr[:, :, l - 1], ai, ALU.mult))
                ch.link(v.tensor_tensor(fi[:], pi[:, :, l - 1], ar, ALU.mult))
                ch.put(v.tensor_tensor(pr[:, :, l], u1[:], u2[:], ALU.subtract))
                ch.link(v.tensor_tensor(pi[:, :, l], fr[:], fi[:], ALU.add))
            tt(u1[:], lr, lr, ALU.mult)
            tt(u2[:], li, li, ALU.mult)
            tt(den[:], u1[:], u2[:], ALU.add)
            ch.link(v.reciprocal(den[:], den[:]))
            ch.link(v.tensor_scalar(nn[:], ar, -1.0, None, ALU.add))
            tt(u1[:], nn[:], lr, ALU.mult)
            tt(u2[:], ai, li, ALU.mult)
            tt(fr[:], u1[:], u2[:], ALU.add)
            tt(fr[:], fr[:], den[:], ALU.mult)
            tt(u1[:], ai, lr, ALU.mult)
            tt(u2[:], nn[:], li, ALU.mult)
            tt(fi[:], u1[:], u2[:], ALU.subtract)
            tt(fi[:], fi[:], den[:], ALU.mult)
            br, bi = raw3["b_re"][:], raw3["b_im"][:]
            frb, fib = bc(fr[:], 2, S5_C), bc(fi[:], 2, S5_C)
            tt(bb[:, 0], frb, br, ALU.mult)
            tt(t3[:], fib, bi, ALU.mult)
            tt(bb[:, 0], bb[:, 0], t3[:], ALU.subtract)
            tt(bb[:, 1], frb, bi, ALU.mult)
            tt(t3[:], fib, br, ALU.mult)
            tt(bb[:, 1], bb[:, 1], t3[:], ALU.add)
            ch.put(v.tensor_copy(pw8[:, 0, :], pr[:, :, S5_L]))
            ch.put(v.tensor_copy(pw8[:, 2, :], pi[:, :, S5_L]))
            ch.put(v.tensor_scalar(pw8[:, 1, :], pi[:, :, S5_L], -1.0, None, ALU.mult))
            for l in range(S5_L):
                ch.put(v.tensor_copy(qr[:, :, l], pr[:, :, S5_L - 1 - l]))
                ch.put(v.tensor_copy(qi[:, :, l], pi[:, :, S5_L - 1 - l]))
            v.wait_ge(dve, ch.n)
            sh = [P, S5_GP, S5_L, S5_C]
            qrb, qib = bc(qr[:], 3, S5_C), bc(qi[:], 3, S5_C)
            bbr, bbi = bc(bb[:, 0], 2, S5_L), bc(bb[:, 1], 2, S5_L)
            tl = tmp[:, :, 0:S5_L, :]
            tt(vr[:], qrb, bbr, ALU.mult)
            tt(tl, qib, bbi, ALU.mult)
            tt(vr[:], vr[:], tl, ALU.subtract)
            tt(vi[:], qrb, bbi, ALU.mult)
            tt(tl, qib, bbr, ALU.mult)
            tt(vi[:], vi[:], tl, ALU.add)
            prb, pib = bc(pr[:], 3, S5_C), bc(pi[:], 3, S5_C)
            cr, ci = bc(raw3["c_re"][:], 2, S5_L + 1), bc(raw3["c_im"][:], 2, S5_L + 1)
            tt(car[:], prb, cr, ALU.mult)
            tt(tmp[:], pib, ci, ALU.mult)
            tt(car[:], car[:], tmp[:], ALU.subtract)
            tt(cai[:], pib, cr, ALU.mult)
            tt(tmp[:], prb, ci, ALU.mult)
            tt(cai[:], cai[:], tmp[:], ALU.add)
            ch.link(v.tensor_scalar(cai[:], cai[:], -1.0, None, ALU.mult))


def s5_scan(nc, c, tag, ins, U, vT, car, cai, pw8, bb, y_sb):
    LC = S5_L * S5_C
    with Tiles(nc, tag) as t:
        toep = t.sb("toep", [P, S5_G, LC])
        kern = t.sb("kern", [S5_C, S5_G, LC])
        skip, dd = t.sb("skip", [S5_C, S5_G]), t.sb("dd", [S5_C, S5_G, S5_C])
        xs = t.sb("xs", [P, 2, S5_GP, S5_NC])
        st = t.sb("st", [P, 3, S5_GP, S5_NC + 1])
        u1, u2 = t.sb("u1", [P, 2, S5_GP]), t.sb("u2", [P, 2, S5_GP])
        bank = t.banks("b", 8)
        skip_in, k_ready, k_there, toep_in = t.sem("skip_in"), t.sem("k_ready"), t.sem("k_there"), t.sem("toep_in")
        cleared, x_ready, x_there, dve = t.sem("cleared"), t.sem("x_ready"), t.sem("x_there"), t.sem("dve")
        scanned, y_ready = t.sem("scanned"), t.sem("y_ready")
        block = t.block()

        @block.gpsimd
        def _(pool):
            pool.memset(toep[:], 0.0).then_inc(cleared, 1)

        @block.sync
        def _(sp):
            sp.dma_start(skip[:], ins["d_skip"]).then_inc(skip_in, 16)
            sp.wait_ge(cleared, 1)
            sp.wait_ge(k_there, 1)
            for l in range(S5_L):
                sp.dma_start(toep[l * S5_C:(l + 1) * S5_C, :, l * S5_C:LC],
                             kern[:, :, 0:LC - l * S5_C]).then_inc(toep_in, 16)

        @block.tensor
        def _(pe):
            for g in range(S5_G):
                lo, gp = 64 * (g % 2), g // 2
                out = bank[4 * (g % 2) + gp // 4][0:S5_C, (gp % 4) * LC:(gp % 4 + 1) * LC]
                pe.matmul(out, bb[lo:lo + 64, 0, gp, :], car[lo:lo + 64, gp, 0:S5_L, :], start=True, stop=False)
                mm = pe.matmul(out, bb[lo:lo + 64, 1, gp, :], cai[lo:lo + 64, gp, 0:S5_L, :], start=False, stop=True)
            mm.then_inc(k_ready, 1)
            pe.wait_ge(k_there, 1)
            for g in range(S5_G):
                lo, gp = 64 * (g % 2), g // 2
                for ri in range(2):
                    out = bank[2 * ri + gp // 8][lo:lo + 64, (gp % 8) * S5_NC:(gp % 8 + 1) * S5_NC]
                    mm = pe.matmul(out, vT[:, ri, gp, lo:lo + 64], U[:, g, :], start=True, stop=True)
            mm.then_inc(x_ready, 1)
            pe.wait_ge(toep_in, 16 * S5_L)
            pe.wait_ge(scanned, S5_NC)
            for g in range(S5_G):
                lo, gp = 64 * (g % 2), g // 2
                out = bank[4 * (g % 2) + gp // 4][0:S5_NC, (gp % 4) * LC:(gp % 4 + 1) * LC]
                pe.matmul(out, U[:, g, :], toep[:, g, :], start=True, stop=False)
                pe.matmul(out, st[lo:lo + 64, 0, gp, 0:S5_NC], car[lo:lo + 64, gp, 1:S5_L + 1, :], start=False,
                          stop=False)
                mm = pe.matmul(out, st[lo:lo + 64, 1, gp, 0:S5_NC], cai[lo:lo + 64, gp, 1:S5_L + 1, :], start=False,
                               stop=True)
                if g % 8 >= 6:
                    mm.then_inc(y_ready, 1)

        @block.vector
        def _(v):
            ch = Chain(v, dve)
            v.wait_ge(k_ready, 1)
            for b in range(8):
                ch.put(v.tensor_copy(kern[:, 8 * (b % 4) + b // 4:8 * (b % 4) + 8:2, :],
                                     bank[b][0:S5_C, :].rearrange("p (g n) -> p g n", g=4)))
            v.wait_ge(dve, ch.n)
            v.wait_ge(skip_in, 16)
            c.there(v)
            ch.link(v.tensor_tensor(dd[:], bc(c["ident"][0:S5_C, 0:S5_C], 1, S5_G), bc(skip[:], 2, S5_C), ALU.mult))
            v.tensor_tensor(kern[:, :, 0:S5_C], kern[:, :, 0:S5_C], dd[:], ALU.add).then_inc(k_there, 1)
            ch.put(v.memset(st[:], 0.0))
            v.wait_ge(x_ready, 1)
            for ri in range(2):
                for b in range(2):
                    ch.put(v.tensor_copy(xs[:, ri, 8 * b:8 * b + 8, :],
                                         bank[2 * ri + b][:].rearrange("p (g n) -> p g n", g=8)))
            v.wait_ge(dve, ch.n)
            first = bc(pw8[:, 0, :], 1, 2)
            with v.Fori(0, S5_NC) as m:
                ch.enter(m, 3)
                now, nxt = ds(m, 1), ds(m + 1, 1)
                ch.put(v.tensor_tensor(u1[:], first, st[:, 0:2, :, now].rearrange("p a g o -> p a (g o)"), ALU.mult))
                ch.link(v.tensor_tensor(u2[:], pw8[:, 1:3, :], st[:, 1:3, :, now].rearrange("p a g o -> p a (g o)"),
                                        ALU.mult))
                ch.link(v.tensor_tensor(u1[:], u1[:], u2[:], ALU.add))
                v.tensor_tensor(st[:, 0:2, :, nxt].rearrange("p a g o -> p a (g o)"), u1[:],
                                xs[:, :, :, now].rearrange("p a g o -> p a (g o)"), ALU.add)
                v.tensor_tensor(st[:, 2:3, :, nxt].rearrange("p a g o -> p a (g o)"), u1[:, 0:1, :],
                                xs[:, 0:1, :, now].rearrange("p a g o -> p a (g o)"), ALU.add).then_inc(scanned, 1)
                v.wait_ge(scanned, m + 1)
            ch.leave(S5_NC)

        @block.scalar
        def _(act):
            y_view = y_sb[:].rearrange("p l (g c) -> p g l c", c=S5_C)
            for n in range(8):
                quad, par = n // 2, n % 2
                act.wait_ge(y_ready, n + 1)
                act.activation(y_view[:, 8 * quad + par:8 * quad + 8:2],
                               bank[4 * par + quad][0:S5_NC, :].rearrange("p (g l c) -> p g l c", g=4, l=S5_L),
                               ACT.Gelu_apprx_tanh)


def glu(nc, c, tag, yT, w, b, oT):
    K = WIDTH_B // P
    with Tiles(nc, tag) as t:
        wb, bias, sg = t.sb("w", [P, K, WIDTH_B]), t.sb("bias", [P, K]), t.sb("sg", [P, K, SEQ])
        bank = t.banks("z", K)
        loaded, z_ready, sg_ready = t.sem("loaded"), t.sem("z_ready"), t.sem("sg_ready")
        block = t.block()

        @block.sync
        def _(sp):
            sp.dma_start(wb[:], w.rearrange("(k p) n -> p k n", p=P)).then_inc(loaded, 16)
            sp.dma_start(bias[:], b).then_inc(loaded, 16)

        @block.tensor
        def _(pe):
            pe.wait_ge(loaded, 32)
            for f in range(K):
                for k in range(K):
                    mm = pe.matmul(bank[f][:], wb[:, k, f * P:(f + 1) * P], yT[:, k, :], start=k == 0, stop=k == K - 1)
                mm.then_inc(z_ready, 1)

        @block.scalar
        def _(act):
            act.wait_ge(loaded, 32)
            for f in range(K):
                act.wait_ge(z_ready, f + 1)
                act.activation(sg[:, f, :], bank[f][:], ACT.Sigmoid, bias=bias[:, f:f + 1]).then_inc(sg_ready, 1)

        @block.vector
        def _(v):
            for f in range(K):
                v.wait_ge(sg_ready, f + 1)
                v.tensor_tensor(oT[:, f, :], yT[:, f, :], sg[:, f, :], ALU.mult)


def layer0_mixer(nc, c, x, a):
    with Tiles(nc, "l0") as keep:
        oT = keep.sb("oT", [P, KD, SEQ])
        with Tiles(nc, "l0in") as inner:
            qkv = inner.sb("qkv", [P, NT, L0_WIDTH])
            u_sb = inner.sb("u", [S5_NC, S5_G, S5_L, S5_C])
            with Tiles(nc, "l0h") as t:
                hT = t.sb("hT", [P, KD, SEQ])
                normed_transpose(nc, c, "n0", x, a["l0_mix_norm"], hT)
                project(nc, c, "p0", hT, a["l0_w_in"][:, 0:L0_WIDTH], L0_WIDTH, L0_WIDTH // 4, qkv)
                s5_inputs(nc, c, "u0", hT, a["l0_w_in"], u_sb)

            def cols(name, heads=None):
                o, n = L0_COLS[name]
                v = qkv[:, :, o:o + n]
                return v.rearrange("p t (h d) -> p t h d", h=heads) if heads else v

            with Tiles(nc, "l0s") as t:
                U = t.sb("U", [P, S5_G, S5_NC])
                vT = t.sb("vT", [P, 2, S5_GP, P])
                car, cai = [t.sb(n, [P, S5_GP, S5_L + 1, S5_C]) for n in ("car", "cai")]
                pw8, bb = t.sb("pw8", [P, 3, S5_GP]), t.sb("bb", [P, 2, S5_GP, S5_C])
                y_sb = t.sb("y", [S5_NC, S5_L, WIDTH_B])
                with Tiles(nc, "l0v") as tv:
                    vr, vi = [tv.sb(n, [P, S5_GP, S5_L, S5_C]) for n in ("vr", "vi")]
                    s5_tables(nc, c, "st", a, vr, vi, car, cai, pw8, bb)
                    turn(nc, c, "tu", [(U[:, 8 * b:8 * b + 8, :].rearrange("p g n -> p (g n)"),
                                        [u_sb[:, g, :, :].rearrange("p l c -> p (l c)") for g in range(8 * b, 8 * b + 8)],
                                        P) for b in range(4)] +
                         [(vT[:, ri, 4 * b:4 * b + 4, :].rearrange("p g n -> p (g n)"),
                           [s[:, gp, :, :].rearrange("p l c -> p (l c)") for gp in range(4 * b, 4 * b + 4)], P)
                          for ri, s in enumerate((vr, vi)) for b in range(4)])
                s5_scan(nc, c, "sc", a, U, vT, car, cai, pw8, bb, y_sb)
                yT, yP = t.sb("yT", [P, 4, SEQ]), t.sb("yP", [P, 4, SEQ])
                turn(nc, c, "ty", [(yT[:, f, :].rearrange("p (n l) -> p l n", l=S5_L),
                                    [y_sb[:, l, f * P:(f + 1) * P] for l in range(S5_L)], P) for f in range(4)])
                glu(nc, c, "gl", yT, a["l0_s5_w_glu"], a["b_glu"], oT[:, 4:8, :])

            prepare_heads(nc, c, "ph", [(cols("q", 8), a["l0_a_q_gain"]), (cols("k", 2), a["l0_a_k_gain"]),
                                        (cols("iq", 8), None), (cols("ik", 1), None)], c["cos"][:], c["sin"][:])
            with Tiles(nc, "l0a") as t:
                kT, ikT = t.sb("kT", [P, 2, SEQ]), t.sb("ikT", [P, SEQ])
                score, bias, iw = t.sb("score", [P, NT, SEQ]), t.sb("bias", [P, NT, SEQ]), t.sb("iw", [P, NT, 8])
                o_a = t.sb("o", [P, NT, SEQ])
                k, ik = cols("k"), cols("ik")
                turn(nc, c, "tk", [(kT[0:HD, g, :], [k[:, m, g * HD:(g + 1) * HD] for m in range(NT)], HD)
                                   for g in range(2)] + [(ikT[0:HD, :], [ik[:, m, :] for m in range(NT)], HD)],
                     zero=[kT[HD:P], ikT[HD:P]])
                scale_small(nc, c, "iw", iw, cols("iw"), 8 ** -0.5)
                index_scores(nc, c, "ix", cols("iq"), iw, ikT, score)
                select_keys(nc, c, "se", score, bias)
                attention(nc, c, "at", cols("q"), kT, cols("v"), bias, o_a)
                turn(nc, c, "to", [(oT[:, f, :], [o_a[:, m, f * P:(f + 1) * P] for m in range(NT)], P)
                                   for f in range(4)])
        project(nc, c, "po", oT, a["l0_w_out"], D, SEQ, x, add=True)


def scale_small(nc, c, tag, out, src, by):
    with Tiles(nc, tag) as t:
        block = t.block()

        @block.vector
        def _(v):
            v.tensor_scalar(out[:], src, by, None, ALU.mult)


def compress(nc, c, tag, cols, a, kcT, vc):
    NB, L = 32, CMP_LEN
    with Tiles(nc, tag) as t:
        posT = t.sb("posT", [HD, L])
        flat = [t.sb(f"flat{n}", [HD, 2, SEQ]) for n in range(2)]
        blk = [t.sb(f"blk{n}", [HD, L, 2, NB]) for n in range(2)]
        w1 = t.sb("w1", [HD, L, CMP_HID])
        w2 = [t.sb(f"w2{n}", [P, CMP_HID // P, HD]) for n in range(2)]
        hid = t.sb("hid", [P, 2, 2, 2 * NB])
        kc = t.sb("kc", [2 * NB, 1, 1, HD])
        srcs = [cols(n) for n in ("kc", "vc")]
        turn(nc, c, tag + "t", [(flat[n][:, g, :], [srcs[n][:, m, g * HD:(g + 1) * HD] for m in range(NT)], HD)
                                for n in range(2) for g in range(2)])
        with Tiles(nc, tag + "h") as t2:
            bank = t2.banks("h", 4)
            bank_v, bank_k = t2.banks("v", 2), t2.banks("k")[0]
            small_in, w1_in, cleared, blocks = t2.sem("small_in"), t2.sem("w1_in"), t2.sem("cleared"), t2.sem("blocks")
            h_ready, h_there, o_ready = t2.sem("h_ready"), t2.sem("h_there"), t2.sem("o_ready")
            block = t2.block()

            @block.sync
            def _(sp):
                sp.dma_start(posT[:], a["l1_nsa_cmp_pos"]).then_inc(small_in, 16)
                for n, name in enumerate(("l1_nsa_k_w2", "l1_nsa_v_w2")):
                    sp.dma_start(w2[n][:], a[name].rearrange("(m p) d -> p m d", p=P)).then_inc(small_in, 16)
                for n, name in enumerate(("l1_nsa_k_w1", "l1_nsa_v_w1")):
                    if n:
                        sp.wait_ge(h_ready, 1)
                    sp.dma_start(w1[:], a[name].rearrange("(l d) h -> d l h", d=HD)).then_inc(w1_in, 16)

            @block.gpsimd
            def _(pool):
                for n in range(2):
                    pool.memset(blk[n][:], 0.0).then_inc(cleared, 1)

            @block.vector
            def _(v):
                v.wait_ge(cleared, 2)
                v.wait_ge(small_in, 48)
                for n in range(2):
                    for g in range(2):
                        for half in range(L // CMP_STRIDE):
                            lo = half * CMP_STRIDE
                            win = flat[n][:, g, lo:lo + NCMP * CMP_STRIDE].rearrange("p (n l) -> p l n", l=CMP_STRIDE)
                            v.tensor_tensor(blk[n][:, lo:lo + CMP_STRIDE, g, 0:NCMP], win,
                                            bc(posT[:, lo:lo + CMP_STRIDE], 2, NCMP), ALU.add).then_inc(blocks, 1)
                v.wait_ge(o_ready, 3)
                v.tensor_copy(kc[:, 0, 0, :], bank_k[0:2 * NB, 0:HD])
                for g in range(2):
                    v.tensor_copy(vc[:, g, :], bank_v[g][0:NB, 0:HD])

            @block.tensor
            def _(pe):
                for n in range(2):
                    pe.wait_ge(blocks, 4 * (n + 1))
                    pe.wait_ge(w1_in, 16 * (n + 1))
                    for m in range(2):
                        for l in range(L):
                            mm = pe.matmul(bank[2 * n + m][:, 0:2 * NB], w1[:, l, m * P:(m + 1) * P],
                                           blk[n][:, l, :, :].rearrange("p g n -> p (g n)"), start=l == 0,
                                           stop=l == L - 1)
                    mm.then_inc(h_ready, 1)
                pe.wait_ge(h_there, 4)
                for m in range(2):
                    mm = pe.matmul(bank_k[0:2 * NB, 0:HD], hid[:, 0, m, :], w2[0][:, m, :], start=m == 0, stop=m == 1)
                mm.then_inc(o_ready, 1)
                for g in range(2):
                    for m in range(2):
                        mm = pe.matmul(bank_v[g][0:NB, 0:HD], hid[:, 1, m, g * NB:(g + 1) * NB], w2[1][:, m, :],
                                       start=m == 0, stop=m == 1)
                    mm.then_inc(o_ready, 1)

            @block.scalar
            def _(act):
                for n in range(2):
                    act.wait_ge(h_ready, n + 1)
                    for m in range(2):
                        act.activation(hid[:, n, m, :], bank[2 * n + m][:, 0:2 * NB],
                                       ACT.Gelu_apprx_tanh).then_inc(h_there, 1)

        prepare_heads(nc, c, tag + "p", [(kc[:], a["l1_c_k_gain"])], c["ccos"][:], c["csin"][:])
        turn(nc, c, tag + "u", [(kcT[0:HD].rearrange("p g n -> p (g n)"), [kc[:, 0, 0, :]], HD)], zero=[kcT[HD:P]])


def compressed_attention(nc, c, tag, q, kcT, vc, out, gate):
    NB = 32
    with Tiles(nc, tag) as t:
        staged = t.sb("staged", [P, NT, P])
        qT, pT = t.sb("qT", [P, SEQ]), t.sb("pT", [NB, SEQ])
        sm, vals = t.sb("sm", [P, NT, NB]), t.sb("vals", [NB, 2, HD])
        mx, den = t.sb("mx", [P, NT, 1]), t.sb("den", [P, NT, 1])
        bank_q, bank_s, bank_t, bank_o = [t.banks(n)[0] for n in ("q", "s", "t", "o")]
        q_staged, q_there, m_ready, e_there, p_ready, pT_there = [
            t.sem(n) for n in ("q_staged", "q_there", "m_ready", "e_there", "p_ready", "pT_there")]
        q_turned, s_ready, s_taken, t_ready, o_ready, o_taken = [
            t.lead(n) for n in ("q_turned", "s_ready", "s_taken", "t_ready", "o_ready", "o_taken")]
        cleared, dve = t.sem("cleared"), t.sem("dve")
        block = t.block()

        @block.gpsimd
        def _(pool):
            pool.memset(staged[:], 0.0).then_inc(cleared, 1)
            pool.wait_ge(cleared, 1)
            with pool.Fori(0, NH) as h:
                pool.wait_ge(q_turned, LEAD + h)
                pool.tensor_copy(staged[:, :, 0:HD], q[:, :, ds(h * HD, HD)]).then_inc(q_staged, 1)

        @block.tensor
        def _(pe):
            c.there(pe)
            with pe.Fori(0, 2) as g:
                with pe.Fori(0, NH // 2) as r:
                    h = g * (NH // 2) + r
                    pe.wait_ge(q_staged, h + 1)
                    for m in range(NT):
                        mm = pe.transpose(bank_q[:, m * P:(m + 1) * P], staged[:, m, :], c["ident"][:])
                    mm.then_inc(q_turned, 1)
                    pe.wait_ge(q_there, h + 1)
                    pe.wait_ge(s_taken, LEAD + h)
                    for m in range(NT):
                        mm = pe.matmul(bank_s[:, m * NB:(m + 1) * NB], qT[:, m * P:(m + 1) * P],
                                       kcT[:, ds(g, 1), :].rearrange("p a n -> p (a n)"), start=True, stop=True)
                    mm.then_inc(s_ready, 1)
                    pe.wait_ge(p_ready, h + 1)
                    for m in range(NT):
                        mm = pe.transpose(bank_t[0:NB, m * P:(m + 1) * P], sm[:, m, :], c["ident"][:])
                    mm.then_inc(t_ready, 1)
                    pe.wait_ge(pT_there, h + 1)
                    pe.wait_ge(o_taken, LEAD + h)
                    for m in range(NT):
                        mm = pe.matmul(bank_o[:, m * HD:(m + 1) * HD], pT[:, m * P:(m + 1) * P],
                                       vc[:, ds(g, 1), :].rearrange("p a n -> p (a n)"), start=True, stop=True)
                    mm.then_inc(o_ready, 1)

        @block.scalar
        def _(act):
            with act.Fori(0, NH) as h:
                act.wait_ge(q_turned, LEAD + h + 1)
                act.wait_ge(s_ready, LEAD + h)
                act.copy(qT[:], bank_q[:]).then_inc(q_there, 1)
                act.wait_ge(m_ready, h + 1)
                act.activation(sm[:], sm[:], ACT.Exp).then_inc(e_there, 1)
                act.wait_ge(t_ready, LEAD + h + 1)
                act.wait_ge(o_ready, LEAD + h)
                act.copy(pT[:], bank_t[0:NB, :]).then_inc(pT_there, 1)

        @block.vector
        def _(v):
            ch = Chain(v, dve)
            c.there(v)
            with v.Fori(0, NH) as h:
                ch.enter(h, 5)
                v.wait_ge(s_ready, LEAD + h + 1)
                v.wait_ge(t_ready, LEAD + h)
                v.scalar_tensor_tensor(out=sm[:], in0=bank_s[:, 0:NT * NB].rearrange("p (m n) -> p m n", m=NT),
                                       scalar=HD ** -0.5, in1=c["cbias"][:], op0=ALU.mult,
                                       op1=ALU.add).then_inc(s_taken, 1)
                v.wait_ge(s_taken, LEAD + h + 1)
                ch.link(v.tensor_reduce(mx[:].rearrange("p m o -> p (m o)"), sm[:], AX.X, ALU.max))
                v.tensor_tensor(sm[:], sm[:], mx[:].broadcast_to([P, NT, NB]), ALU.subtract).then_inc(m_ready, 1)
                v.wait_ge(e_there, h + 1)
                v.tensor_tensor(sm[:], sm[:], c["cmask"][:], ALU.mult).then_inc(p_ready, 1)
                v.wait_ge(p_ready, h + 1)
                ch.link(v.tensor_reduce(den[:].rearrange("p m o -> p (m o)"), sm[:], AX.X, ALU.add))
                ch.link(v.tensor_scalar(den[:], den[:], 1e-30, None, ALU.max))
                ch.link(v.reciprocal(den[:], den[:]))
                ch.link(v.tensor_tensor(den[:], den[:], gate[:, :, ds(h, 1)], ALU.mult))
                v.wait_ge(o_ready, LEAD + h + 1)
                v.tensor_tensor(out[:, :, ds(h * HD, HD)], bank_o[:, 0:NT * HD].rearrange("p (m d) -> p m d", m=NT),
                                den[:].broadcast_to([P, NT, HD]), ALU.mult).then_inc(o_taken, 1)
            ch.leave(NH)


def gla_decays(nc, c, tag, cols, a, qd, ki, kd, dec, la):
    W = GLA_H * GLA_K
    with Tiles(nc, tag) as t:
        lowT, wg, bg = t.sb("lowT", [16, SEQ]), t.sb("wg", [16, W]), t.sb("bg", [P, W])
        lg, e1 = t.sb("lg", [P, NT, W]), t.sb("e1", [P, NT, W])
        bank = t.banks("b", 8)
        loaded, turned, low_there, l_ready, lg_ready = [
            t.sem(n) for n in ("loaded", "turned", "low_there", "l_ready", "lg_ready")]
        e_there, la_ready, s_ready, x_there, dve = [
            t.sem(n) for n in ("e_there", "la_ready", "s_ready", "x_there", "dve")]
        block = t.block()
        low, gq, gk = cols("glow"), cols("gq"), cols("gk")

        @block.sync
        def _(sp):
            sp.dma_start(wg[:], a["l1_gla_w_gate"]).then_inc(loaded, 16)
            sp.dma_start(bg[:], a["l1_gla_b_gate"].partition_broadcast(P)).then_inc(loaded, 16)

        @block.tensor
        def _(pe):
            c.there(pe)
            for m in range(NT):
                mm = pe.transpose(bank[0][0:16, m * P:(m + 1) * P], low[:, m, :], c["ident"][:])
            mm.then_inc(turned, 1)
            pe.wait_ge(loaded, 32)
            pe.wait_ge(low_there, 1)
            for m in range(NT):
                pe.matmul(bank[1 + m][:, 0:W], lowT[:, m * P:(m + 1) * P], wg[:], start=True,
                          stop=True).then_inc(l_ready, 1)
            pe.wait_ge(la_ready, NT)
            for h in range(GLA_H):
                for m in range(NT):
                    mm = pe.matmul(bank[0][0:GLA_K, (h * NT + m) * 4:(h * NT + m + 1) * 4],
                                   la[:, m, h * GLA_K:(h + 1) * GLA_K], c["chunk"][:], start=True, stop=True)
            mm.then_inc(s_ready, 1)
            for m in range(NT):
                pe.matmul(bank[1 + m][:, 0:W], c["upto"][:], la[:, m, :], start=True, stop=True)
                pe.matmul(bank[1 + m][:, W:2 * W], c["after"][:], la[:, m, :], start=True,
                          stop=True).then_inc(s_ready, 1)

        @block.scalar
        def _(act):
            act.wait_ge(turned, 1)
            act.copy(lowT[:], bank[0][0:16, :]).then_inc(low_there, 1)
            act.wait_ge(lg_ready, NT)
            act.activation(e1[:], lg[:], ACT.Abs).then_inc(e_there, 1)
            act.wait_ge(e_there, 1)
            act.activation(e1[:], e1[:], ACT.Exp, scale=-1.0).then_inc(e_there, 1)
            act.wait_ge(e_there, 2)
            act.activation(e1[:], e1[:], ACT.Ln, bias=1.0).then_inc(e_there, 1)
            act.wait_ge(s_ready, 1)
            act.activation(dec[:].rearrange("p h n -> p (h n)"), bank[0][0:GLA_K, 0:GLA_H * GLA_N], ACT.Exp)
            for m in range(NT):
                act.wait_ge(s_ready, m + 2)
                act.activation(qd[:, m, :], bank[1 + m][:, 0:W], ACT.Exp).then_inc(x_there, 1)
                act.activation(ki[:, m, :], bank[1 + m][:, 0:W], ACT.Exp, scale=-1.0).then_inc(x_there, 1)
                act.activation(kd[:, m, :], bank[1 + m][:, W:2 * W], ACT.Exp).then_inc(x_there, 1)

        @block.vector
        def _(v):
            ch = Chain(v, dve)
            v.wait_ge(loaded, 32)
            for m in range(NT):
                v.wait_ge(l_ready, m + 1)
                v.tensor_tensor(lg[:, m, :], bank[1 + m][:, 0:W], bg[:], ALU.add).then_inc(lg_ready, 1)
            v.wait_ge(e_there, 3)
            ch.link(v.scalar_tensor_tensor(out=lg[:], in0=lg[:], scalar=0.0, in1=e1[:], op0=ALU.min, op1=ALU.subtract))
            for m in range(NT):
                v.tensor_scalar(la[:, m, :], lg[:, m, :], 1.0 / 16.0, None, ALU.mult).then_inc(la_ready, 1)
            for m in range(NT):
                v.wait_ge(x_there, 3 * m + 3)
                v.scalar_tensor_tensor(out=qd[:, m, :], in0=gq[:, m, :], scalar=GLA_K ** -0.5, in1=qd[:, m, :],
                                       op0=ALU.mult, op1=ALU.mult)
                v.tensor_tensor(ki[:, m, :], gk[:, m, :], ki[:, m, :], ALU.mult)
                v.tensor_tensor(kd[:, m, :], gk[:, m, :], kd[:, m, :], ALU.mult)


def gla_mix(nc, c, tag, gv, qdT, kiT, kd, dec, o):
    C4 = P // GLA_C
    with Tiles(nc, tag) as t:
        att = t.sb("att", [P, NT, GLA_H, P])
        state = t.sb("state", [GLA_K, GLA_N + 1, GLA_H, GLA_V])
        bank_a, bank_u, bank_o = t.banks("a", 2), t.banks("u", 4), t.banks("o", 2)
        cleared, a_ready, a_there, u_ready, u_there, o_ready, o_taken, dve = [
            t.sem(n) for n in ("cleared", "a_ready", "a_there", "u_ready", "u_there", "o_ready", "o_taken", "dve")]
        block = t.block()

        @block.gpsimd
        def _(pool):
            pool.memset(att[:], 0.0).then_inc(cleared, 1)
            pool.memset(state[:, 0], 0.0).then_inc(cleared, 1)

        @block.tensor
        def _(pe):
            for m in range(NT):
                if m >= 2:
                    pe.wait_ge(a_there, m - 1)
                for h in range(GLA_H):
                    mm = pe.matmul(bank_a[m % 2][:, h * P:(h + 1) * P], kiT[:, h, m * P:(m + 1) * P],
                                   qdT[:, h, m * P:(m + 1) * P], start=True, stop=True)
                mm.then_inc(a_ready, 1)
                for n in range(C4):
                    lo = n * GLA_C
                    if m:
                        pe.wait_ge(u_there, (m - 1) * C4 + n + 1)
                    for h in range(GLA_H):
                        mm = pe.matmul(bank_u[n][0:GLA_K, h * GLA_V:(h + 1) * GLA_V],
                                       kd[lo:lo + GLA_C, m, h * GLA_K:(h + 1) * GLA_K],
                                       gv[lo:lo + GLA_C, m, h * GLA_V:(h + 1) * GLA_V], start=True, stop=True)
                    mm.then_inc(u_ready, 1)
            for m in range(NT):
                pe.wait_ge(a_there, m + 1)
                pe.wait_ge(u_there, (m + 1) * C4)
                if m >= 2:
                    pe.wait_ge(o_taken, m - 1)
                for h in range(GLA_H):
                    out = bank_o[m % 2][:, h * GLA_V:(h + 1) * GLA_V]
                    pe.matmul(out, att[:, m, h, :], gv[:, m, h * GLA_V:(h + 1) * GLA_V], start=True, stop=False,
                              skip_group_check=True)
                    for n in range(C4):
                        lo = n * GLA_C
                        mm = pe.matmul(out[lo:lo + GLA_C], qdT[:, h, m * P + lo:m * P + lo + GLA_C],
                                       state[:, m * C4 + n, h, :], start=False, stop=True, skip_group_check=True)
                mm.then_inc(o_ready, 1)

        @block.vector
        def _(v):
            ch = Chain(v, dve)
            c.there(v)
            v.wait_ge(cleared, 2)
            for m in range(NT):
                v.wait_ge(a_ready, m + 1)
                for h in range(GLA_H):
                    ins = v.copy_predicated(att[:, m, h, :], c["upto"][:].bitcast(U32), bank_a[m % 2][:, h * P:(h + 1) * P])
                ins.then_inc(a_there, 1)
                for n in range(C4):
                    at = m * C4 + n
                    v.wait_ge(u_ready, at + 1)
                    for h in range(GLA_H):
                        ins = v.scalar_tensor_tensor(out=state[:, at + 1, h, :], in0=state[:, at, h, :],
                                                     scalar=dec[:, h, at:at + 1],
                                                     in1=bank_u[n][0:GLA_K, h * GLA_V:(h + 1) * GLA_V],
                                                     op0=ALU.mult, op1=ALU.add)
                    ins.then_inc(u_there, 1)
                    v.wait_ge(u_there, at + 1)

        @block.scalar
        def _(act):
            for m in range(NT):
                act.wait_ge(o_ready, m + 1)
                act.copy(o[:, m, :], bank_o[m % 2][:]).then_inc(o_taken, 1)


def gla_gate(nc, c, tag, o, gr, gain):
    with Tiles(nc, tag) as t:
        sq, sg, gb = t.sb("sq", [P, NT, GLA_H, GLA_V]), t.sb("sg", [P, NT, SEQ]), t.sb("gain", [P, GLA_V])
        ms, root, r = [t.sb(n, [P, NT, GLA_H]) for n in ("ms", "root", "r")]
        gain_in, ms_ready, root_ready, sg_ready, dve = [
            t.sem(n) for n in ("gain_in", "ms_ready", "root_ready", "sg_ready", "dve")]
        block = t.block()
        o4 = o[:].rearrange("p m (h e) -> p m h e", h=GLA_H)
        full = [P, NT, GLA_H, GLA_V]

        @block.sync
        def _(sp):
            sp.dma_start(gb[:], gain.partition_broadcast(P)).then_inc(gain_in, 16)

        @block.scalar
        def _(act):
            act.activation(sg[:], gr, ACT.Sigmoid).then_inc(sg_ready, 1)
            act.wait_ge(ms_ready, 1)
            act.activation(root[:], ms[:], ACT.Sqrt).then_inc(root_ready, 1)

        @block.vector
        def _(v):
            ch = Chain(v, dve)
            ch.link(v.tensor_tensor(sq[:], o4, o4, ALU.mult))
            ch.link(v.tensor_reduce(ms[:], sq[:], AX.X, ALU.add))
            v.tensor_scalar(ms[:], ms[:], 1.0 / GLA_V, EPS, ALU.mult, ALU.add).then_inc(ms_ready, 1)
            rstd_steps(v, ch, ms[:], root[:], r[:], root_ready, 1)
            ch.link(v.tensor_tensor(o4, o4, r[:].unsqueeze(3).broadcast_to(full), ALU.mult))
            v.wait_ge(gain_in, 16)
            ch.link(v.tensor_tensor(o4, o4, gb[:].unsqueeze(1).unsqueeze(1).broadcast_to(full), ALU.mult))
            v.wait_ge(sg_ready, 1)
            ch.link(v.tensor_tensor(sg[:], sg[:], gr, ALU.mult))
            ch.link(v.tensor_tensor(o[:], o[:], sg[:], ALU.mult))


def sigmoid_gates(nc, c, tag, gates, src):
    with Tiles(nc, tag) as t:
        block = t.block()

        @block.scalar
        def _(act):
            act.activation(gates[:], src.rearrange("p m (h b) -> p m b h", b=3), ACT.Sigmoid)


def layer1_mixer(nc, c, x, a):
    with Tiles(nc, "l1") as keep:
        oT = keep.sb("oT", [P, KD, SEQ])
        with Tiles(nc, "l1in") as inner:
            qkv = inner.sb("qkv", [P, NT, L1_WIDTH])
            with Tiles(nc, "l1h") as t:
                hT = t.sb("hT", [P, KD, SEQ])
                normed_transpose(nc, c, "n1", x, a["l1_mix_norm"], hT)
                project(nc, c, "p1", hT, a["l1_w_in"], L1_WIDTH, L1_WIDTH // 6, qkv)

            def cols(name, heads=None):
                o, n = L1_COLS[name]
                v = qkv[:, :, o:o + n]
                return v.rearrange("p t (h d) -> p t h d", h=heads) if heads else v

            with Tiles(nc, "l1g") as t:
                kd, dec = t.sb("kd", [P, NT, 256]), t.sb("dec", [GLA_K, GLA_H, GLA_N])
                qdT, kiT = [t.sb(n, [GLA_K, GLA_H, SEQ]) for n in ("qdT", "kiT")]
                o_d = t.sb("o", [P, NT, SEQ])
                with Tiles(nc, "l1gd") as t2:
                    qd, ki, la = [t2.sb(n, [P, NT, 256]) for n in ("qd", "ki", "la")]
                    gla_decays(nc, c, "gd", cols, a, qd, ki, kd, dec, la)
                    turn(nc, c, "gt", [(d[:, h, :], [s[:, m, h * GLA_K:(h + 1) * GLA_K] for m in range(NT)], GLA_K)
                                       for d, s in ((qdT, qd), (kiT, ki)) for h in range(GLA_H)])
                gla_mix(nc, c, "gm", cols("gv"), qdT, kiT, kd, dec, o_d)
                gla_gate(nc, c, "gg", o_d, cols("gr"), a["l1_gla_o_gain"])
                turn(nc, c, "go", [(oT[:, 4 + f, :], [o_d[:, m, f * P:(f + 1) * P] for m in range(NT)], P)
                                   for f in range(4)])

            with Tiles(nc, "l1a") as t:
                kcT, vc = t.sb("kcT", [P, 2, 32]), t.sb("vc", [32, 2, HD])
                gates = t.sb("gates", [P, NT, 3, NH])
                compress(nc, c, "cm", cols, a, kcT, vc)
                prepare_heads(nc, c, "pq", [(cols("q", 8), a["l1_c_q_gain"]), (cols("ks", 2), a["l1_c_k_gain"]),
                                            (cols("kw", 2), a["l1_c_k_gain"])], c["cos"][:], c["sin"][:])
                kT = [t.sb(f"kT{n}", [P, 2, SEQ]) for n in range(2)]
                bias, o_c = t.sb("bias", [P, NT, SEQ]), t.sb("o", [P, NT, SEQ])
                ks = [cols("ks"), cols("kw")]
                turn(nc, c, "tk1", [(kT[n][0:HD, g, :], [ks[n][:, m, g * HD:(g + 1) * HD] for m in range(NT)], HD)
                                    for n in range(2) for g in range(2)], zero=[k[HD:P] for k in kT])
                sigmoid_gates(nc, c, "sg", gates, cols("gl"))
                causal_bias(nc, c, "cb", bias)
                compressed_attention(nc, c, "ca", cols("q"), kcT, vc, o_c, gates[:, :, 0, :])
                attention(nc, c, "as", cols("q"), kT[0], cols("vs"), bias, o_c, gate=gates[:, :, 1, :], add=True)
                attention(nc, c, "aw", cols("q"), kT[1], cols("vw"), bias, o_c, gate=gates[:, :, 2, :], add=True)
                turn(nc, c, "to1", [(oT[:, f, :], [o_c[:, m, f * P:(f + 1) * P] for m in range(NT)], P)
                                    for f in range(4)])
        project(nc, c, "po1", oT, a["l1_w_out"], D, SEQ, x, add=True)


def retrieve(nc, c, tag, xT, wq, subkeysT, gates, rows, cols):
    with Tiles(nc, tag) as t:
        wb = [t.sb(f"wq{s}", [P, KD, P]) for s in range(2)]
        keys = t.sb("keys", [P, NLIST, PEER_K])
        qT = [t.sb(f"qT{s}", [P, SEQ]) for s in range(2)]
        T = PEER_TOP
        val = [t.sb(f"val{s}", [P, NT, T]) for s in range(2)]
        idx = [t.sb(f"idx{s}", [P, NT, T], U32) for s in range(2)]
        idf = [t.sb(f"idf{s}", [P, NT, T]) for s in range(2)]
        work = t.sb("work", [P, NT, P])
        cand, rest = t.sb("cand", [P, NT, T * T]), t.sb("rest", [P, NT, T * T])
        top, pos = t.sb("top", [P, NT, T]), t.sb("pos", [P, NT, T], U32)
        place = [t.sb(f"place{s}", [P, NT, T], U32) for s in range(2)]
        placef = [t.sb(f"placef{s}", [P, NT, T]) for s in range(2)]
        onehot = t.sb("onehot", [P, NT, T, T])
        low = t.sb("low", [P, NT, PEER_H, 1])
        wait_taker = t.sb("wait_taker", [P, 1])
        bank_q, bank_s = t.banks("q", 2), t.banks("s", 2)
        keys_in, wq_in = t.sem("keys_in"), t.sems("wq_in", 2)
        q_ready, q_there = t.leads("q_ready", 2), t.leads("q_there", 2)
        s_ready, s_taken = t.leads("s_ready", 2), t.leads("s_taken", 2)
        dve, e_ready, e_there = t.sem("dve"), t.sem("e_ready"), t.sem("e_there")
        block = t.block()
        wq_view = wq.rearrange("(k p) n -> p k n", p=P)

        @block.sync
        def _(sp):
            sp.dma_start(keys[:], subkeysT).then_inc(keys_in, 16)
            with sp.Fori(0, PEER_H) as h:
                for s in range(2):
                    sp.wait_ge(q_ready[s], LEAD + h)
                    sp.dma_start(wb[s][:], wq_view[:, :, ds((h * 2 + s) * P, P)]).then_inc(wq_in[s], 16)

        @block.tensor
        def _(pe):
            pe.wait_ge(keys_in, 16)
            with pe.Fori(0, PEER_H) as h:
                for s in range(2):
                    pe.wait_ge(wq_in[s], h * 16 + 16)
                    pe.wait_ge(q_there[s], LEAD + h)
                    for k in range(KD):
                        mm = pe.matmul(bank_q[s][:], wb[s][:, k, :], xT[:, k, :], start=k == 0, stop=k == KD - 1)
                    mm.then_inc(q_ready[s], 1)
                for s in range(2):
                    pe.wait_ge(q_there[s], LEAD + h + 1)
                    pe.wait_ge(s_taken[s], LEAD + h)
                    for m in range(NT):
                        mm = pe.matmul(bank_s[s][:, m * P:(m + 1) * P], qT[s][:, m * P:(m + 1) * P],
                                       keys[:, ds(h * 2 + s, 1), :].rearrange("p a n -> p (a n)"),
                                       start=True, stop=True)
                    mm.then_inc(s_ready[s], 1)

        @block.scalar
        def _(act):
            with act.Fori(0, PEER_H) as h:
                for s in range(2):
                    act.wait_ge(q_ready[s], LEAD + h + 1)
                    act.wait_ge(s_ready[s], LEAD + h)
                    act.copy(qT[s][:], bank_q[s][:]).then_inc(q_there[s], 1)
            act.wait_ge(e_ready, 1)
            act.activation(gates[:], gates[:], ACT.Exp).then_inc(e_there, 1)

        @block.vector
        def _(v):
            ch = Chain(v, dve)
            c.there(v)

            def sync():
                v.wait_ge(dve, ch.n + ch.off)
                v.memset(wait_taker[:], 0.0)

            def best16(src, spare, values, indices, done=None):
                for m in range(NT):
                    ch.put(v.max(values[:, m, 0:8], src(m)))
                sync()
                for m in range(NT):
                    ch.put(v.max_index(indices[:, m, 0:8], values[:, m, 0:8], src(m)))
                for m in range(NT):
                    ins = v.match_replace(spare(m), values[:, m, 0:8], src(m), TAKEN)
                    if m < NT - 1 or done is None:
                        ch.put(ins)
                    else:
                        ins.then_inc(done[0], 1)
                        v.wait_ge(done[0], done[1])
                sync()
                for m in range(NT):
                    ch.put(v.max(values[:, m, 8:T], spare(m)))
                sync()
                for m in range(NT):
                    ch.put(v.max_index(indices[:, m, 8:T], values[:, m, 8:T], spare(m)))
                v.wait_ge(dve, ch.n + ch.off)

            with v.Fori(0, PEER_H) as h:
                ch.enter(h, 2 * (5 * NT - 1 + 1) + NT + 5 * NT + 2 + 4 * 2 + 1)
                for s in range(2):
                    v.wait_ge(s_ready[s], LEAD + h + 1)
                    v.memset(wait_taker[:], 0.0)
                    best16(lambda m: bank_s[s][:, m * P:(m + 1) * P], lambda m: work[:, m, :], val[s], idx[s],
                           (s_taken[s], LEAD + h + 1))
                    ch.put(v.tensor_copy(idf[s][:], idx[s][:]))
                for m in range(NT):
                    ch.put(v.tensor_tensor(cand[:, m, :].rearrange("p (a b) -> p a b", b=T),
                                           bc(val[0][:, m, :], 2, T), bc(val[1][:, m, :], 1, T), ALU.add))
                sync()
                best16(lambda m: cand[:, m, :], lambda m: rest[:, m, :], top, pos)
                ch.put(v.tensor_scalar(place[0][:], pos[:], 4, None, ALU.logical_shift_right))
                ch.link(v.tensor_scalar(place[1][:], pos[:], T - 1, None, ALU.bitwise_and))
                for s, e in ((0, rows), (1, cols)):
                    ch.link(v.tensor_copy(placef[s][:], place[s][:]))
                    ch.link(v.tensor_tensor(onehot[:], bc(placef[s][:], 3, T),
                                            c["iota"][:, 0:T].unsqueeze(1).unsqueeze(1).broadcast_to([P, NT, T, T]),
                                            ALU.is_equal))
                    ch.link(v.tensor_tensor(onehot[:], onehot[:], bc(idf[s][:], 2, T), ALU.mult))
                    ch.link(v.tensor_reduce(e[:, :, ds(h * T, T)], onehot[:], AX.X, ALU.add))
                ch.put(v.tensor_copy(gates[:, :, ds(h * T, T)], top[:]))
                v.wait_ge(dve, ch.n + ch.off)
            ch.leave(PEER_H)
            g4 = gates[:].rearrange("p m (h k) -> p m h k", k=T)
            full = [P, NT, PEER_H, T]
            ch.link(v.tensor_copy(low[:], g4[:, :, :, 0:1]))
            v.tensor_tensor(g4, g4, low[:].broadcast_to(full), ALU.subtract).then_inc(e_ready, 1)
            v.wait_ge(e_there, 1)
            ch.link(v.tensor_reduce(low[:].rearrange("p m h o -> p m (h o)"), g4, AX.X, ALU.add))
            ch.link(v.reciprocal(low[:], low[:]))
            ch.link(v.tensor_tensor(g4, g4, low[:].broadcast_to(full), ALU.mult))


def spread_gates(nc, c, tag, gT, rT, cT, gmat):
    QUAD, GROUPS = 4, 2
    trips = P // (QUAD * GROUPS)
    with Tiles(nc, tag) as t:
        wide = [t.sb(f"wide{s}", [P, PEER_K, P]) for s in range(2)]
        left = [t.sb(f"left{g}", [P, QUAD, P]) for g in range(GROUPS)]
        right = [t.sb(f"right{g}", [P, QUAD, P]) for g in range(GROUPS)]
        bank = t.banks("g", GROUPS)
        made, spread, taken, stored = (t.leads("made", GROUPS), t.leads("spread", GROUPS), t.leads("taken", GROUPS),
                                       t.leads("stored", 2))
        block = t.block()

        def walk(eng, body):
            with eng.Fori(0, NT // 2) as o:
                for s in range(2):
                    tile = o * 2 + s
                    with eng.Fori(0, trips) as j:
                        body(tile, j, tile * trips + j, o, s)

        @block.vector
        def _(v):
            c.there(v)

            def body(tile, j, n, o, s):
                for g in range(GROUPS):
                    v.wait_ge(spread[g], LEAD + n)
                    for q in range(QUAD):
                        tok = tile * P + j * (QUAD * GROUPS) + (g * QUAD + q)
                        v.tensor_scalar(left[g][:, q, :], c["iota"][:], rT[:, ds(tok, 1)], gT[:, ds(tok, 1)],
                                        ALU.is_equal, ALU.mult)
                        ins = v.tensor_scalar(right[g][:, q, :], c["iota"][:], cT[:, ds(tok, 1)], None, ALU.is_equal)
                    ins.then_inc(made[g], 1)
            walk(v, body)

        @block.tensor
        def _(pe):
            def body(tile, j, n, o, s):
                for g in range(GROUPS):
                    pe.wait_ge(made[g], LEAD + n + 1)
                    pe.wait_ge(taken[g], LEAD + n)
                    for q in range(QUAD):
                        mm = pe.matmul(bank[g][:, q * P:(q + 1) * P], left[g][:, q, :], right[g][:, q, :],
                                       start=True, stop=True)
                    mm.then_inc(spread[g], 1)
            walk(pe, body)

        @block.scalar
        def _(act):
            def body(tile, j, n, o, s):
                for g in range(GROUPS):
                    act.wait_ge(spread[g], LEAD + n + 1)
                    act.wait_ge(stored[s], LEAD + o * 16)
                    act.copy(wide[s][:, :, ds(j * (QUAD * GROUPS) + g * QUAD, QUAD)],
                             bank[g][:].rearrange("p (q b) -> p b q", q=QUAD)).then_inc(taken[g], 1)
            walk(act, body)

        @block.sync
        def _(sp):
            with sp.Fori(0, NT // 2) as o:
                for s in range(2):
                    tile = o * 2 + s
                    for g in range(GROUPS):
                        sp.wait_ge(taken[g], LEAD + (tile + 1) * trips)
                    sp.dma_start(gmat[:, :, ds(tile * P, P)].rearrange("b a t -> a b t"),
                                 wide[s][:]).then_inc(stored[s], 16)
            for s in range(2):
                sp.wait_ge(stored[s], LEAD + 16 * (NT // 2))


def all_experts(nc, c, tag, xT, uT, v_tab, gmat, x):
    SETS, SUM = 8, 4
    trips = PEER_K // SETS
    v_view = v_tab.rearrange("(a b) d -> b a d", b=PEER_K)
    OUTS = NT * 2
    with Tiles(nc, tag) as t:
        u = [t.sb(f"u{j}", [P, KD, P]) for j in range(SETS)]
        vb = [t.sb(f"v{j}", [P, D]) for j in range(SETS)]
        gb = [t.sb(f"g{j}", [P, SEQ]) for j in range(SETS)]
        act_h = [t.sb(f"h{j}", [P, SEQ]) for j in range(SUM)]
        prod = [t.sb(f"p{j}", [P, SEQ]) for j in range(SETS)]
        y = t.sb("y", [P, NT, D])
        bank_h, bank_y = t.banks("hb", SUM), t.banks("yb", 4)
        u_in, v_in, g_in = t.sems("u_in", SETS), t.sems("v_in", SETS), t.sems("g_in", SETS)
        h_ready, h_there, p_ready = t.lead("h_ready", 8), t.lead("h_there", 4), t.lead("p_ready", 8)
        y_ready, y_taken = t.lead("y_ready", 16), t.lead("y_taken", 4)
        cleared = t.sem("cleared")
        block = t.block()

        @block.gpsimd
        def _(pool):
            pool.memset(y[:], 0.0).then_inc(cleared, 1)

        @block.sync
        def _(sp):
            with sp.Fori(0, trips) as i:
                for j in range(SETS):
                    sp.wait_ge(h_ready, 8 + i * SETS + j + 1 - SETS)
                    sp.dma_start(u[j][:], uT[ds(i * SETS + j, 1)].rearrange("o p (k a) -> p (o k) a", k=KD))\
                      .then_inc(u_in[j], 16)
                for j in range(SETS):
                    sp.wait_ge(p_ready, 8 + i * SETS + j + 1 - SETS)
                    sp.dma_start(gb[j][:], gmat[ds(i * SETS + j, 1)].rearrange("o a t -> a (o t)"))\
                      .then_inc(g_in[j], 16)
                for j in range(SETS):
                    sp.wait_ge(y_ready, 16 + i * (2 * OUTS) + (j // SUM + 1) * OUTS - 2 * OUTS)
                    sp.dma_start(vb[j][:], v_view[ds(i * SETS + j, 1)].rearrange("o a d -> a (o d)"))\
                      .then_inc(v_in[j], 16)

        @block.tensor
        def _(pe):
            with pe.Fori(0, trips) as i:
                for j in range(SETS):
                    pe.wait_ge(u_in[j], i * 16 + 16)
                    pe.wait_ge(h_there, 4 + i * SETS + j + 1 - SUM)
                    for k in range(KD):
                        mm = pe.matmul(bank_h[j % SUM][:], u[j][:, k, :], xT[:, k, :], start=k == 0,
                                       stop=k == KD - 1)
                    mm.then_inc(h_ready, 1)
                for part in range(SETS // SUM):
                    pe.wait_ge(p_ready, 8 + i * SETS + (part + 1) * SUM)
                    for j in range(part * SUM, (part + 1) * SUM):
                        pe.wait_ge(v_in[j], i * 16 + 16)
                    for o in range(OUTS):
                        m, half = o // 2, o % 2
                        pe.wait_ge(y_taken, 4 + i * (2 * OUTS) + part * OUTS + o + 1 - 4)
                        for n in range(SUM):
                            j = part * SUM + n
                            mm = pe.matmul(bank_y[o % 4][:], prod[j][:, m * P:(m + 1) * P],
                                           vb[j][:, half * 512:(half + 1) * 512], start=n == 0, stop=n == SUM - 1)
                        mm.then_inc(y_ready, 1)

        @block.scalar
        def _(act):
            with act.Fori(0, trips) as i:
                for j in range(SETS):
                    act.wait_ge(h_ready, 8 + i * SETS + j + 1)
                    act.wait_ge(p_ready, 8 + i * SETS + j + 1 - SUM)
                    act.activation(act_h[j % SUM][:], bank_h[j % SUM][:], ACT.Gelu_apprx_tanh).then_inc(h_there, 1)

        @block.vector
        def _(v):
            v.wait_ge(cleared, 1)
            with v.Fori(0, trips) as i:
                for j in range(SETS):
                    v.wait_ge(h_there, 4 + i * SETS + j + 1)
                    v.wait_ge(g_in[j], i * 16 + 16)
                    v.wait_ge(y_ready, 16 + i * (2 * OUTS))
                    v.tensor_tensor(prod[j][:], act_h[j % SUM][:], gb[j][:], ALU.mult).then_inc(p_ready, 1)
                for n in range(2 * OUTS):
                    o = n % OUTS
                    part = y[:, o // 2, (o % 2) * 512:(o % 2 + 1) * 512]
                    v.wait_ge(y_ready, 16 + i * (2 * OUTS) + n + 1)
                    v.wait_ge(y_taken, 4 + i * (2 * OUTS) + n + 1 - 4)
                    v.tensor_tensor(part, bank_y[o % 4][:], part, ALU.add).then_inc(y_taken, 1)
            v.wait_ge(y_taken, 4 + trips * 2 * OUTS)
            v.tensor_tensor(x[:], x[:], y[:], ALU.add)


def peer(nc, c, tag, x, a, l):
    gmat = nc.dram_tensor(f"{tag}_gmat", (PEER_K, PEER_K, SEQ), F32, kind="Internal").ap()
    with Tiles(nc, tag) as keep:
        xT = keep.sb("xT", [P, KD, SEQ])
        normed_transpose(nc, c, tag + "n", x, a[f"{l}_ffn_norm"], xT)
        with Tiles(nc, tag + "g") as t:
            names = ("gT", "rT", "cT")
            turned = [t.sb(n, [P, SEQ]) for n in names]
            with Tiles(nc, tag + "r") as t2:
                parts = [t2.sb(n, [P, NT, P]) for n in ("gates", "rows", "cols")]
                retrieve(nc, c, tag + "q", xT, a[f"{l}_peer_wq"], a[f"{l}_peer_subkeysT"], *parts)
                turn(nc, c, tag + "t", [(d[:], [p[:, m, :] for m in range(NT)], P) for d, p in zip(turned, parts)])
            spread_gates(nc, c, tag + "s", *turned, gmat)
        all_experts(nc, c, tag + "e", xT, a[f"{l}_peer_uT"], a[f"{l}_peer_v"], gmat, x)


def store(nc, c, tag, x, out):
    with Tiles(nc, tag) as t:
        stored = t.sem("stored")
        block = t.block()

        @block.sync
        def _(sp):
            sp.dma_start(out.rearrange("(t p) d -> p t d", p=P), x[:]).then_inc(stored, 16)
            sp.wait_ge(stored, 16)


def trunk(nc, a, tables, out):
    with Tiles(nc, "all") as t:
        c = Consts(nc, t, tables)
        x = t.sb("x", [P, NT, D])
        load_all(nc, t, c, a["x"], x)
        layer0_mixer(nc, c, x, a)
        end_half(nc)
        peer(nc, c, "f0", x, a, "l0")
        end_half(nc)
        layer1_mixer(nc, c, x, a)
        end_half(nc)
        peer(nc, c, "f1", x, a, "l1")
        store(nc, c, "out", x, out)


def host_tables():
    f = np.float32
    half = HD // 2
    inv = (f(10000.0) ** (-np.arange(half, dtype=f) / f(half))).astype(f)

    def rope(pos):
        ang = pos.astype(f)[:, None] * inv[None, :]
        return np.cos(ang).astype(f), np.sin(ang).astype(f)

    cos, sin = rope(np.arange(SEQ))
    tiles = lambda m: np.ascontiguousarray(m.reshape(NT, P, half).transpose(1, 0, 2))
    pos = np.tile(np.arange(32) * CMP_STRIDE + CMP_LEN - 1, 2)
    ccos, csin = rope(pos)
    i = np.arange(P)
    same = (i[:, None] // GLA_C) == (i[None, :] // GLA_C)
    tq = np.arange(SEQ).reshape(NT, P).T
    cmask = ((np.arange(32) * CMP_STRIDE + CMP_LEN - 1)[None, None, :] <= tq[:, :, None]).astype(f)
    return {
        "ident": np.eye(P, dtype=f),
        "causal": np.where(i[None, :] <= i[:, None], 0.0, NEG).astype(f),
        "cos": tiles(cos), "sin": tiles(sin),
        "ccos": ccos[:, None, :], "csin": csin[:, None, :],
        "cmask": cmask, "cbias": np.where(cmask > 0, 0.0, NEG).astype(f),
        "upto": (same & (i[:, None] <= i[None, :])).astype(f),
        "after": (same & (i[:, None] > i[None, :])).astype(f),
        "chunk": ((i[:, None] // GLA_C) == np.arange(4)[None, :]).astype(f),
        "iota": np.tile(np.arange(P, dtype=f), (P, 1)),
    }


def lay_out(inputs):
    f = {k: np.asarray(v) for k, v in inputs.items()}
    out = {k: np.ascontiguousarray(v) for k, v in f.items() if not k.startswith("l0_s5") and not k.endswith("_peer_u")
           and not k.endswith("_peer_subkeys")}
    out["x"] = f["x"].reshape(SEQ, D)
    out["l0_s5_w_glu"] = f["l0_s5_w_glu"]

    def states(m):
        m = m.reshape(S5_GP, 2, *m.shape[1:])
        m = np.moveaxis(m, 0, 2)
        return np.ascontiguousarray(m.reshape(P, *m.shape[2:]))

    out["log_dt"] = states(np.repeat(f["l0_s5_log_dt"][:, None], S5_P, axis=1))
    out["a_re"], out["a_im"] = states(f["l0_s5_a_re"]), states(f["l0_s5_a_im"])
    out["b_re"], out["b_im"] = states(f["l0_s5_b_re"]), states(f["l0_s5_b_im"])
    out["c_re"] = states(np.swapaxes(f["l0_s5_c_re"], 1, 2))
    out["c_im"] = states(np.swapaxes(f["l0_s5_c_im"], 1, 2))
    out["d_skip"] = np.ascontiguousarray(f["l0_s5_d"].T)
    out["b_glu"] = np.ascontiguousarray(f["l0_s5_b_glu"].reshape(4, P).T)
    out["l1_nsa_cmp_pos"] = np.ascontiguousarray(f["l1_nsa_cmp_pos"].T)
    for l in ("l0", "l1"):
        u = f[f"{l}_peer_u"].reshape(PEER_K, PEER_K, KD, P)
        out[f"{l}_peer_uT"] = np.ascontiguousarray(u.transpose(1, 3, 2, 0)).reshape(PEER_K, P, D)
        sk = f[f"{l}_peer_subkeys"].reshape(NLIST, PEER_K, P)
        out[f"{l}_peer_subkeysT"] = np.ascontiguousarray(sk.transpose(2, 0, 1))
    return out


def kernel(**inputs):
    import concourse.bacc as bacc
    from concourse.bass_utils import run_bass_kernel_spmd as run

    nc = bacc.Bacc("TRN2", target_bir_lowering=False, num_devices=1)
    arrays = lay_out(inputs)
    tables = host_tables()
    aps = {k: nc.dram_tensor(k, v.shape, mybir.dt.from_np(v.dtype), kind="ExternalInput").ap()
           for k, v in arrays.items()}
    taps = {k: nc.dram_tensor(f"table_{k}", v.shape, F32, kind="ExternalInput").ap() for k, v in tables.items()}
    out = nc.dram_tensor("out", (SEQ, D), F32, kind="ExternalOutput").ap()
    trunk(nc, aps, taps, out)
    r = run(nc, [{**arrays, **{f"table_{k}": v for k, v in tables.items()}}], core_ids=[0])
    return r.results[0]["out"].reshape(1, SEQ, D)
```

```python
from contextlib import ExitStack

import numpy as np

import concourse.bass as bass
from concourse import mybir

F32 = mybir.dt.float32
F32R = mybir.dt.float32r
U32 = mybir.dt.uint32
ALU = mybir.AluOpType
ACT = mybir.ActivationFunctionType
AX = mybir.AxisListType
ds = bass.ds

P = 128
D = 1024
KD = D // P
SEQ = 512
NT = SEQ // P
HD = 64
NH = 8
EPS = 1e-6
NEG = -1e30
TAKEN = -3e38
LEAD = 1

S5_G, S5_C, S5_P = 32, 16, 64
S5_L = 8
S5_NC = SEQ // S5_L
S5_GP = S5_G // 2
WIDTH_B = S5_G * S5_C

L0_COLS = dict(q=(0, 512), k=(512, 128), v=(640, 128), iq=(768, 512), ik=(1280, 64), iw=(1344, 8), u=(1352, 512))
L1_COLS = dict(q=(0, 512), kc=(512, 128), vc=(640, 128), ks=(768, 128), vs=(896, 128), kw=(1024, 128),
               vw=(1152, 128), gl=(1280, 24), gq=(1304, 256), gk=(1560, 256), gv=(1816, 512),
               glow=(2328, 16), gr=(2344, 512))
L0_WIDTH = 1352
L1_WIDTH = 2856
TOPK_ATT = 128
CMP_LEN, CMP_STRIDE, CMP_HID = 32, 16, 256
NCMP = (SEQ - CMP_LEN) // CMP_STRIDE + 1
GLA_H, GLA_K, GLA_V, GLA_C = 4, 64, 128, 32
GLA_N = SEQ // GLA_C
PEER_H, PEER_K, PEER_TOP = 8, 128, 16
NLIST = 2 * PEER_H


class Tiles:

    opened = []

    def __init__(self, nc, tag):
        self.nc, self.tag, self.stack = nc, tag, ExitStack()

    def __enter__(self):
        self.stack.__enter__()
        return self

    def __exit__(self, *a):
        return self.stack.__exit__(*a)

    def sb(self, name, shape, dt=F32):
        return self.stack.enter_context(self.nc.sbuf_tensor(f"{self.tag}_{name}", shape, dt))

    def banks(self, name, n=1):
        return [self.stack.enter_context(self.nc.psum_tensor(f"{self.tag}_{name}{i}", [P, 512], F32))
                for i in range(n)]

    def sem(self, name):
        Tiles.opened.append(self.nc.alloc_semaphore(f"{self.tag}_{name}"))
        return Tiles.opened[-1]

    def sems(self, name, n):
        return [self.sem(f"{name}{i}") for i in range(n)]

    def lead(self, name, by=LEAD):
        sem = self.sem(name)
        self.nc.sync.sem_inc(sem, by)
        return sem

    def leads(self, name, n):
        return [self.lead(f"{name}{i}") for i in range(n)]

    def block(self):
        return self.stack.enter_context(self.nc.Block())


def end_half(nc):
    nc.all_engine_barrier()
    nc.clear_and_free_semaphores(Tiles.opened)
    Tiles.opened.clear()
    nc.all_engine_barrier()


class Chain:

    def __init__(self, eng, sem):
        self.eng, self.sem, self.n, self.off = eng, sem, 0, 0

    def put(self, ins):
        self.n += 1
        ins.then_inc(self.sem, 1)

    def link(self, ins):
        self.put(ins)
        self.eng.wait_ge(self.sem, self.n + self.off)

    def enter(self, i, per):
        self.off, self.per, self.first = i * per, per, self.n

    def leave(self, trips):
        assert self.n == self.first + self.per, (self.n - self.first, self.per)
        self.n, self.off = self.first + trips * self.per, 0


class Consts:

    def __init__(self, nc, t, tables):
        self.loaded = t.stack.enter_context(nc.semaphore("constants_loaded"))
        self.n = 16 * len(tables)
        self.tile, self.src = {}, tables
        for name, ap in tables.items():
            self.tile[name] = t.sb(name, list(ap.shape))

    def __getitem__(self, name):
        return self.tile[name]

    def there(self, eng):
        eng.wait_ge(self.loaded, self.n)


def bc(ap, axis, n):
    a = ap.unsqueeze(axis)
    shape = list(a.shape)
    shape[axis] = n
    return a.broadcast_to(shape)


def passes(pe, out, w, m, first, final):
    pe.matmul(out, w[0], m[0], start=first, stop=False)
    pe.matmul(out, w[0], m[1], start=False, stop=False)
    return pe.matmul(out, w[1], m[0], start=False, stop=final)


def load_all(nc, t, c, x_in, x):
    x_loaded = t.sem("x_loaded")
    with nc.Block() as block:
        @block.sync
        def _(sp):
            sp.dma_start(x[:], x_in.rearrange("(t p) d -> p t d", p=P)).then_inc(x_loaded, 16)
            for name, ap in c.src.items():
                sp.dma_start(c[name][:], ap).then_inc(c.loaded, 16)
            sp.wait_ge(x_loaded, 16)
            sp.wait_ge(c.loaded, c.n)


def rstd_steps(v, ch, ms, root, r, root_ready, count):
    v.wait_ge(root_ready, count)
    ch.link(v.reciprocal(r, root))
    ch.link(v.tensor_tensor(root, r, r, ALU.mult))
    ch.link(v.tensor_tensor(root, root, ms, ALU.mult))
    ch.link(v.tensor_scalar(root, root, -0.5, 1.5, ALU.mult, ALU.add))
    ch.link(v.tensor_tensor(r, r, root, ALU.mult))


def normed_transpose(nc, c, tag, x, gain_dram, hT):
    with Tiles(nc, tag) as t:
        gain = t.sb("gain", [P, D])
        xn = t.sb("xn", [P, NT, D])
        ms, root, r = t.sb("ms", [P, NT]), t.sb("root", [P, NT]), t.sb("r", [P, NT])
        bank = t.banks("turned", 4)
        gain_in, ms_ready, root_ready = t.sem("gain_in"), t.sem("ms_ready"), t.sem("root_ready")
        dve, turned, taken, normed = t.sem("dve"), t.sem("turned"), t.sems("taken", 4), t.sem("normed")
        high = t.sem("high")
        block = t.block()

        @block.sync
        def _(sp):
            sp.dma_start(gain[:], gain_dram.partition_broadcast(P)).then_inc(gain_in, 16)

        @block.vector
        def _(v):
            ch = Chain(v, dve)
            for i in range(NT):
                ch.put(v.tensor_tensor_reduce(out=xn[:, i, :], in0=x[:, i, :], in1=x[:, i, :], scale=1.0 / D,
                                              scalar=0.0, op0=ALU.mult, op1=ALU.add, accum_out=ms[:, i:i + 1]))
            v.wait_ge(dve, ch.n)
            v.tensor_scalar(ms[:], ms[:], EPS, None, ALU.add).then_inc(ms_ready, 1)
            rstd_steps(v, ch, ms[:], root[:], r[:], root_ready, 1)
            v.wait_ge(gain_in, 16)
            for i in range(NT):
                v.scalar_tensor_tensor(out=xn[:, i, :], in0=x[:, i, :], scalar=r[:, i:i + 1], in1=gain[:],
                                       op0=ALU.mult, op1=ALU.mult).then_inc(normed, 1)
            for k in range(KD):
                v.wait_ge(high, k + 1)
                v.tensor_tensor(hT[1][:, k, :], bank[k % 4][:], hT[0][:, k, :].bitcast(F32),
                                ALU.subtract).then_inc(taken[k % 4], 1)

        @block.scalar
        def _(act):
            act.wait_ge(ms_ready, 1)
            act.activation(root[:], ms[:], ACT.Sqrt).then_inc(root_ready, 1)
            for k in range(KD):
                act.wait_ge(turned, k + 1)
                act.copy(hT[0][:, k, :], bank[k % 4][:]).then_inc(high, 1)

        @block.tensor
        def _(pe):
            c.there(pe)
            pe.wait_ge(normed, NT)
            for k in range(KD):
                if k >= 4:
                    pe.wait_ge(taken[k % 4], k // 4)
                for i in range(NT):
                    mm = pe.transpose(bank[k % 4][:, i * P:(i + 1) * P], xn[:, i, k * P:(k + 1) * P], c["ident"][:])
                mm.then_inc(turned, 1)


def project(nc, c, tag, lhsT, w, width, step, dst, add=False):
    w_view = w.rearrange("(k p) n -> p k n", p=P)
    kk = w_view.shape[1]
    trips = width // (2 * step)
    assert trips * 2 * step == width
    with Tiles(nc, tag) as t:
        raw = [t.sb(f"raw{s}", [P, kk, step]) for s in range(2)]
        halves = [[t.sb(f"w{s}{half}", [P, kk, step], F32R) for half in "hl"] for s in range(2)]
        bank = t.banks("out", 8)
        w_in, high, low = t.sems("w_in", 2), t.sems("high", 2), t.leads("low", 2)
        ready, taken = t.leads("ready", 2), t.leads("taken", 2)
        block = t.block()

        @block.sync
        def _(sp):
            with sp.Fori(0, trips) as i:
                for s in range(2):
                    sp.wait_ge(low[s], LEAD + i)
                    sp.dma_start(raw[s][:], w_view[:, :, ds((i * 2 + s) * step, step)]).then_inc(w_in[s], 16)

        @block.scalar
        def _(act):
            with act.Fori(0, trips) as i:
                for s in range(2):
                    act.wait_ge(w_in[s], i * 16 + 16)
                    act.wait_ge(ready[s], LEAD + i * NT)
                    act.copy(halves[s][0][:], raw[s][:]).then_inc(high[s], 1)

        @block.gpsimd
        def _(pool):
            with pool.Fori(0, trips) as i:
                for s in range(2):
                    pool.wait_ge(high[s], i + 1)
                    pool.tensor_tensor(halves[s][1][:], raw[s][:], halves[s][0][:].bitcast(F32),
                                       ALU.subtract).then_inc(low[s], 1)

        @block.tensor
        def _(pe):
            with pe.Fori(0, trips) as i:
                for s in range(2):
                    pe.wait_ge(low[s], LEAD + i + 1)
                    pe.wait_ge(taken[s], LEAD + i * NT)
                    for m in range(NT):
                        for k in range(kk):
                            mm = passes(pe, bank[s * 4 + m][:, 0:step], [h[:, k, m * P:(m + 1) * P] for h in lhsT],
                                        [h[:, k, :] for h in halves[s]], k == 0, k == kk - 1)
                        mm.then_inc(ready[s], 1)

        @block.vector
        def _(v):
            with v.Fori(0, trips) as i:
                for s in range(2):
                    for m in range(NT):
                        out = dst[:, m, ds((i * 2 + s) * step, step)]
                        v.wait_ge(ready[s], LEAD + i * NT + m + 1)
                        if add:
                            ins = v.tensor_tensor(out, bank[s * 4 + m][:, 0:step], out, ALU.add)
                        else:
                            ins = v.tensor_copy(out, bank[s * 4 + m][:, 0:step])
                        ins.then_inc(taken[s], 1)


def prepare_heads(nc, c, tag, jobs, cos, sin):
    with Tiles(nc, tag) as t:
        rows, nt = jobs[0][0].shape[0], jobs[0][0].shape[1]
        widest = max(a.shape[2] for a, _ in jobs)
        ta, tb = t.sb("ta", [rows, nt, widest, HD]), t.sb("tb", [rows, nt, widest, HD])
        ms, root, r = [t.sb(n, [rows, nt, widest]) for n in ("ms", "root", "r")]
        gains = [g for _, g in jobs if g is not None]
        gain = t.sb("gain", [rows, max(len(gains), 1), HD])
        dve, ms_ready, root_ready, gain_in = t.sem("dve"), t.sem("ms_ready"), t.sem("root_ready"), t.sem("gain_in")
        block = t.block()

        @block.sync
        def _(sp):
            for n, g in enumerate(gains):
                sp.dma_start(gain[:, n, :], g.partition_broadcast(rows)).then_inc(gain_in, 16)

        @block.vector
        def _(v):
            ch = Chain(v, dve)
            n = 0
            for a, g in jobs:
                heads = a.shape[2]
                if g is not None:
                    full, few = [rows, nt, heads, HD], slice(0, heads)
                    ch.link(v.tensor_tensor(ta[:, :, few, :], a, a, ALU.mult))
                    ch.link(v.tensor_reduce(ms[:, :, few], ta[:, :, few, :], AX.X, ALU.add))
                    v.tensor_scalar(ms[:, :, few], ms[:, :, few], 1.0 / HD, EPS, ALU.mult,
                                    ALU.add).then_inc(ms_ready, 1)
                    n += 1
                    rstd_steps(v, ch, ms[:, :, few], root[:, :, few], r[:, :, few], root_ready, n)
                    v.wait_ge(gain_in, 16 * len(gains))
                    ch.link(v.tensor_tensor(a, a, r[:, :, few].unsqueeze(3).broadcast_to(full), ALU.mult))
                    ch.link(v.tensor_tensor(a, a, gain[:, n - 1, :].unsqueeze(1).unsqueeze(1).broadcast_to(full),
                                            ALU.mult))
                x1, x2 = a[:, :, :, 0:HD // 2], a[:, :, :, HD // 2:HD]
                cs, sn = [bc(m, 2, heads) for m in (cos, sin)]
                a1, a2 = ta[:, :, 0:heads, 0:HD // 2], ta[:, :, 0:heads, HD // 2:HD]
                b1, b2 = tb[:, :, 0:heads, 0:HD // 2], tb[:, :, 0:heads, HD // 2:HD]
                ch.put(v.tensor_tensor(a1, x1, cs, ALU.mult))
                ch.put(v.tensor_tensor(a2, x2, sn, ALU.mult))
                ch.put(v.tensor_tensor(b1, x1, sn, ALU.mult))
                ch.link(v.tensor_tensor(b2, x2, cs, ALU.mult))
                ch.put(v.tensor_tensor(x1, a1, a2, ALU.subtract))
                ch.link(v.tensor_tensor(x2, b1, b2, ALU.add))

        @block.scalar
        def _(act):
            n = 0
            for a, g in jobs:
                if g is not None:
                    few = slice(0, a.shape[2])
                    n += 1
                    act.wait_ge(ms_ready, n)
                    act.activation(root[:, :, few], ms[:, :, few], ACT.Sqrt).then_inc(root_ready, 1)


def turn(nc, c, tag, blocks, zero=()):
    with Tiles(nc, tag) as t:
        bank = t.banks("turned", 4)
        turned, taken, high = t.sem("turned"), t.sems("taken", 4), t.sem("high")
        block = t.block()
        split = isinstance(blocks[0][0], tuple)

        @block.tensor
        def _(pe):
            c.there(pe)
            for n, (dst, srcs, rows) in enumerate(blocks):
                if n >= 4:
                    pe.wait_ge(taken[n % 4], n // 4)
                at = 0
                for src in srcs:
                    k = src.shape[0]
                    mm = pe.transpose(bank[n % 4][0:rows, at:at + k], src, c["ident"][0:k, 0:k])
                    at += k
                mm.then_inc(turned, 1)

        def turned_block(n):
            _, srcs, rows = blocks[n]
            return bank[n % 4][0:rows, 0:sum(s.shape[0] for s in srcs)]

        @block.gpsimd
        def _(pool):
            for z in zero:
                pool.memset(z, 0.0)

        @block.vector
        def _(v):
            for n, (dst, _, _) in enumerate(blocks):
                if split:
                    v.wait_ge(high, n + 1)
                    v.tensor_tensor(dst[1], turned_block(n), dst[0].bitcast(F32),
                                    ALU.subtract).then_inc(taken[n % 4], 1)
                elif n % 2 == 0:
                    v.wait_ge(turned, n + 1)
                    v.tensor_copy(dst, turned_block(n)).then_inc(taken[n % 4], 1)

        @block.scalar
        def _(act):
            for n, (dst, _, _) in enumerate(blocks):
                if split:
                    act.wait_ge(turned, n + 1)
                    act.copy(dst[0], turned_block(n)).then_inc(high, 1)
                elif n % 2 == 1:
                    act.wait_ge(turned, n + 1)
                    act.copy(dst, turned_block(n)).then_inc(taken[n % 4], 1)


def index_scores(nc, c, tag, iq, iw, ikT, score):
    with Tiles(nc, tag) as t:
        staged = t.sb("staged", [P, NT, P])
        qT = t.sb("qT", [P, SEQ])
        rel = [t.sb(f"rel{m}", [P, (m + 1) * P]) for m in range(1, NT)]
        bank_q = t.banks("q")[0]
        bank = t.banks("s", NT - 1)
        q_staged, q_turned, q_there = t.sem("q_staged"), t.lead("q_turned"), t.sem("q_there")
        s_ready, rel_ready, rel_used, cleared = t.lead("s_ready"), t.lead("rel_ready"), t.lead("rel_used"), t.sem("clr")
        block = t.block()
        M = NT - 1

        @block.gpsimd
        def _(pool):
            pool.memset(score[:], 0.0).then_inc(cleared, 1)
            pool.memset(staged[:], 0.0).then_inc(cleared, 1)
            pool.wait_ge(cleared, 2)
            with pool.Fori(0, NH) as h:
                pool.wait_ge(q_turned, LEAD + h)
                pool.tensor_copy(staged[:, :, 0:HD], iq[:, :, ds(h * HD, HD)]).then_inc(q_staged, 1)

        @block.tensor
        def _(pe):
            c.there(pe)
            with pe.Fori(0, NH) as h:
                pe.wait_ge(q_staged, h + 1)
                for m in range(NT):
                    mm = pe.transpose(bank_q[:, m * P:(m + 1) * P], staged[:, m, :], c["ident"][:])
                mm.then_inc(q_turned, 1)
                pe.wait_ge(q_there, h + 1)
                pe.wait_ge(rel_ready, LEAD + h * M)
                for m in range(1, NT):
                    n = (m + 1) * P
                    pe.matmul(bank[m - 1][:, 0:n], qT[:, m * P:(m + 1) * P], ikT[:, 0:n],
                              start=True, stop=True).then_inc(s_ready, 1)

        @block.scalar
        def _(act):
            with act.Fori(0, NH) as h:
                act.wait_ge(q_turned, LEAD + h + 1)
                act.wait_ge(s_ready, LEAD + h * M)
                act.copy(qT[:], bank_q[:]).then_inc(q_there, 1)
                for m in range(1, NT):
                    act.wait_ge(s_ready, LEAD + h * M + m)
                    act.wait_ge(rel_used, LEAD + h * M)
                    act.activation(rel[m - 1][:], bank[m - 1][:, 0:(m + 1) * P], ACT.Relu,
                                   scale=HD ** -0.5).then_inc(rel_ready, 1)

        @block.vector
        def _(v):
            v.wait_ge(cleared, 2)
            with v.Fori(0, NH) as h:
                for m in range(1, NT):
                    s = score[:, m, 0:(m + 1) * P]
                    v.wait_ge(rel_ready, LEAD + h * M + m)
                    v.wait_ge(rel_used, LEAD + h * M)
                    v.scalar_tensor_tensor(out=s, in0=rel[m - 1][:], scalar=iw[:, m, ds(h, 1)], in1=s,
                                           op0=ALU.mult, op1=ALU.add).then_inc(rel_used, 1)


def select_keys(nc, c, tag, score, bias):
    with Tiles(nc, tag) as t:
        best = [t.sb(f"best{m}", [P, 8]) for m in range(NT)]
        dve = t.sem("dve")
        block = t.block()

        @block.vector
        def _(v):
            ch = Chain(v, dve)
            c.there(v)
            for m in range(1, NT):
                diag = score[:, m, m * P:(m + 1) * P]
                ch.put(v.tensor_tensor(diag, diag, c["causal"][:], ALU.add))
            ch.link(v.tensor_copy(bias[:, 0, 0:P], c["causal"][:]))
            for _ in range(TOPK_ATT // 8):
                for m in range(1, NT):
                    ch.put(v.max(best[m][:], score[:, m, 0:(m + 1) * P]))
                v.wait_ge(dve, ch.n)
                for m in range(1, NT):
                    s = score[:, m, 0:(m + 1) * P]
                    ch.put(v.match_replace(s, best[m][:], s, TAKEN))
                v.wait_ge(dve, ch.n)
            for m in range(1, NT):
                n = (m + 1) * P
                ch.put(v.tensor_scalar(bias[:, m, 0:n], score[:, m, 0:n], TAKEN / 2, -NEG, ALU.is_lt, ALU.mult))
            v.wait_ge(dve, ch.n)
            for m in range(1, NT):
                n = (m + 1) * P
                ch.put(v.tensor_scalar(bias[:, m, 0:n], bias[:, m, 0:n], NEG, None, ALU.add))
            v.wait_ge(dve, ch.n)


def causal_bias(nc, c, tag, bias):
    with Tiles(nc, tag) as t:
        dve = t.sem("dve")
        block = t.block()

        @block.vector
        def _(v):
            ch = Chain(v, dve)
            c.there(v)
            ch.link(v.memset(bias[:], 0.0))
            for m in range(NT):
                ch.link(v.tensor_copy(bias[:, m, m * P:(m + 1) * P], c["causal"][:]))


def attention(nc, c, tag, q, kT, vals, bias, out, gate=None, add=False):
    with Tiles(nc, tag) as t:
        staged = t.sb("staged", [P, NT, P])
        qT = t.sb("qT", [P, SEQ])
        sm = [t.sb(f"sm{m}", [P, (m + 1) * P]) for m in range(NT)]
        pT = [t.sb(f"pT{b}", [P, SEQ]) for b in range(2)]
        mx, nmx, den, rden = [t.sb(n, [P, NT]) for n in ("mx", "nmx", "den", "rden")]
        bank_q = t.banks("q")[0]
        bank_s, bank_t, bank_o = t.banks("s", 2), t.banks("t", 2), t.banks("o", 2)
        q_staged, q_turned, q_there = t.sem("q_staged"), t.lead("q_turned"), t.sem("q_there")
        s_ready, s_taken = t.lead("s_ready"), t.leads("s_taken", 2)
        m_ready, p_ready = t.sem("m_ready"), t.sem("p_ready")
        t_ready, t_taken = t.lead("t_ready"), t.leads("t_taken", 2)
        o_ready, o_taken, dve = t.sem("o_ready"), t.leads("o_taken", 2), t.sem("dve")
        cleared, wait_taker = t.sem("cleared"), t.sb("wait_taker", [P, 1])
        block = t.block()

        @block.gpsimd
        def _(pool):
            pool.memset(staged[:], 0.0).then_inc(cleared, 1)
            pool.wait_ge(cleared, 1)
            with pool.Fori(0, NH) as h:
                pool.wait_ge(q_turned, LEAD + h)
                pool.tensor_copy(staged[:, :, 0:HD], q[:, :, ds(h * HD, HD)]).then_inc(q_staged, 1)

        @block.tensor
        def _(pe):
            def scores(h, g, m):
                b = m % 2
                pe.wait_ge(s_taken[b], LEAD + h * 2 + m // 2)
                n = (m + 1) * P
                pe.matmul(bank_s[b][:, 0:n], qT[:, m * P:(m + 1) * P],
                          kT[:, ds(g, 1), 0:n].rearrange("p a n -> p (a n)"),
                          start=True, stop=True).then_inc(s_ready, 1)

            def turn_probs(h, m):
                pe.wait_ge(p_ready, h * NT + m + 1)
                pe.wait_ge(t_taken[m % 2], LEAD + h * 2 + m // 2)
                for s in range(m + 1):
                    mm = pe.transpose(bank_t[m % 2][:, s * P:(s + 1) * P], sm[m][:, s * P:(s + 1) * P], c["ident"][:])
                mm.then_inc(t_ready, 1)

            def weigh(h, g, m):
                pe.wait_ge(t_taken[m % 2], LEAD + h * 2 + m // 2 + 1)
                pe.wait_ge(o_taken[m % 2], LEAD + h * 2 + m // 2)
                for s in range(m + 1):
                    mm = pe.matmul(bank_o[m % 2][:, 0:HD], pT[m % 2][:, s * P:(s + 1) * P],
                                   vals[:, s, ds(g * HD, HD)], start=s == 0, stop=s == m)
                mm.then_inc(o_ready, 1)

            c.there(pe)
            with pe.Fori(0, 2) as g:
                with pe.Fori(0, NH // 2) as r:
                    h = g * (NH // 2) + r
                    pe.wait_ge(q_staged, h + 1)
                    for m in range(NT):
                        mm = pe.transpose(bank_q[:, m * P:(m + 1) * P], staged[:, m, :], c["ident"][:])
                    mm.then_inc(q_turned, 1)
                    pe.wait_ge(q_there, h + 1)
                    scores(h, g, 0)
                    scores(h, g, 1)
                    for m in range(NT):
                        turn_probs(h, m)
                        if m + 2 < NT:
                            scores(h, g, m + 2)
                        weigh(h, g, m)

        @block.scalar
        def _(act):
            with act.Fori(0, NH) as h:
                act.wait_ge(q_turned, LEAD + h + 1)
                act.wait_ge(s_ready, LEAD + h * NT)
                act.copy(qT[:], bank_q[:]).then_inc(q_there, 1)
                for m in range(NT):
                    act.wait_ge(m_ready, h * NT + m + 1)
                    act.activation(sm[m][:], sm[m][:], ACT.Exp, bias=nmx[:, m:m + 1],
                                   accum_out=den[:, m:m + 1]).then_inc(p_ready, 1)

        @block.vector
        def _(v):
            ch = Chain(v, dve)

            def add_bias(h, m):
                n = (m + 1) * P
                v.wait_ge(s_ready, LEAD + h * NT + m + 1)
                v.wait_ge(t_ready, LEAD + h * NT)
                v.memset(wait_taker[:], 0.0)
                ins = v.tensor_tensor_reduce(out=sm[m][:], in0=bank_s[m % 2][:, 0:n], in1=bias[:, m, 0:n],
                                             scale=HD ** -0.5, scalar=TAKEN, op0=ALU.add, op1=ALU.max,
                                             accum_out=mx[:, m:m + 1])
                ins.then_inc(s_taken[m % 2], 1)
                v.wait_ge(s_taken[m % 2], LEAD + h * 2 + m // 2 + 1)
                v.tensor_scalar(nmx[:, m:m + 1], mx[:, m:m + 1], -1.0, None, ALU.mult).then_inc(m_ready, 1)

            with v.Fori(0, NH) as h:
                ch.enter(h, NT * (2 if gate is None else 3))
                add_bias(h, 0)
                add_bias(h, 1)
                for m in range(NT):
                    n = (m + 1) * P
                    v.wait_ge(t_ready, LEAD + h * NT + m + 1)
                    ins = v.tensor_copy(pT[m % 2][:, 0:n], bank_t[m % 2][:, 0:n])
                    ins.then_inc(t_taken[m % 2], 1)
                    if m + 2 < NT:
                        add_bias(h, m + 2)
                    v.wait_ge(p_ready, h * NT + m + 1)
                    ch.link(v.tensor_scalar(rden[:, m:m + 1], den[:, m:m + 1], 1e-30, None, ALU.max))
                    ch.link(v.reciprocal(rden[:, m:m + 1], rden[:, m:m + 1]))
                    if gate is not None:
                        ch.link(v.tensor_tensor(rden[:, m:m + 1], rden[:, m:m + 1], gate[:, m, ds(h, 1)], ALU.mult))
                    o = out[:, m, ds(h * HD, HD)]
                    v.wait_ge(o_ready, h * NT + m + 1)
                    if add:
                        ins = v.scalar_tensor_tensor(out=o, in0=bank_o[m % 2][:, 0:HD], scalar=rden[:, m:m + 1],
                                                     in1=o, op0=ALU.mult, op1=ALU.add)
                    else:
                        ins = v.tensor_scalar(o, bank_o[m % 2][:, 0:HD], rden[:, m:m + 1], None, ALU.mult)
                    ins.then_inc(o_taken[m % 2], 1)
                ch.leave(NH)


def s5_inputs(nc, c, tag, hT, w, U):
    off = L0_COLS["u"][0]
    w_view = w.rearrange("(k p) n -> p k n", p=P)[:, :, off:off + WIDTH_B]
    PAIRS, STEP, HALF = S5_L // 2, WIDTH_B // 2, S5_G // 2
    with Tiles(nc, tag) as t:
        raw = [t.sb(f"raw{s}", [P, KD, STEP]) for s in range(2)]
        halves = [[t.sb(f"w{s}{half}", [P, KD, STEP], F32R) for half in "hl"] for s in range(2)]
        u_sb = t.sb("u", [P, S5_G, PAIRS, S5_C])
        bank = t.banks("out", 4)
        bank_t = t.banks("t", 4)
        w_in, high, low = t.sems("w_in", 2), t.sem("high"), t.sem("low")
        ready, taken, turned = t.sem("ready"), t.sem("taken"), t.sem("turned")
        early_moved, moved = t.sem("early_moved"), t.sem("moved")
        block = t.block()

        @block.sync
        def _(sp):
            for s in range(2):
                sp.dma_start(raw[s][:], w_view[:, :, s * STEP:(s + 1) * STEP]).then_inc(w_in[s], 16)

        @block.gpsimd
        def _(pool):
            for s in range(2):
                pool.wait_ge(high, s + 1)
                pool.tensor_tensor(halves[s][1][:], raw[s][:], halves[s][0][:].bitcast(F32),
                                   ALU.subtract).then_inc(low, 1)

        @block.tensor
        def _(pe):
            for s in range(2):
                pe.wait_ge(low, s + 1)
                if s:
                    pe.wait_ge(taken, PAIRS)
                for l in range(PAIRS):
                    for k in range(KD):
                        mm = passes(pe, bank[l][:, 0:STEP],
                                    [h[:, k, l:SEQ:PAIRS] for h in hT],
                                    [h[:, k, :] for h in halves[s]], k == 0, k == KD - 1)
                    mm.then_inc(ready, 1)
            c.there(pe)
            pe.wait_ge(taken, 2 * PAIRS)
            for g in range(S5_G):
                b = g // 4 % 4
                if g % 4 == 0 and g >= 16:
                    pe.wait_ge(moved, g // 4 - 3)
                mm = pe.transpose(bank_t[b][0:64, (g % 4) * P:(g % 4 + 1) * P],
                                  u_sb[:, g, :, :].rearrange("p l c -> p (l c)"), c["ident"][:])
                if g % 4 == 3:
                    mm.then_inc(turned, 1)

        @block.scalar
        def _(act):
            for s in range(2):
                act.wait_ge(w_in[s], 16)
                act.copy(halves[s][0][:], raw[s][:]).then_inc(high, 1)
            for n in range(S5_G // 4):
                act.wait_ge(early_moved, n + 1)
                src = bank_t[n % 4][0:64, :].rearrange("p (g n q) -> p g n q", g=4, q=2)
                act.copy(U[64:128, 4 * n:4 * n + 4, :], src[:, :, :, 1]).then_inc(moved, 1)

        @block.vector
        def _(v):
            for s in range(2):
                for l in range(PAIRS):
                    v.wait_ge(ready, s * PAIRS + l + 1)
                    v.tensor_copy(u_sb[:, s * HALF:(s + 1) * HALF, l, :],
                                  bank[l][:, 0:STEP].rearrange("p (g c) -> p g c", c=S5_C)).then_inc(taken, 1)
            for n in range(S5_G // 4):
                v.wait_ge(turned, n + 1)
                src = bank_t[n % 4][0:64, :].rearrange("p (g n q) -> p g n q", g=4, q=2)
                v.tensor_copy(U[0:64, 4 * n:4 * n + 4, :], src[:, :, :, 0]).then_inc(early_moved, 1)


def s5_tables(nc, c, tag, ins, vr, vi, car, cai, pw8, bb):
    with Tiles(nc, tag) as t:
        raw = {n: t.sb(n, [P, S5_GP]) for n in ("log_dt", "a_re", "a_im")}
        raw3 = {n: t.sb(n, [P, S5_GP, S5_C]) for n in ("b_re", "b_im", "c_re", "c_im")}
        dt, dlr, mag, th, nn, red, half, sin_t, sin_h, cos_t, den, u1, u2, fr, fi = [
            t.sb(n, [P, S5_GP]) for n in ("dt", "dlr", "mag", "th", "nn", "red", "half", "sin_t", "sin_h", "cos_t",
                                          "den", "u1", "u2", "fr", "fi")]
        pr, pi = t.sb("pr", [P, S5_GP, S5_L + 1]), t.sb("pi", [P, S5_GP, S5_L + 1])
        qr, qi = t.sb("qr", [P, S5_GP, S5_L]), t.sb("qi", [P, S5_GP, S5_L])
        tmp = t.sb("tmp", [P, S5_GP, S5_L + 1, S5_C])
        t3 = t.sb("t3", [P, S5_GP, S5_C])
        loaded, dve, act_in, act_out = t.sem("loaded"), t.sem("dve"), t.sem("act_in"), t.sem("act_out")
        block = t.block()
        every = {**raw, **raw3}

        @block.sync
        def _(sp):
            for n, tile in every.items():
                sp.dma_start(tile[:], ins[n]).then_inc(loaded, 16)

        @block.scalar
        def _(act):
            act.wait_ge(loaded, 16 * len(every))
            act.activation(dt[:], raw["log_dt"][:], ACT.Exp).then_inc(act_out, 1)
            act.wait_ge(act_in, 1)
            act.activation(mag[:], dlr[:], ACT.Exp).then_inc(act_out, 1)
            act.wait_ge(act_in, 2)
            act.activation(sin_t[:], red[:], ACT.Sin).then_inc(act_out, 1)
            act.activation(sin_h[:], half[:], ACT.Sin).then_inc(act_out, 1)

        @block.vector
        def _(v):
            ch = Chain(v, dve)

            def tt(out, a, b, op):
                ch.link(v.tensor_tensor(out, a, b, op))

            lr, li = raw["a_re"][:], raw["a_im"][:]
            v.wait_ge(loaded, 16 * len(every))
            v.wait_ge(act_out, 1)
            v.tensor_tensor(dlr[:], dt[:], lr, ALU.mult).then_inc(act_in, 1)
            tt(th[:], dt[:], li, ALU.mult)
            rnd = 1.5 * 2 ** 23
            ch.link(v.tensor_scalar(nn[:], th[:], 0.15915494309189535, rnd, ALU.mult, ALU.add))
            ch.link(v.tensor_scalar(nn[:], nn[:], -rnd, None, ALU.add))
            c1 = 6.28125
            c2 = 0.0019350051879882812
            c3 = 2 * np.pi - c1 - c2
            src = th
            for cc in (c1, c2, c3):
                ch.link(v.scalar_tensor_tensor(out=red[:], in0=nn[:], scalar=-float(cc), in1=src[:], op0=ALU.mult,
                                               op1=ALU.add))
                src = red
            ch.link(v.tensor_scalar(red[:], red[:], 3.1415925, -3.1415925, ALU.min, ALU.max))
            v.tensor_scalar(half[:], red[:], 0.5, None, ALU.mult).then_inc(act_in, 1)
            v.wait_ge(act_out, 4)
            tt(cos_t[:], sin_h[:], sin_h[:], ALU.mult)
            ch.link(v.tensor_scalar(cos_t[:], cos_t[:], -2.0, 1.0, ALU.mult, ALU.add))
            ch.put(v.memset(pr[:, :, 0], 1.0))
            ch.put(v.memset(pi[:, :, 0], 0.0))
            ch.put(v.tensor_tensor(pr[:, :, 1], mag[:], cos_t[:], ALU.mult))
            ch.link(v.tensor_tensor(pi[:, :, 1], mag[:], sin_t[:], ALU.mult))
            ar, ai = pr[:, :, 1], pi[:, :, 1]
            for l in range(2, S5_L + 1):
                ch.put(v.tensor_tensor(u1[:], pr[:, :, l - 1], ar, ALU.mult))
                ch.put(v.tensor_tensor(u2[:], pi[:, :, l - 1], ai, ALU.mult))
                ch.put(v.tensor_tensor(fr[:], pr[:, :, l - 1], ai, ALU.mult))
                ch.link(v.tensor_tensor(fi[:], pi[:, :, l - 1], ar, ALU.mult))
                ch.put(v.tensor_tensor(pr[:, :, l], u1[:], u2[:], ALU.subtract))
                ch.link(v.tensor_tensor(pi[:, :, l], fr[:], fi[:], ALU.add))
            tt(u1[:], lr, lr, ALU.mult)
            tt(u2[:], li, li, ALU.mult)
            tt(den[:], u1[:], u2[:], ALU.add)
            ch.link(v.reciprocal(den[:], den[:]))
            ch.link(v.tensor_scalar(nn[:], ar, -1.0, None, ALU.add))
            tt(u1[:], nn[:], lr, ALU.mult)
            tt(u2[:], ai, li, ALU.mult)
            tt(fr[:], u1[:], u2[:], ALU.add)
            tt(fr[:], fr[:], den[:], ALU.mult)
            tt(u1[:], ai, lr, ALU.mult)
            tt(u2[:], nn[:], li, ALU.mult)
            tt(fi[:], u1[:], u2[:], ALU.subtract)
            tt(fi[:], fi[:], den[:], ALU.mult)
            br, bi = raw3["b_re"][:], raw3["b_im"][:]
            frb, fib = bc(fr[:], 2, S5_C), bc(fi[:], 2, S5_C)
            tt(bb[:, 0], frb, br, ALU.mult)
            tt(t3[:], fib, bi, ALU.mult)
            tt(bb[:, 0], bb[:, 0], t3[:], ALU.subtract)
            tt(bb[:, 1], frb, bi, ALU.mult)
            tt(t3[:], fib, br, ALU.mult)
            tt(bb[:, 1], bb[:, 1], t3[:], ALU.add)
            ch.put(v.tensor_copy(pw8[:, 0, :], pr[:, :, S5_L]))
            ch.put(v.tensor_copy(pw8[:, 2, :], pi[:, :, S5_L]))
            ch.put(v.tensor_scalar(pw8[:, 1, :], pi[:, :, S5_L], -1.0, None, ALU.mult))
            for l in range(S5_L):
                ch.put(v.tensor_copy(qr[:, :, l], pr[:, :, S5_L - 1 - l]))
                ch.put(v.tensor_copy(qi[:, :, l], pi[:, :, S5_L - 1 - l]))
            v.wait_ge(dve, ch.n)
            sh = [P, S5_GP, S5_L, S5_C]
            qrb, qib = bc(qr[:], 3, S5_C), bc(qi[:], 3, S5_C)
            bbr, bbi = bc(bb[:, 0], 2, S5_L), bc(bb[:, 1], 2, S5_L)
            tl = tmp[:, :, 0:S5_L, :]
            tt(vr[:], qrb, bbr, ALU.mult)
            tt(tl, qib, bbi, ALU.mult)
            tt(vr[:], vr[:], tl, ALU.subtract)
            tt(vi[:], qrb, bbi, ALU.mult)
            tt(tl, qib, bbr, ALU.mult)
            tt(vi[:], vi[:], tl, ALU.add)
            prb, pib = bc(pr[:], 3, S5_C), bc(pi[:], 3, S5_C)
            cr, ci = bc(raw3["c_re"][:], 2, S5_L + 1), bc(raw3["c_im"][:], 2, S5_L + 1)
            tt(car[:], prb, cr, ALU.mult)
            tt(tmp[:], pib, ci, ALU.mult)
            tt(car[:], car[:], tmp[:], ALU.subtract)
            tt(cai[:], pib, cr, ALU.mult)
            tt(tmp[:], prb, ci, ALU.mult)
            tt(cai[:], cai[:], tmp[:], ALU.add)
            ch.link(v.tensor_scalar(cai[:], cai[:], -1.0, None, ALU.mult))


def s5_scan(nc, c, tag, ins, U, vT, car, cai, pw8, bb, y_sb):
    LC = S5_L * S5_C
    with Tiles(nc, tag) as t:
        toep = t.sb("toep", [P, S5_G, LC])
        kern = t.sb("kern", [S5_C, S5_G, LC])
        skip, dd = t.sb("skip", [S5_C, S5_G]), t.sb("dd", [S5_C, S5_G, S5_C])
        xs = t.sb("xs", [P, 2, S5_GP, S5_NC])
        st = t.sb("st", [P, 3, S5_GP, S5_NC + 1])
        u1, u2 = t.sb("u1", [P, 2, S5_GP]), t.sb("u2", [P, 2, S5_GP])
        bank = t.banks("b", 8)
        skip_in, k_ready, k_there, toep_in = t.sem("skip_in"), t.sem("k_ready"), t.sem("k_there"), t.sem("toep_in")
        cleared, x_ready, x_there, dve = t.sem("cleared"), t.sem("x_ready"), t.sem("x_there"), t.sem("dve")
        scanned, y_ready = t.sem("scanned"), t.sem("y_ready")
        block = t.block()

        @block.gpsimd
        def _(pool):
            pool.memset(toep[:], 0.0).then_inc(cleared, 1)

        @block.sync
        def _(sp):
            sp.dma_start(skip[:], ins["d_skip"]).then_inc(skip_in, 16)
            sp.wait_ge(cleared, 1)
            sp.wait_ge(k_there, 1)
            for l in range(S5_L):
                sp.dma_start(toep[l * S5_C:(l + 1) * S5_C, :, l * S5_C:LC],
                             kern[:, :, 0:LC - l * S5_C]).then_inc(toep_in, 16)

        @block.tensor
        def _(pe):
            for g in range(S5_G):
                lo, gp = 64 * (g % 2), g // 2
                out = bank[4 * (g % 2) + gp // 4][0:S5_C, (gp % 4) * LC:(gp % 4 + 1) * LC]
                pe.matmul(out, bb[lo:lo + 64, 0, gp, :], car[lo:lo + 64, gp, 0:S5_L, :], start=True, stop=False)
                mm = pe.matmul(out, bb[lo:lo + 64, 1, gp, :], cai[lo:lo + 64, gp, 0:S5_L, :], start=False, stop=True)
            mm.then_inc(k_ready, 1)
            pe.wait_ge(k_there, 1)
            for g in range(S5_G):
                lo, gp = 64 * (g % 2), g // 2
                for ri in range(2):
                    out = bank[2 * ri + gp // 8][lo:lo + 64, (gp % 8) * S5_NC:(gp % 8 + 1) * S5_NC]
                    mm = pe.matmul(out, vT[:, ri, gp, lo:lo + 64], U[:, g, :], start=True, stop=True)
            mm.then_inc(x_ready, 1)
            pe.wait_ge(toep_in, 16 * S5_L)
            pe.wait_ge(scanned, S5_NC)
            for g in range(S5_G):
                lo, gp = 64 * (g % 2), g // 2
                out = bank[4 * (g % 2) + gp // 4][0:S5_NC, (gp % 4) * LC:(gp % 4 + 1) * LC]
                pe.matmul(out, U[:, g, :], toep[:, g, :], start=True, stop=False)
                pe.matmul(out, st[lo:lo + 64, 0, gp, 0:S5_NC], car[lo:lo + 64, gp, 1:S5_L + 1, :], start=False,
                          stop=False)
                mm = pe.matmul(out, st[lo:lo + 64, 1, gp, 0:S5_NC], cai[lo:lo + 64, gp, 1:S5_L + 1, :], start=False,
                               stop=True)
                if g % 8 >= 6:
                    mm.then_inc(y_ready, 1)

        @block.vector
        def _(v):
            ch = Chain(v, dve)
            v.wait_ge(k_ready, 1)
            for b in range(8):
                ch.put(v.tensor_copy(kern[:, 8 * (b % 4) + b // 4:8 * (b % 4) + 8:2, :],
                                     bank[b][0:S5_C, :].rearrange("p (g n) -> p g n", g=4)))
            v.wait_ge(dve, ch.n)
            v.wait_ge(skip_in, 16)
            c.there(v)
            ch.link(v.tensor_tensor(dd[:], bc(c["ident"][0:S5_C, 0:S5_C], 1, S5_G), bc(skip[:], 2, S5_C), ALU.mult))
            v.tensor_tensor(kern[:, :, 0:S5_C], kern[:, :, 0:S5_C], dd[:], ALU.add).then_inc(k_there, 1)
            ch.put(v.memset(st[:], 0.0))
            v.wait_ge(x_ready, 1)
            for ri in range(2):
                for b in range(2):
                    ch.put(v.tensor_copy(xs[:, ri, 8 * b:8 * b + 8, :],
                                         bank[2 * ri + b][:].rearrange("p (g n) -> p g n", g=8)))
            v.wait_ge(dve, ch.n)
            first = bc(pw8[:, 0, :], 1, 2)
            with v.Fori(0, S5_NC) as m:
                ch.enter(m, 3)
                now, nxt = ds(m, 1), ds(m + 1, 1)
                ch.put(v.tensor_tensor(u1[:], first, st[:, 0:2, :, now].rearrange("p a g o -> p a (g o)"), ALU.mult))
                ch.link(v.tensor_tensor(u2[:], pw8[:, 1:3, :], st[:, 1:3, :, now].rearrange("p a g o -> p a (g o)"),
                                        ALU.mult))
                ch.link(v.tensor_tensor(u1[:], u1[:], u2[:], ALU.add))
                v.tensor_tensor(st[:, 0:2, :, nxt].rearrange("p a g o -> p a (g o)"), u1[:],
                                xs[:, :, :, now].rearrange("p a g o -> p a (g o)"), ALU.add)
                v.tensor_tensor(st[:, 2:3, :, nxt].rearrange("p a g o -> p a (g o)"), u1[:, 0:1, :],
                                xs[:, 0:1, :, now].rearrange("p a g o -> p a (g o)"), ALU.add).then_inc(scanned, 1)
                v.wait_ge(scanned, m + 1)
            ch.leave(S5_NC)

        @block.scalar
        def _(act):
            y_view = y_sb[:].rearrange("p l (g c) -> p g l c", c=S5_C)
            for n in range(8):
                quad, par = n // 2, n % 2
                act.wait_ge(y_ready, n + 1)
                act.activation(y_view[:, 8 * quad + par:8 * quad + 8:2],
                               bank[4 * par + quad][0:S5_NC, :].rearrange("p (g l c) -> p g l c", g=4, l=S5_L),
                               ACT.Gelu_apprx_tanh)


def glu(nc, c, tag, yT, w, b, oT):
    K = WIDTH_B // P
    with Tiles(nc, tag) as t:
        wb, bias, sg = t.sb("w", [P, K, WIDTH_B]), t.sb("bias", [P, K]), t.sb("sg", [P, K, SEQ])
        gated, high = t.sem("gated"), t.sem("high")
        bank = t.banks("z", K)
        loaded, z_ready, sg_ready = t.sem("loaded"), t.sem("z_ready"), t.sem("sg_ready")
        block = t.block()

        @block.sync
        def _(sp):
            sp.dma_start(wb[:], w.rearrange("(k p) n -> p k n", p=P)).then_inc(loaded, 16)
            sp.dma_start(bias[:], b).then_inc(loaded, 16)

        @block.tensor
        def _(pe):
            pe.wait_ge(loaded, 32)
            for f in range(K):
                for k in range(K):
                    mm = pe.matmul(bank[f][:], wb[:, k, f * P:(f + 1) * P], yT[:, k, :], start=k == 0, stop=k == K - 1)
                mm.then_inc(z_ready, 1)

        @block.scalar
        def _(act):
            act.wait_ge(loaded, 32)
            for f in range(K):
                act.wait_ge(z_ready, f + 1)
                act.activation(sg[:, f, :], bank[f][:], ACT.Sigmoid, bias=bias[:, f:f + 1]).then_inc(sg_ready, 1)
            for f in range(K):
                act.wait_ge(gated, f + 1)
                act.copy(oT[0][:, f, :], sg[:, f, :]).then_inc(high, 1)

        @block.vector
        def _(v):
            for f in range(K):
                v.wait_ge(sg_ready, f + 1)
                v.tensor_tensor(sg[:, f, :], yT[:, f, :], sg[:, f, :], ALU.mult).then_inc(gated, 1)
            for f in range(K):
                v.wait_ge(high, f + 1)
                v.tensor_tensor(oT[1][:, f, :], sg[:, f, :], oT[0][:, f, :].bitcast(F32), ALU.subtract)


def halves(t, name, shape):
    return [t.sb(f"{name}{half}", shape, F32R) for half in "hl"]


def layer0_mixer(nc, c, x, a):
    with Tiles(nc, "l0in") as inner:
        qkv = inner.sb("qkv", [P, NT, L0_WIDTH])
        U = inner.sb("U", [P, S5_G, S5_NC])
        with Tiles(nc, "l0h") as t:
            hT = halves(t, "hT", [P, KD, SEQ])
            normed_transpose(nc, c, "n0", x, a["l0_mix_norm"], hT)
            project(nc, c, "p0", hT, a["l0_w_in"][:, 0:L0_WIDTH], L0_WIDTH, L0_WIDTH // 4, qkv)
            s5_inputs(nc, c, "u0", hT, a["l0_w_in"], U)
        oT = halves(inner, "oT", [P, KD, SEQ])

        def cols(name, heads=None):
            o, n = L0_COLS[name]
            v = qkv[:, :, o:o + n]
            return v.rearrange("p t (h d) -> p t h d", h=heads) if heads else v

        with Tiles(nc, "l0s") as t:
            vT = t.sb("vT", [P, 2, S5_GP, P])
            car, cai = [t.sb(n, [P, S5_GP, S5_L + 1, S5_C]) for n in ("car", "cai")]
            pw8, bb = t.sb("pw8", [P, 3, S5_GP]), t.sb("bb", [P, 2, S5_GP, S5_C])
            y_sb = t.sb("y", [S5_NC, S5_L, WIDTH_B])
            with Tiles(nc, "l0v") as tv:
                vr, vi = [tv.sb(n, [P, S5_GP, S5_L, S5_C]) for n in ("vr", "vi")]
                s5_tables(nc, c, "st", a, vr, vi, car, cai, pw8, bb)
                turn(nc, c, "tu", [(vT[:, ri, 4 * b:4 * b + 4, :].rearrange("p g n -> p (g n)"),
                                    [s[:, gp, :, :].rearrange("p l c -> p (l c)") for gp in range(4 * b, 4 * b + 4)], P)
                                   for ri, s in enumerate((vr, vi)) for b in range(4)])
            s5_scan(nc, c, "sc", a, U, vT, car, cai, pw8, bb, y_sb)
            yT = t.sb("yT", [P, 4, SEQ])
            turn(nc, c, "ty", [(yT[:, f, :].rearrange("p (n l) -> p l n", l=S5_L),
                                [y_sb[:, l, f * P:(f + 1) * P] for l in range(S5_L)], P) for f in range(4)])
            glu(nc, c, "gl", yT, a["l0_s5_w_glu"], a["b_glu"], [o[:, 4:8, :] for o in oT])

        prepare_heads(nc, c, "ph", [(cols("q", 8), a["l0_a_q_gain"]), (cols("k", 2), a["l0_a_k_gain"]),
                                    (cols("iq", 8), None), (cols("ik", 1), None)], c["cos"][:], c["sin"][:])
        with Tiles(nc, "l0a") as t:
            kT, ikT = t.sb("kT", [P, 2, SEQ]), t.sb("ikT", [P, SEQ])
            score, bias, iw = t.sb("score", [P, NT, SEQ]), t.sb("bias", [P, NT, SEQ]), t.sb("iw", [P, NT, 8])
            o_a = t.sb("o", [P, NT, SEQ])
            k, ik = cols("k"), cols("ik")
            turn(nc, c, "tk", [(kT[0:HD, g, :], [k[:, m, g * HD:(g + 1) * HD] for m in range(NT)], HD)
                               for g in range(2)] + [(ikT[0:HD, :], [ik[:, m, :] for m in range(NT)], HD)],
                 zero=[kT[HD:P], ikT[HD:P]])
            scale_small(nc, c, "iw", iw, cols("iw"), 8 ** -0.5)
            index_scores(nc, c, "ix", cols("iq"), iw, ikT, score)
            select_keys(nc, c, "se", score, bias)
            attention(nc, c, "at", cols("q"), kT, cols("v"), bias, o_a)
            turn(nc, c, "to", [(tuple(o[:, f, :] for o in oT), [o_a[:, m, f * P:(f + 1) * P] for m in range(NT)], P)
                               for f in range(4)])
        project(nc, c, "po", oT, a["l0_w_out"], D, D // 4, x, add=True)


def scale_small(nc, c, tag, out, src, by):
    with Tiles(nc, tag) as t:
        block = t.block()

        @block.vector
        def _(v):
            v.tensor_scalar(out[:], src, by, None, ALU.mult)


def compress(nc, c, tag, cols, a, kcT, vc):
    NB, L = 32, CMP_LEN
    with Tiles(nc, tag) as t:
        posT = t.sb("posT", [HD, L])
        flat = [t.sb(f"flat{n}", [HD, 2, SEQ]) for n in range(2)]
        blk = [t.sb(f"blk{n}", [HD, L, 2, NB]) for n in range(2)]
        w1 = t.sb("w1", [HD, L, CMP_HID])
        w2 = [t.sb(f"w2{n}", [P, CMP_HID // P, HD]) for n in range(2)]
        hid = t.sb("hid", [P, 2, 2, 2 * NB])
        kc = t.sb("kc", [2 * NB, 1, 1, HD])
        srcs = [cols(n) for n in ("kc", "vc")]
        turn(nc, c, tag + "t", [(flat[n][:, g, :], [srcs[n][:, m, g * HD:(g + 1) * HD] for m in range(NT)], HD)
                                for n in range(2) for g in range(2)])
        with Tiles(nc, tag + "h") as t2:
            bank = t2.banks("h", 4)
            bank_v, bank_k = t2.banks("v", 2), t2.banks("k")[0]
            small_in, w1_in, cleared, blocks = t2.sem("small_in"), t2.sem("w1_in"), t2.sem("cleared"), t2.sem("blocks")
            h_ready, h_there, o_ready = t2.sem("h_ready"), t2.sem("h_there"), t2.sem("o_ready")
            block = t2.block()

            @block.sync
            def _(sp):
                sp.dma_start(posT[:], a["l1_nsa_cmp_pos"]).then_inc(small_in, 16)
                for n, name in enumerate(("l1_nsa_k_w2", "l1_nsa_v_w2")):
                    sp.dma_start(w2[n][:], a[name].rearrange("(m p) d -> p m d", p=P)).then_inc(small_in, 16)
                for n, name in enumerate(("l1_nsa_k_w1", "l1_nsa_v_w1")):
                    if n:
                        sp.wait_ge(h_ready, 1)
                    sp.dma_start(w1[:], a[name].rearrange("(l d) h -> d l h", d=HD)).then_inc(w1_in, 16)

            @block.gpsimd
            def _(pool):
                for n in range(2):
                    pool.memset(blk[n][:], 0.0).then_inc(cleared, 1)

            @block.vector
            def _(v):
                v.wait_ge(cleared, 2)
                v.wait_ge(small_in, 48)
                for n in range(2):
                    for g in range(2):
                        for half in range(L // CMP_STRIDE):
                            lo = half * CMP_STRIDE
                            win = flat[n][:, g, lo:lo + NCMP * CMP_STRIDE].rearrange("p (n l) -> p l n", l=CMP_STRIDE)
                            v.tensor_tensor(blk[n][:, lo:lo + CMP_STRIDE, g, 0:NCMP], win,
                                            bc(posT[:, lo:lo + CMP_STRIDE], 2, NCMP), ALU.add).then_inc(blocks, 1)
                v.wait_ge(o_ready, 3)
                v.tensor_copy(kc[:, 0, 0, :], bank_k[0:2 * NB, 0:HD])
                for g in range(2):
                    v.tensor_copy(vc[:, g, :], bank_v[g][0:NB, 0:HD])

            @block.tensor
            def _(pe):
                for n in range(2):
                    pe.wait_ge(blocks, 4 * (n + 1))
                    pe.wait_ge(w1_in, 16 * (n + 1))
                    for m in range(2):
                        for l in range(L):
                            mm = pe.matmul(bank[2 * n + m][:, 0:2 * NB], w1[:, l, m * P:(m + 1) * P],
                                           blk[n][:, l, :, :].rearrange("p g n -> p (g n)"), start=l == 0,
                                           stop=l == L - 1)
                    mm.then_inc(h_ready, 1)
                pe.wait_ge(h_there, 4)
                for m in range(2):
                    mm = pe.matmul(bank_k[0:2 * NB, 0:HD], hid[:, 0, m, :], w2[0][:, m, :], start=m == 0, stop=m == 1)
                mm.then_inc(o_ready, 1)
                for g in range(2):
                    for m in range(2):
                        mm = pe.matmul(bank_v[g][0:NB, 0:HD], hid[:, 1, m, g * NB:(g + 1) * NB], w2[1][:, m, :],
                                       start=m == 0, stop=m == 1)
                    mm.then_inc(o_ready, 1)

            @block.scalar
            def _(act):
                for n in range(2):
                    act.wait_ge(h_ready, n + 1)
                    for m in range(2):
                        act.activation(hid[:, n, m, :], bank[2 * n + m][:, 0:2 * NB],
                                       ACT.Gelu_apprx_tanh).then_inc(h_there, 1)

        prepare_heads(nc, c, tag + "p", [(kc[:], a["l1_c_k_gain"])], c["ccos"][:], c["csin"][:])
        turn(nc, c, tag + "u", [(kcT[0:HD].rearrange("p g n -> p (g n)"), [kc[:, 0, 0, :]], HD)], zero=[kcT[HD:P]])


def compressed_attention(nc, c, tag, q, kcT, vc, out, gate):
    NB = 32
    with Tiles(nc, tag) as t:
        staged = t.sb("staged", [P, NT, P])
        qT, pT = t.sb("qT", [P, SEQ]), t.sb("pT", [NB, SEQ])
        sm, vals = t.sb("sm", [P, NT, NB]), t.sb("vals", [NB, 2, HD])
        mx, den = t.sb("mx", [P, NT, 1]), t.sb("den", [P, NT, 1])
        bank_q, bank_s, bank_t, bank_o = [t.banks(n)[0] for n in ("q", "s", "t", "o")]
        q_staged, q_there, m_ready, e_there, p_ready, pT_there = [
            t.sem(n) for n in ("q_staged", "q_there", "m_ready", "e_there", "p_ready", "pT_there")]
        q_turned, s_ready, s_taken, t_ready, o_ready, o_taken = [
            t.lead(n) for n in ("q_turned", "s_ready", "s_taken", "t_ready", "o_ready", "o_taken")]
        cleared, dve = t.sem("cleared"), t.sem("dve")
        block = t.block()

        @block.gpsimd
        def _(pool):
            pool.memset(staged[:], 0.0).then_inc(cleared, 1)
            pool.wait_ge(cleared, 1)
            with pool.Fori(0, NH) as h:
                pool.wait_ge(q_turned, LEAD + h)
                pool.tensor_copy(staged[:, :, 0:HD], q[:, :, ds(h * HD, HD)]).then_inc(q_staged, 1)

        @block.tensor
        def _(pe):
            c.there(pe)
            with pe.Fori(0, 2) as g:
                with pe.Fori(0, NH // 2) as r:
                    h = g * (NH // 2) + r
                    pe.wait_ge(q_staged, h + 1)
                    for m in range(NT):
                        mm = pe.transpose(bank_q[:, m * P:(m + 1) * P], staged[:, m, :], c["ident"][:])
                    mm.then_inc(q_turned, 1)
                    pe.wait_ge(q_there, h + 1)
                    pe.wait_ge(s_taken, LEAD + h)
                    for m in range(NT):
                        mm = pe.matmul(bank_s[:, m * NB:(m + 1) * NB], qT[:, m * P:(m + 1) * P],
                                       kcT[:, ds(g, 1), :].rearrange("p a n -> p (a n)"), start=True, stop=True)
                    mm.then_inc(s_ready, 1)
                    pe.wait_ge(p_ready, h + 1)
                    for m in range(NT):
                        mm = pe.transpose(bank_t[0:NB, m * P:(m + 1) * P], sm[:, m, :], c["ident"][:])
                    mm.then_inc(t_ready, 1)
                    pe.wait_ge(pT_there, h + 1)
                    pe.wait_ge(o_taken, LEAD + h)
                    for m in range(NT):
                        mm = pe.matmul(bank_o[:, m * HD:(m + 1) * HD], pT[:, m * P:(m + 1) * P],
                                       vc[:, ds(g, 1), :].rearrange("p a n -> p (a n)"), start=True, stop=True)
                    mm.then_inc(o_ready, 1)

        @block.scalar
        def _(act):
            with act.Fori(0, NH) as h:
                act.wait_ge(q_turned, LEAD + h + 1)
                act.wait_ge(s_ready, LEAD + h)
                act.copy(qT[:], bank_q[:]).then_inc(q_there, 1)
                act.wait_ge(m_ready, h + 1)
                act.activation(sm[:], sm[:], ACT.Exp).then_inc(e_there, 1)
                act.wait_ge(t_ready, LEAD + h + 1)
                act.wait_ge(o_ready, LEAD + h)
                act.copy(pT[:], bank_t[0:NB, :]).then_inc(pT_there, 1)

        @block.vector
        def _(v):
            ch = Chain(v, dve)
            c.there(v)
            with v.Fori(0, NH) as h:
                ch.enter(h, 5)
                v.wait_ge(s_ready, LEAD + h + 1)
                v.wait_ge(t_ready, LEAD + h)
                v.scalar_tensor_tensor(out=sm[:], in0=bank_s[:, 0:NT * NB].rearrange("p (m n) -> p m n", m=NT),
                                       scalar=HD ** -0.5, in1=c["cbias"][:], op0=ALU.mult,
                                       op1=ALU.add).then_inc(s_taken, 1)
                v.wait_ge(s_taken, LEAD + h + 1)
                ch.link(v.tensor_reduce(mx[:].rearrange("p m o -> p (m o)"), sm[:], AX.X, ALU.max))
                v.tensor_tensor(sm[:], sm[:], mx[:].broadcast_to([P, NT, NB]), ALU.subtract).then_inc(m_ready, 1)
                v.wait_ge(e_there, h + 1)
                v.tensor_tensor(sm[:], sm[:], c["cmask"][:], ALU.mult).then_inc(p_ready, 1)
                v.wait_ge(p_ready, h + 1)
                ch.link(v.tensor_reduce(den[:].rearrange("p m o -> p (m o)"), sm[:], AX.X, ALU.add))
                ch.link(v.tensor_scalar(den[:], den[:], 1e-30, None, ALU.max))
                ch.link(v.reciprocal(den[:], den[:]))
                ch.link(v.tensor_tensor(den[:], den[:], gate[:, :, ds(h, 1)], ALU.mult))
                v.wait_ge(o_ready, LEAD + h + 1)
                v.tensor_tensor(out[:, :, ds(h * HD, HD)], bank_o[:, 0:NT * HD].rearrange("p (m d) -> p m d", m=NT),
                                den[:].broadcast_to([P, NT, HD]), ALU.mult).then_inc(o_taken, 1)
            ch.leave(NH)


def gla_decays(nc, c, tag, cols, a, qd, ki, kd, dec, la):
    W = GLA_H * GLA_K
    with Tiles(nc, tag) as t:
        lowT, wg, bg = t.sb("lowT", [16, SEQ]), t.sb("wg", [16, W]), t.sb("bg", [P, W])
        lg, e1 = t.sb("lg", [P, NT, W]), t.sb("e1", [P, NT, W])
        bank = t.banks("b", 8)
        loaded, turned, low_there, l_ready, lg_ready = [
            t.sem(n) for n in ("loaded", "turned", "low_there", "l_ready", "lg_ready")]
        e_there, la_ready, s_ready, x_there, dve = [
            t.sem(n) for n in ("e_there", "la_ready", "s_ready", "x_there", "dve")]
        block = t.block()
        low, gq, gk = cols("glow"), cols("gq"), cols("gk")

        @block.sync
        def _(sp):
            sp.dma_start(wg[:], a["l1_gla_w_gate"]).then_inc(loaded, 16)
            sp.dma_start(bg[:], a["l1_gla_b_gate"].partition_broadcast(P)).then_inc(loaded, 16)

        @block.tensor
        def _(pe):
            c.there(pe)
            for m in range(NT):
                mm = pe.transpose(bank[0][0:16, m * P:(m + 1) * P], low[:, m, :], c["ident"][:])
            mm.then_inc(turned, 1)
            pe.wait_ge(loaded, 32)
            pe.wait_ge(low_there, 1)
            for m in range(NT):
                pe.matmul(bank[1 + m][:, 0:W], lowT[:, m * P:(m + 1) * P], wg[:], start=True,
                          stop=True).then_inc(l_ready, 1)
            pe.wait_ge(la_ready, NT)
            for h in range(GLA_H):
                for m in range(NT):
                    mm = pe.matmul(bank[0][0:GLA_K, (h * NT + m) * 4:(h * NT + m + 1) * 4],
                                   la[:, m, h * GLA_K:(h + 1) * GLA_K], c["chunk"][:], start=True, stop=True)
            mm.then_inc(s_ready, 1)
            for m in range(NT):
                pe.matmul(bank[1 + m][:, 0:W], c["upto"][:], la[:, m, :], start=True, stop=True)
                pe.matmul(bank[1 + m][:, W:2 * W], c["after"][:], la[:, m, :], start=True,
                          stop=True).then_inc(s_ready, 1)

        @block.scalar
        def _(act):
            act.wait_ge(turned, 1)
            act.copy(lowT[:], bank[0][0:16, :]).then_inc(low_there, 1)
            act.wait_ge(lg_ready, NT)
            act.activation(e1[:], lg[:], ACT.Abs).then_inc(e_there, 1)
            act.wait_ge(e_there, 1)
            act.activation(e1[:], e1[:], ACT.Exp, scale=-1.0).then_inc(e_there, 1)
            act.wait_ge(e_there, 2)
            act.activation(e1[:], e1[:], ACT.Ln, bias=1.0).then_inc(e_there, 1)
            act.wait_ge(s_ready, 1)
            act.activation(dec[:].rearrange("p h n -> p (h n)"), bank[0][0:GLA_K, 0:GLA_H * GLA_N], ACT.Exp)
            for m in range(NT):
                act.wait_ge(s_ready, m + 2)
                act.activation(qd[:, m, :], bank[1 + m][:, 0:W], ACT.Exp).then_inc(x_there, 1)
                act.activation(ki[:, m, :], bank[1 + m][:, 0:W], ACT.Exp, scale=-1.0).then_inc(x_there, 1)
                act.activation(kd[:, m, :], bank[1 + m][:, W:2 * W], ACT.Exp).then_inc(x_there, 1)

        @block.vector
        def _(v):
            ch = Chain(v, dve)
            v.wait_ge(loaded, 32)
            for m in range(NT):
                v.wait_ge(l_ready, m + 1)
                v.tensor_tensor(lg[:, m, :], bank[1 + m][:, 0:W], bg[:], ALU.add).then_inc(lg_ready, 1)
            v.wait_ge(e_there, 3)
            ch.link(v.scalar_tensor_tensor(out=lg[:], in0=lg[:], scalar=0.0, in1=e1[:], op0=ALU.min, op1=ALU.subtract))
            for m in range(NT):
                v.tensor_scalar(la[:, m, :], lg[:, m, :], 1.0 / 16.0, None, ALU.mult).then_inc(la_ready, 1)
            for m in range(NT):
                v.wait_ge(x_there, 3 * m + 3)
                v.scalar_tensor_tensor(out=qd[:, m, :], in0=gq[:, m, :], scalar=GLA_K ** -0.5, in1=qd[:, m, :],
                                       op0=ALU.mult, op1=ALU.mult)
                v.tensor_tensor(ki[:, m, :], gk[:, m, :], ki[:, m, :], ALU.mult)
                v.tensor_tensor(kd[:, m, :], gk[:, m, :], kd[:, m, :], ALU.mult)


def gla_mix(nc, c, tag, gv, qdT, kiT, kd, dec, o):
    C4 = P // GLA_C
    with Tiles(nc, tag) as t:
        att = t.sb("att", [P, NT, GLA_H, P])
        state = t.sb("state", [GLA_K, GLA_N + 1, GLA_H, GLA_V])
        bank_a, bank_u, bank_o = t.banks("a", 2), t.banks("u", 4), t.banks("o", 2)
        cleared, a_ready, a_there, u_ready, u_there, o_ready, o_taken, dve = [
            t.sem(n) for n in ("cleared", "a_ready", "a_there", "u_ready", "u_there", "o_ready", "o_taken", "dve")]
        block = t.block()

        @block.gpsimd
        def _(pool):
            pool.memset(att[:], 0.0).then_inc(cleared, 1)
            pool.memset(state[:, 0], 0.0).then_inc(cleared, 1)

        @block.tensor
        def _(pe):
            for m in range(NT):
                if m >= 2:
                    pe.wait_ge(a_there, m - 1)
                for h in range(GLA_H):
                    mm = pe.matmul(bank_a[m % 2][:, h * P:(h + 1) * P], kiT[:, h, m * P:(m + 1) * P],
                                   qdT[:, h, m * P:(m + 1) * P], start=True, stop=True)
                mm.then_inc(a_ready, 1)
                for n in range(C4):
                    lo = n * GLA_C
                    if m:
                        pe.wait_ge(u_there, (m - 1) * C4 + n + 1)
                    for h in range(GLA_H):
                        mm = pe.matmul(bank_u[n][0:GLA_K, h * GLA_V:(h + 1) * GLA_V],
                                       kd[lo:lo + GLA_C, m, h * GLA_K:(h + 1) * GLA_K],
                                       gv[lo:lo + GLA_C, m, h * GLA_V:(h + 1) * GLA_V], start=True, stop=True)
                    mm.then_inc(u_ready, 1)
            for m in range(NT):
                pe.wait_ge(a_there, m + 1)
                pe.wait_ge(u_there, (m + 1) * C4)
                if m >= 2:
                    pe.wait_ge(o_taken, m - 1)
                for h in range(GLA_H):
                    out = bank_o[m % 2][:, h * GLA_V:(h + 1) * GLA_V]
                    pe.matmul(out, att[:, m, h, :], gv[:, m, h * GLA_V:(h + 1) * GLA_V], start=True, stop=False,
                              skip_group_check=True)
                    for n in range(C4):
                        lo = n * GLA_C
                        mm = pe.matmul(out[lo:lo + GLA_C], qdT[:, h, m * P + lo:m * P + lo + GLA_C],
                                       state[:, m * C4 + n, h, :], start=False, stop=True, skip_group_check=True)
                mm.then_inc(o_ready, 1)

        @block.vector
        def _(v):
            ch = Chain(v, dve)
            c.there(v)
            v.wait_ge(cleared, 2)
            for m in range(NT):
                v.wait_ge(a_ready, m + 1)
                for h in range(GLA_H):
                    ins = v.copy_predicated(att[:, m, h, :], c["upto"][:].bitcast(U32), bank_a[m % 2][:, h * P:(h + 1) * P])
                ins.then_inc(a_there, 1)
                for n in range(C4):
                    at = m * C4 + n
                    v.wait_ge(u_ready, at + 1)
                    for h in range(GLA_H):
                        ins = v.scalar_tensor_tensor(out=state[:, at + 1, h, :], in0=state[:, at, h, :],
                                                     scalar=dec[:, h, at:at + 1],
                                                     in1=bank_u[n][0:GLA_K, h * GLA_V:(h + 1) * GLA_V],
                                                     op0=ALU.mult, op1=ALU.add)
                    ins.then_inc(u_there, 1)
                    v.wait_ge(u_there, at + 1)

        @block.scalar
        def _(act):
            for m in range(NT):
                act.wait_ge(o_ready, m + 1)
                act.copy(o[:, m, :], bank_o[m % 2][:]).then_inc(o_taken, 1)


def gla_gate(nc, c, tag, o, gr, gain):
    with Tiles(nc, tag) as t:
        sq, sg, gb = t.sb("sq", [P, NT, GLA_H, GLA_V]), t.sb("sg", [P, NT, SEQ]), t.sb("gain", [P, GLA_V])
        ms, root, r = [t.sb(n, [P, NT, GLA_H]) for n in ("ms", "root", "r")]
        gain_in, ms_ready, root_ready, sg_ready, dve = [
            t.sem(n) for n in ("gain_in", "ms_ready", "root_ready", "sg_ready", "dve")]
        block = t.block()
        o4 = o[:].rearrange("p m (h e) -> p m h e", h=GLA_H)
        full = [P, NT, GLA_H, GLA_V]

        @block.sync
        def _(sp):
            sp.dma_start(gb[:], gain.partition_broadcast(P)).then_inc(gain_in, 16)

        @block.scalar
        def _(act):
            act.activation(sg[:], gr, ACT.Sigmoid).then_inc(sg_ready, 1)
            act.wait_ge(ms_ready, 1)
            act.activation(root[:], ms[:], ACT.Sqrt).then_inc(root_ready, 1)

        @block.vector
        def _(v):
            ch = Chain(v, dve)
            ch.link(v.tensor_tensor(sq[:], o4, o4, ALU.mult))
            ch.link(v.tensor_reduce(ms[:], sq[:], AX.X, ALU.add))
            v.tensor_scalar(ms[:], ms[:], 1.0 / GLA_V, EPS, ALU.mult, ALU.add).then_inc(ms_ready, 1)
            rstd_steps(v, ch, ms[:], root[:], r[:], root_ready, 1)
            ch.link(v.tensor_tensor(o4, o4, r[:].unsqueeze(3).broadcast_to(full), ALU.mult))
            v.wait_ge(gain_in, 16)
            ch.link(v.tensor_tensor(o4, o4, gb[:].unsqueeze(1).unsqueeze(1).broadcast_to(full), ALU.mult))
            v.wait_ge(sg_ready, 1)
            ch.link(v.tensor_tensor(sg[:], sg[:], gr, ALU.mult))
            ch.link(v.tensor_tensor(o[:], o[:], sg[:], ALU.mult))


def sigmoid_gates(nc, c, tag, gates, src):
    with Tiles(nc, tag) as t:
        block = t.block()

        @block.scalar
        def _(act):
            act.activation(gates[:], src.rearrange("p m (h b) -> p m b h", b=3), ACT.Sigmoid)


def layer1_mixer(nc, c, x, a):
    with Tiles(nc, "l1in") as inner:
        qkv = inner.sb("qkv", [P, NT, L1_WIDTH])
        with Tiles(nc, "l1h") as t:
            hT = halves(t, "hT", [P, KD, SEQ])
            normed_transpose(nc, c, "n1", x, a["l1_mix_norm"], hT)
            project(nc, c, "p1", hT, a["l1_w_in"], L1_WIDTH, L1_WIDTH // 6, qkv)
        oT = halves(inner, "oT", [P, KD, SEQ])

        def cols(name, heads=None):
            o, n = L1_COLS[name]
            v = qkv[:, :, o:o + n]
            return v.rearrange("p t (h d) -> p t h d", h=heads) if heads else v

        with Tiles(nc, "l1g") as t:
            kd, dec = t.sb("kd", [P, NT, 256]), t.sb("dec", [GLA_K, GLA_H, GLA_N])
            qdT, kiT = [t.sb(n, [GLA_K, GLA_H, SEQ]) for n in ("qdT", "kiT")]
            o_d = t.sb("o", [P, NT, SEQ])
            with Tiles(nc, "l1gd") as t2:
                qd, ki, la = [t2.sb(n, [P, NT, 256]) for n in ("qd", "ki", "la")]
                gla_decays(nc, c, "gd", cols, a, qd, ki, kd, dec, la)
                turn(nc, c, "gt", [(d[:, h, :], [s[:, m, h * GLA_K:(h + 1) * GLA_K] for m in range(NT)], GLA_K)
                                   for d, s in ((qdT, qd), (kiT, ki)) for h in range(GLA_H)])
            gla_mix(nc, c, "gm", cols("gv"), qdT, kiT, kd, dec, o_d)
            gla_gate(nc, c, "gg", o_d, cols("gr"), a["l1_gla_o_gain"])
            turn(nc, c, "go", [(tuple(o[:, 4 + f, :] for o in oT), [o_d[:, m, f * P:(f + 1) * P] for m in range(NT)], P)
                               for f in range(4)])

        with Tiles(nc, "l1a") as t:
            kcT, vc = t.sb("kcT", [P, 2, 32]), t.sb("vc", [32, 2, HD])
            gates = t.sb("gates", [P, NT, 3, NH])
            compress(nc, c, "cm", cols, a, kcT, vc)
            prepare_heads(nc, c, "pq", [(cols("q", 8), a["l1_c_q_gain"]), (cols("ks", 2), a["l1_c_k_gain"]),
                                        (cols("kw", 2), a["l1_c_k_gain"])], c["cos"][:], c["sin"][:])
            kT = [t.sb(f"kT{n}", [P, 2, SEQ]) for n in range(2)]
            bias, o_c = t.sb("bias", [P, NT, SEQ]), t.sb("o", [P, NT, SEQ])
            ks = [cols("ks"), cols("kw")]
            turn(nc, c, "tk1", [(kT[n][0:HD, g, :], [ks[n][:, m, g * HD:(g + 1) * HD] for m in range(NT)], HD)
                                for n in range(2) for g in range(2)], zero=[k[HD:P] for k in kT])
            sigmoid_gates(nc, c, "sg", gates, cols("gl"))
            causal_bias(nc, c, "cb", bias)
            compressed_attention(nc, c, "ca", cols("q"), kcT, vc, o_c, gates[:, :, 0, :])
            attention(nc, c, "as", cols("q"), kT[0], cols("vs"), bias, o_c, gate=gates[:, :, 1, :], add=True)
            attention(nc, c, "aw", cols("q"), kT[1], cols("vw"), bias, o_c, gate=gates[:, :, 2, :], add=True)
            turn(nc, c, "to1", [(tuple(o[:, f, :] for o in oT), [o_c[:, m, f * P:(f + 1) * P] for m in range(NT)], P)
                                for f in range(4)])
        project(nc, c, "po1", oT, a["l1_w_out"], D, D // 4, x, add=True)


def retrieve(nc, c, tag, xs, wq, subkeysT, gates, rows, cols):
    with Tiles(nc, tag) as t:
        raw = [t.sb(f"raw{s}", [P, KD, P]) for s in range(2)]
        wb = [halves(t, f"wq{s}", [P, KD, P]) for s in range(2)]
        keys = t.sb("keys", [P, NLIST, PEER_K])
        qT = [t.sb(f"qT{s}", [P, SEQ]) for s in range(2)]
        T = PEER_TOP
        val = [t.sb(f"val{s}", [P, NT, T]) for s in range(2)]
        idx = [t.sb(f"idx{s}", [P, NT, T], U32) for s in range(2)]
        idf = [t.sb(f"idf{s}", [P, NT, T]) for s in range(2)]
        work = t.sb("work", [P, NT, P])
        cand, rest = t.sb("cand", [P, NT, T * T]), t.sb("rest", [P, NT, T * T])
        top, pos = t.sb("top", [P, NT, T]), t.sb("pos", [P, NT, T], U32)
        place = [t.sb(f"place{s}", [P, NT, T], U32) for s in range(2)]
        placef = [t.sb(f"placef{s}", [P, NT, T]) for s in range(2)]
        onehot = t.sb("onehot", [P, NT, T, T])
        peak = t.sb("peak", [P, NT, PEER_H, 1])
        wait_taker = t.sb("wait_taker", [P, 1])
        bank_q, bank_s = t.banks("q", 2), t.banks("s", 2)
        keys_in, wq_in = t.sem("keys_in"), t.sems("wq_in", 2)
        high, low = t.sems("high", 2), t.leads("low", 2)
        q_ready, q_there = t.leads("q_ready", 2), t.leads("q_there", 2)
        s_ready, s_taken = t.leads("s_ready", 2), t.leads("s_taken", 2)
        dve, e_ready, e_there = t.sem("dve"), t.sem("e_ready"), t.sem("e_there")
        block = t.block()
        wq_view = wq.rearrange("(k p) n -> p k n", p=P)

        @block.sync
        def _(sp):
            sp.dma_start(keys[:], subkeysT).then_inc(keys_in, 16)
            with sp.Fori(0, PEER_H) as h:
                for s in range(2):
                    sp.wait_ge(low[s], LEAD + h)
                    sp.dma_start(raw[s][:], wq_view[:, :, ds((h * 2 + s) * P, P)]).then_inc(wq_in[s], 16)

        @block.tensor
        def _(pe):
            pe.wait_ge(keys_in, 16)
            with pe.Fori(0, PEER_H) as h:
                for s in range(2):
                    pe.wait_ge(low[s], LEAD + h + 1)
                    pe.wait_ge(q_there[s], LEAD + h)
                    for k in range(KD):
                        mm = passes(pe, bank_q[s][:], [w[:, k, :] for w in wb[s]], [m[:, k, :] for m in xs], k == 0,
                                    k == KD - 1)
                    mm.then_inc(q_ready[s], 1)
                for s in range(2):
                    pe.wait_ge(q_there[s], LEAD + h + 1)
                    pe.wait_ge(s_taken[s], LEAD + h)
                    for m in range(NT):
                        mm = pe.matmul(bank_s[s][:, m * P:(m + 1) * P], qT[s][:, m * P:(m + 1) * P],
                                       keys[:, ds(h * 2 + s, 1), :].rearrange("p a n -> p (a n)"),
                                       start=True, stop=True)
                    mm.then_inc(s_ready[s], 1)

        @block.gpsimd
        def _(pool):
            with pool.Fori(0, PEER_H) as h:
                for s in range(2):
                    pool.wait_ge(high[s], h + 1)
                    pool.tensor_tensor(wb[s][1][:], raw[s][:], wb[s][0][:].bitcast(F32),
                                       ALU.subtract).then_inc(low[s], 1)

        @block.scalar
        def _(act):
            with act.Fori(0, PEER_H) as h:
                for s in range(2):
                    act.wait_ge(wq_in[s], h * 16 + 16)
                    act.wait_ge(q_ready[s], LEAD + h)
                    act.copy(wb[s][0][:], raw[s][:]).then_inc(high[s], 1)
                for s in range(2):
                    act.wait_ge(q_ready[s], LEAD + h + 1)
                    act.wait_ge(s_ready[s], LEAD + h)
                    act.copy(qT[s][:], bank_q[s][:]).then_inc(q_there[s], 1)
            act.wait_ge(e_ready, 1)
            act.activation(gates[:], gates[:], ACT.Exp).then_inc(e_there, 1)

        @block.vector
        def _(v):
            ch = Chain(v, dve)
            c.there(v)

            def sync():
                v.wait_ge(dve, ch.n + ch.off)
                v.memset(wait_taker[:], 0.0)

            def best16(src, spare, values, indices, done=None):
                for m in range(NT):
                    ch.put(v.max(values[:, m, 0:8], src(m)))
                sync()
                for m in range(NT):
                    ch.put(v.max_index(indices[:, m, 0:8], values[:, m, 0:8], src(m)))
                for m in range(NT):
                    ins = v.match_replace(spare(m), values[:, m, 0:8], src(m), TAKEN)
                    if m < NT - 1 or done is None:
                        ch.put(ins)
                    else:
                        ins.then_inc(done[0], 1)
                        v.wait_ge(done[0], done[1])
                sync()
                for m in range(NT):
                    ch.put(v.max(values[:, m, 8:T], spare(m)))
                sync()
                for m in range(NT):
                    ch.put(v.max_index(indices[:, m, 8:T], values[:, m, 8:T], spare(m)))
                v.wait_ge(dve, ch.n + ch.off)

            with v.Fori(0, PEER_H) as h:
                ch.enter(h, 2 * (5 * NT - 1 + 1) + NT + 5 * NT + 2 + 4 * 2 + 1)
                for s in range(2):
                    v.wait_ge(s_ready[s], LEAD + h + 1)
                    v.memset(wait_taker[:], 0.0)
                    best16(lambda m: bank_s[s][:, m * P:(m + 1) * P], lambda m: work[:, m, :], val[s], idx[s],
                           (s_taken[s], LEAD + h + 1))
                    ch.put(v.tensor_copy(idf[s][:], idx[s][:]))
                for m in range(NT):
                    ch.put(v.tensor_tensor(cand[:, m, :].rearrange("p (a b) -> p a b", b=T),
                                           bc(val[0][:, m, :], 2, T), bc(val[1][:, m, :], 1, T), ALU.add))
                sync()
                best16(lambda m: cand[:, m, :], lambda m: rest[:, m, :], top, pos)
                ch.put(v.tensor_scalar(place[0][:], pos[:], 4, None, ALU.logical_shift_right))
                ch.link(v.tensor_scalar(place[1][:], pos[:], T - 1, None, ALU.bitwise_and))
                for s, e in ((0, rows), (1, cols)):
                    ch.link(v.tensor_copy(placef[s][:], place[s][:]))
                    ch.link(v.tensor_tensor(onehot[:], bc(placef[s][:], 3, T),
                                            c["iota"][:, 0:T].unsqueeze(1).unsqueeze(1).broadcast_to([P, NT, T, T]),
                                            ALU.is_equal))
                    ch.link(v.tensor_tensor(onehot[:], onehot[:], bc(idf[s][:], 2, T), ALU.mult))
                    ch.link(v.tensor_reduce(e[:, :, ds(h * T, T)], onehot[:], AX.X, ALU.add))
                ch.put(v.tensor_copy(gates[:, :, ds(h * T, T)], top[:]))
                v.wait_ge(dve, ch.n + ch.off)
            ch.leave(PEER_H)
            g4 = gates[:].rearrange("p m (h k) -> p m h k", k=T)
            full = [P, NT, PEER_H, T]
            ch.link(v.tensor_copy(peak[:], g4[:, :, :, 0:1]))
            v.tensor_tensor(g4, g4, peak[:].broadcast_to(full), ALU.subtract).then_inc(e_ready, 1)
            v.wait_ge(e_there, 1)
            ch.link(v.tensor_reduce(peak[:].rearrange("p m h o -> p m (h o)"), g4, AX.X, ALU.add))
            ch.link(v.reciprocal(peak[:], peak[:]))
            ch.link(v.tensor_tensor(g4, g4, peak[:].broadcast_to(full), ALU.mult))


def spread_gates(nc, c, tag, gT, rT, cT, gmat):
    QUAD, GROUPS = 4, 2
    trips = P // (QUAD * GROUPS)
    with Tiles(nc, tag) as t:
        wide = [t.sb(f"wide{s}", [P, PEER_K, P]) for s in range(2)]
        left = [t.sb(f"left{g}", [P, QUAD, P]) for g in range(GROUPS)]
        right = [t.sb(f"right{g}", [P, QUAD, P]) for g in range(GROUPS)]
        bank = t.banks("g", GROUPS)
        made, spread, taken, stored = (t.leads("made", GROUPS), t.leads("spread", GROUPS), t.leads("taken", GROUPS),
                                       t.leads("stored", 2))
        block = t.block()

        def walk(eng, body):
            with eng.Fori(0, NT // 2) as o:
                for s in range(2):
                    tile = o * 2 + s
                    with eng.Fori(0, trips) as j:
                        body(tile, j, tile * trips + j, o, s)

        @block.vector
        def _(v):
            c.there(v)

            def body(tile, j, n, o, s):
                for g in range(GROUPS):
                    v.wait_ge(spread[g], LEAD + n)
                    for q in range(QUAD):
                        tok = tile * P + j * (QUAD * GROUPS) + (g * QUAD + q)
                        v.tensor_scalar(left[g][:, q, :], c["iota"][:], rT[:, ds(tok, 1)], gT[:, ds(tok, 1)],
                                        ALU.is_equal, ALU.mult)
                        ins = v.tensor_scalar(right[g][:, q, :], c["iota"][:], cT[:, ds(tok, 1)], None, ALU.is_equal)
                    ins.then_inc(made[g], 1)
            walk(v, body)

        @block.tensor
        def _(pe):
            def body(tile, j, n, o, s):
                for g in range(GROUPS):
                    pe.wait_ge(made[g], LEAD + n + 1)
                    pe.wait_ge(taken[g], LEAD + n)
                    for q in range(QUAD):
                        mm = pe.matmul(bank[g][:, q * P:(q + 1) * P], left[g][:, q, :], right[g][:, q, :],
                                       start=True, stop=True)
                    mm.then_inc(spread[g], 1)
            walk(pe, body)

        @block.scalar
        def _(act):
            def body(tile, j, n, o, s):
                for g in range(GROUPS):
                    act.wait_ge(spread[g], LEAD + n + 1)
                    act.wait_ge(stored[s], LEAD + o * 16)
                    act.copy(wide[s][:, :, ds(j * (QUAD * GROUPS) + g * QUAD, QUAD)],
                             bank[g][:].rearrange("p (q b) -> p b q", q=QUAD)).then_inc(taken[g], 1)
            walk(act, body)

        @block.sync
        def _(sp):
            with sp.Fori(0, NT // 2) as o:
                for s in range(2):
                    tile = o * 2 + s
                    for g in range(GROUPS):
                        sp.wait_ge(taken[g], LEAD + (tile + 1) * trips)
                    sp.dma_start(gmat[:, :, ds(tile * P, P)].rearrange("b a t -> a b t"),
                                 wide[s][:]).then_inc(stored[s], 16)
            for s in range(2):
                sp.wait_ge(stored[s], LEAD + 16 * (NT // 2))


class Set:

    def __init__(self, n, quad, j):
        self.n, self.quad, self.j = n, quad, j

    def __add__(self, k):
        return Set(self.n + k, self.quad + (self.j % 4 + k) // 4, (self.j + k) % 8)

    def from_(self, k):
        return not isinstance(self.n, int) or self.n >= k


def all_experts(nc, c, tag, xs, uT, v_tab, gmat, x):
    SETS, PART, OUTS = PEER_K, 4, NT * 2
    BODY = 2 * PART
    trips = (SETS - BODY) // BODY
    last = PART + trips * BODY
    v_view = v_tab.rearrange("(a b) d -> b a d", b=PEER_K)
    with Tiles(nc, tag) as t:
        u_raw, v_raw = [[t.sb(f"{n}{j}", [P, D]) for j in range(PART)] for n in ("ur", "vr")]
        u_half = [[t.sb(f"u{j}{half}", [P, D], F32R) for half in "hl"] for j in range(2)]
        v_half = [[t.sb(f"v{j}{half}", [P, D], F32R) for half in "hl"] for j in range(PART)]
        g_raw = [t.sb(f"g{j}", [P, SEQ]) for j in range(PART)]
        hid = [t.sb(f"hid{j}", [P, SEQ]) for j in range(2)]
        prod = [t.sb(f"prod{j}", [P, SEQ]) for j in range(2)]
        p_half = [[t.sb(f"p{j}{half}", [P, SEQ], F32R) for half in "hl"] for j in range(BODY)]
        y = t.sb("y", [P, NT, D])
        bank_h, bank_y = t.banks("hb", PART), t.banks("yb", 4)
        u_in, v_in, g_in = t.sems("u_in", PART), t.sems("v_in", PART), t.sems("g_in", PART)
        uh_made, ul_made, vh_made, ph_made, pl_made = [
            t.sem(n) for n in ("uh_made", "ul_made", "vh_made", "ph_made", "pl_made")]
        h_ready, hid_made, prod_made, cleared = [t.sem(n) for n in ("h_ready", "hid_made", "prod_made", "cleared")]
        vl_made, y_ready, y_taken = t.lead("vl_made", PART), t.lead("y_ready", OUTS), t.lead("y_taken", OUTS)
        block = t.block()

        def walk(eng, hidden, output, behind=lambda s: None):
            for k in range(PART):
                hidden(Set(k, 0, k))
            with eng.Fori(0, trips) as i:
                for j in range(BODY):
                    s = Set(i * BODY + j, i * 2 + j // PART, j)
                    behind(s)
                    hidden(s + PART)
                    if j % PART == PART - 1:
                        output(s)
            for k in range(BODY):
                s = Set(last - PART + k, last // PART - 1 + k // PART, k)
                behind(s)
                if k < PART:
                    hidden(s + PART)
                if k % PART == PART - 1:
                    output(s)

        @block.gpsimd
        def _(pool):
            pool.memset(y[:], 0.0).then_inc(cleared, 1)

        @block.sync
        def _(sp):
            def load(buf, src, done, s):
                sp.dma_start(buf[s.j % PART][:], src[ds(s.n, 1)].rearrange("o a d -> a (o d)"))\
                  .then_inc(done[s.j % PART], 16)

            def ahead(s):
                if s.from_(PART):
                    sp.wait_ge(ul_made, s.n - PART + 1)
                load(u_raw, uT, u_in, s)
                if s.from_(PART):
                    sp.wait_ge(prod_made, s.n - PART + 1)
                load(g_raw, gmat, g_in, s)

            def values(s):
                sp.wait_ge(vl_made, s.n + 1)
                load(v_raw, v_view, v_in, s)

            for k in range(PART):
                ahead(Set(k, 0, k))
            walk(sp, lambda s: ahead(s) if s.from_(PART) else None, lambda s: None, values)

        @block.tensor
        def _(pe):
            def hidden(s):
                pe.wait_ge(ul_made, s.n + 1)
                if s.from_(PART):
                    pe.wait_ge(hid_made, s.n - PART + 1)
                for k in range(KD):
                    mm = passes(pe, bank_h[s.j % PART][:], [h[:, k * P:(k + 1) * P] for h in u_half[s.j % 2]],
                                [h[:, k, :] for h in xs], k == 0, k == KD - 1)
                mm.then_inc(h_ready, 1)

            def output(s):
                pe.wait_ge(pl_made, s.n + 1)
                pe.wait_ge(vl_made, PART + s.n + 1)
                for o in range(OUTS):
                    m, half = o // 2, o % 2
                    pe.wait_ge(y_taken, OUTS + s.quad * OUTS + o - 3)
                    for k in range(PART):
                        mm = passes(pe, bank_y[o % 4][:],
                                    [h[:, m * P:(m + 1) * P] for h in p_half[s.j // PART * PART + k]],
                                    [h[:, half * 512:(half + 1) * 512] for h in v_half[k]], k == 0, k == PART - 1)
                    mm.then_inc(y_ready, 1)

            walk(pe, hidden, output)

        @block.scalar
        def _(act):
            def split_u(s):
                act.wait_ge(u_in[s.j % PART], s.quad * 16 + 16)
                if s.from_(2):
                    act.wait_ge(h_ready, s.n - 1)
                act.copy(u_half[s.j % 2][0][:], u_raw[s.j % PART][:]).then_inc(uh_made, 1)

            def hidden(s):
                if not (isinstance(s.n, int) and s.n >= SETS - 2):
                    split_u(s + 2)
                act.wait_ge(h_ready, s.n + 1)
                if s.from_(2):
                    act.wait_ge(prod_made, s.n - 1)
                act.activation(hid[s.j % 2][:], bank_h[s.j % PART][:], ACT.Gelu_apprx_tanh).then_inc(hid_made, 1)
                act.wait_ge(prod_made, s.n + 1)
                if s.from_(BODY):
                    act.wait_ge(y_ready, s.quad * OUTS)
                act.copy(p_half[s.j][0][:], prod[s.j % 2][:]).then_inc(ph_made, 1)

            def behind(s):
                act.wait_ge(v_in[s.j % PART], s.quad * 16 + 16)
                act.wait_ge(y_ready, OUTS + s.quad * OUTS)
                act.copy(v_half[s.j % PART][0][:], v_raw[s.j % PART][:]).then_inc(vh_made, 1)

            split_u(Set(0, 0, 0))
            split_u(Set(1, 0, 1))
            walk(act, hidden, lambda s: None, behind)

        @block.vector
        def _(v):
            def low(halves, raw, n, made, done):
                v.wait_ge(made, n + 1)
                v.tensor_tensor(halves[1][:], raw[:], halves[0][:].bitcast(F32), ALU.subtract).then_inc(done, 1)

            def hidden(s):
                if not (isinstance(s.n, int) and s.n >= SETS - 2):
                    u = s + 2
                    low(u_half[u.j % 2], u_raw[u.j % PART], u.n, uh_made, ul_made)
                v.wait_ge(hid_made, s.n + 1)
                v.wait_ge(g_in[s.j % PART], s.quad * 16 + 16)
                v.tensor_tensor(prod[s.j % 2][:], hid[s.j % 2][:], g_raw[s.j % PART][:],
                                ALU.mult).then_inc(prod_made, 1)
                low(p_half[s.j], prod[s.j % 2], s.n, ph_made, pl_made)

            def output(s):
                for o in range(OUTS):
                    part = y[:, o // 2, (o % 2) * 512:(o % 2 + 1) * 512]
                    v.wait_ge(y_ready, OUTS + s.quad * OUTS + o + 1)
                    v.wait_ge(y_taken, s.quad * OUTS + o + 1)
                    v.tensor_tensor(part, bank_y[o % 4][:], part, ALU.add).then_inc(y_taken, 1)

            v.wait_ge(cleared, 1)
            for k in range(2):
                low(u_half[k], u_raw[k], k, uh_made, ul_made)
            walk(v, hidden, output,
                 lambda s: low(v_half[s.j % PART], v_raw[s.j % PART], s.n, vh_made, vl_made))
            v.wait_ge(y_taken, OUTS + SETS // PART * OUTS)
            v.tensor_tensor(x[:], x[:], y[:], ALU.add)


def peer(nc, c, tag, x, a, l):
    gmat = nc.dram_tensor(f"{tag}_gmat", (PEER_K, PEER_K, SEQ), F32, kind="Internal").ap()
    with Tiles(nc, tag) as keep:
        xs = halves(keep, "xs", [P, KD, SEQ])
        normed_transpose(nc, c, tag + "n", x, a[f"{l}_ffn_norm"], xs)
        with Tiles(nc, tag + "g") as t:
            turned = [t.sb(n, [P, SEQ]) for n in ("gT", "rT", "cT")]
            with Tiles(nc, tag + "r") as t2:
                parts = [t2.sb(n, [P, NT, P]) for n in ("gates", "rows", "cols")]
                retrieve(nc, c, tag + "q", xs, a[f"{l}_peer_wq"], a[f"{l}_peer_subkeysT"], *parts)
                turn(nc, c, tag + "t", [(d[:], [p[:, m, :] for m in range(NT)], P) for d, p in zip(turned, parts)])
            spread_gates(nc, c, tag + "s", *turned, gmat)
        all_experts(nc, c, tag + "e", xs, a[f"{l}_peer_uT"], a[f"{l}_peer_v"], gmat, x)


def store(nc, c, tag, x, out):
    with Tiles(nc, tag) as t:
        stored = t.sem("stored")
        block = t.block()

        @block.sync
        def _(sp):
            sp.dma_start(out.rearrange("(t p) d -> p t d", p=P), x[:]).then_inc(stored, 16)
            sp.wait_ge(stored, 16)


def trunk(nc, a, tables, out):
    with Tiles(nc, "all") as t:
        c = Consts(nc, t, tables)
        x = t.sb("x", [P, NT, D])
        load_all(nc, t, c, a["x"], x)
        layer0_mixer(nc, c, x, a)
        end_half(nc)
        peer(nc, c, "f0", x, a, "l0")
        end_half(nc)
        layer1_mixer(nc, c, x, a)
        end_half(nc)
        peer(nc, c, "f1", x, a, "l1")
        store(nc, c, "out", x, out)


def host_tables():
    f = np.float32
    half = HD // 2
    inv = (f(10000.0) ** (-np.arange(half, dtype=f) / f(half))).astype(f)

    def rope(pos):
        ang = pos.astype(f)[:, None] * inv[None, :]
        return np.cos(ang).astype(f), np.sin(ang).astype(f)

    cos, sin = rope(np.arange(SEQ))
    tiles = lambda m: np.ascontiguousarray(m.reshape(NT, P, half).transpose(1, 0, 2))
    pos = np.tile(np.arange(32) * CMP_STRIDE + CMP_LEN - 1, 2)
    ccos, csin = rope(pos)
    i = np.arange(P)
    same = (i[:, None] // GLA_C) == (i[None, :] // GLA_C)
    tq = np.arange(SEQ).reshape(NT, P).T
    cmask = ((np.arange(32) * CMP_STRIDE + CMP_LEN - 1)[None, None, :] <= tq[:, :, None]).astype(f)
    return {
        "ident": np.eye(P, dtype=f),
        "causal": np.where(i[None, :] <= i[:, None], 0.0, NEG).astype(f),
        "cos": tiles(cos), "sin": tiles(sin),
        "ccos": ccos[:, None, :], "csin": csin[:, None, :],
        "cmask": cmask, "cbias": np.where(cmask > 0, 0.0, NEG).astype(f),
        "upto": (same & (i[:, None] <= i[None, :])).astype(f),
        "after": (same & (i[:, None] > i[None, :])).astype(f),
        "chunk": ((i[:, None] // GLA_C) == np.arange(4)[None, :]).astype(f),
        "iota": np.tile(np.arange(P, dtype=f), (P, 1)),
    }


def lay_out(inputs):
    f = {k: np.asarray(v) for k, v in inputs.items()}
    out = {k: np.ascontiguousarray(v) for k, v in f.items() if not k.startswith("l0_s5") and not k.endswith("_peer_u")
           and not k.endswith("_peer_subkeys")}
    out["x"] = f["x"].reshape(SEQ, D)
    out["l0_s5_w_glu"] = f["l0_s5_w_glu"]

    def states(m):
        m = m.reshape(S5_GP, 2, *m.shape[1:])
        m = np.moveaxis(m, 0, 2)
        return np.ascontiguousarray(m.reshape(P, *m.shape[2:]))

    out["log_dt"] = states(np.repeat(f["l0_s5_log_dt"][:, None], S5_P, axis=1))
    out["a_re"], out["a_im"] = states(f["l0_s5_a_re"]), states(f["l0_s5_a_im"])
    out["b_re"], out["b_im"] = states(f["l0_s5_b_re"]), states(f["l0_s5_b_im"])
    out["c_re"] = states(np.swapaxes(f["l0_s5_c_re"], 1, 2))
    out["c_im"] = states(np.swapaxes(f["l0_s5_c_im"], 1, 2))
    out["d_skip"] = np.ascontiguousarray(f["l0_s5_d"].T)
    out["b_glu"] = np.ascontiguousarray(f["l0_s5_b_glu"].reshape(4, P).T)
    out["l1_nsa_cmp_pos"] = np.ascontiguousarray(f["l1_nsa_cmp_pos"].T)
    for l in ("l0", "l1"):
        u = f[f"{l}_peer_u"].reshape(PEER_K, PEER_K, KD, P)
        out[f"{l}_peer_uT"] = np.ascontiguousarray(u.transpose(1, 3, 2, 0)).reshape(PEER_K, P, D)
        sk = f[f"{l}_peer_subkeys"].reshape(NLIST, PEER_K, P)
        out[f"{l}_peer_subkeysT"] = np.ascontiguousarray(sk.transpose(2, 0, 1))
    return out


def kernel(**inputs):
    import concourse.bacc as bacc
    from concourse.bass_utils import run_bass_kernel_spmd as run

    nc = bacc.Bacc("TRN2", target_bir_lowering=False, num_devices=1)
    arrays = lay_out(inputs)
    tables = host_tables()
    aps = {k: nc.dram_tensor(k, v.shape, mybir.dt.from_np(v.dtype), kind="ExternalInput").ap()
           for k, v in arrays.items()}
    taps = {k: nc.dram_tensor(f"table_{k}", v.shape, F32, kind="ExternalInput").ap() for k, v in tables.items()}
    out = nc.dram_tensor("out", (SEQ, D), F32, kind="ExternalOutput").ap()
    trunk(nc, aps, taps, out)
    r = run(nc, [{**arrays, **{f"table_{k}": v for k, v in tables.items()}}], core_ids=[0])
    return r.results[0]["out"].reshape(1, SEQ, D)
```

```python
from contextlib import ExitStack

import numpy as np

import concourse.bass as bass
from concourse import mybir

F32 = mybir.dt.float32
F32R = mybir.dt.float32r
U32 = mybir.dt.uint32
ALU = mybir.AluOpType
ACT = mybir.ActivationFunctionType
AX = mybir.AxisListType
ds = bass.ds

P = 128
D = 1024
KD = D // P
SEQ = 512
NT = SEQ // P
HD = 64
NH = 8
EPS = 1e-6
NEG = -1e30
TAKEN = -3e38
LEAD = 1

S5_G, S5_C, S5_P = 32, 16, 64
S5_L = 8
S5_NC = SEQ // S5_L
S5_GP = S5_G // 2
WIDTH_B = S5_G * S5_C

L0_COLS = dict(q=(0, 512), k=(512, 128), v=(640, 128), iq=(768, 512), ik=(1280, 64), iw=(1344, 8), u=(1352, 512))
L1_COLS = dict(q=(0, 512), kc=(512, 128), vc=(640, 128), ks=(768, 128), vs=(896, 128), kw=(1024, 128),
               vw=(1152, 128), gl=(1280, 24), gq=(1304, 256), gk=(1560, 256), gv=(1816, 512),
               glow=(2328, 16), gr=(2344, 512))
L0_WIDTH = 1352
L1_WIDTH = 2856
TOPK_ATT = 128
CMP_LEN, CMP_STRIDE, CMP_HID = 32, 16, 256
NCMP = (SEQ - CMP_LEN) // CMP_STRIDE + 1
GLA_H, GLA_K, GLA_V, GLA_C = 4, 64, 128, 32
GLA_N = SEQ // GLA_C
PEER_H, PEER_K, PEER_TOP = 8, 128, 16
NLIST = 2 * PEER_H
PART_T = 64
PARTS = SEQ // PART_T


class Tiles:

    opened = []

    def __init__(self, nc, tag, shared=None):
        self.nc, self.tag, self.shared = nc, tag, shared
        self.stack = shared.stack if shared else ExitStack()
        self.running = None

    def __enter__(self):
        if not self.shared:
            self.stack.__enter__()
        return self

    def __exit__(self, *a):
        return None if self.shared else self.stack.__exit__(*a)

    def sb(self, name, shape, dt=F32):
        return self.stack.enter_context(self.nc.sbuf_tensor(f"{self.tag}_{name}", shape, dt))

    def banks(self, name, n=1):
        return [self.stack.enter_context(self.nc.psum_tensor(f"{self.tag}_{name}{i}", [P, 512], F32))
                for i in range(n)]

    def sem(self, name):
        Tiles.opened.append(self.nc.alloc_semaphore(f"{self.tag}_{name}"))
        return Tiles.opened[-1]

    def sems(self, name, n):
        return [self.sem(f"{name}{i}") for i in range(n)]

    def lead(self, name, by=LEAD):
        sem = self.sem(name)
        if self.shared:
            @self.shared.running.sync
            def _(sp):
                sp.sem_inc(sem, by)
        else:
            self.nc.sync.sem_inc(sem, by)
        return sem

    def leads(self, name, n):
        return [self.lead(f"{name}{i}") for i in range(n)]

    def block(self):
        if self.shared:
            return self.shared.running
        self.running = self.stack.enter_context(self.nc.Block())
        return self.running


def end_half(nc):
    nc.all_engine_barrier()
    nc.clear_and_free_semaphores(Tiles.opened)
    Tiles.opened.clear()
    nc.all_engine_barrier()


class Chain:

    def __init__(self, eng, sem):
        self.eng, self.sem, self.n, self.off = eng, sem, 0, 0

    def put(self, ins):
        self.n += 1
        ins.then_inc(self.sem, 1)

    def link(self, ins):
        self.put(ins)
        self.eng.wait_ge(self.sem, self.n + self.off)

    def enter(self, i, per):
        self.off, self.per, self.first = i * per, per, self.n

    def leave(self, trips):
        assert self.n == self.first + self.per, (self.n - self.first, self.per)
        self.n, self.off = self.first + trips * self.per, 0


class Consts:

    def __init__(self, nc, t, tables):
        self.loaded = t.stack.enter_context(nc.semaphore("constants_loaded"))
        self.n = 16 * len(tables)
        self.tile, self.src = {}, tables
        for name, ap in tables.items():
            self.tile[name] = t.sb(name, list(ap.shape))

    def __getitem__(self, name):
        return self.tile[name]

    def there(self, eng):
        eng.wait_ge(self.loaded, self.n)


def bc(ap, axis, n):
    a = ap.unsqueeze(axis)
    shape = list(a.shape)
    shape[axis] = n
    return a.broadcast_to(shape)


def passes(pe, out, w, m, first, final):
    pe.matmul(out, w[0], m[0], start=first, stop=False)
    pe.matmul(out, w[0], m[1], start=False, stop=False)
    return pe.matmul(out, w[1], m[0], start=False, stop=final)


def load_all(nc, t, c, x_in, x):
    x_loaded = t.sem("x_loaded")
    with nc.Block() as block:
        @block.sync
        def _(sp):
            sp.dma_start(x[:], x_in.rearrange("(t p) d -> p t d", p=P)).then_inc(x_loaded, 16)
            for name, ap in c.src.items():
                sp.dma_start(c[name][:], ap).then_inc(c.loaded, 16)
            sp.wait_ge(x_loaded, 16)
            sp.wait_ge(c.loaded, c.n)


def rstd_steps(v, ch, ms, root, r, root_ready, count):
    v.wait_ge(root_ready, count)
    ch.link(v.reciprocal(r, root))
    ch.link(v.tensor_tensor(root, r, r, ALU.mult))
    ch.link(v.tensor_tensor(root, root, ms, ALU.mult))
    ch.link(v.tensor_scalar(root, root, -0.5, 1.5, ALU.mult, ALU.add))
    ch.link(v.tensor_tensor(r, r, root, ALU.mult))


def normed_transpose(nc, c, tag, x, gain_dram, hT):
    with Tiles(nc, tag) as t:
        gain = t.sb("gain", [P, D])
        xn = t.sb("xn", [P, NT, D])
        ms, root, r = t.sb("ms", [P, NT]), t.sb("root", [P, NT]), t.sb("r", [P, NT])
        bank = t.banks("turned", 4)
        gain_in, ms_ready, root_ready = t.sem("gain_in"), t.sem("ms_ready"), t.sem("root_ready")
        dve, turned, taken, normed = t.sem("dve"), t.sem("turned"), t.sems("taken", 4), t.sem("normed")
        high = t.sem("high")
        block = t.block()

        @block.sync
        def _(sp):
            sp.dma_start(gain[:], gain_dram.partition_broadcast(P)).then_inc(gain_in, 16)

        @block.vector
        def _(v):
            ch = Chain(v, dve)
            for i in range(NT):
                ch.put(v.tensor_tensor_reduce(out=xn[:, i, :], in0=x[:, i, :], in1=x[:, i, :], scale=1.0 / D,
                                              scalar=0.0, op0=ALU.mult, op1=ALU.add, accum_out=ms[:, i:i + 1]))
            v.wait_ge(dve, ch.n)
            v.tensor_scalar(ms[:], ms[:], EPS, None, ALU.add).then_inc(ms_ready, 1)
            rstd_steps(v, ch, ms[:], root[:], r[:], root_ready, 1)
            v.wait_ge(gain_in, 16)
            for i in range(NT):
                v.scalar_tensor_tensor(out=xn[:, i, :], in0=x[:, i, :], scalar=r[:, i:i + 1], in1=gain[:],
                                       op0=ALU.mult, op1=ALU.mult).then_inc(normed, 1)
            for k in range(KD):
                v.wait_ge(high, k + 1)
                v.tensor_tensor(hT[1][:, k, :], bank[k % 4][:], hT[0][:, k, :].bitcast(F32),
                                ALU.subtract).then_inc(taken[k % 4], 1)

        @block.scalar
        def _(act):
            act.wait_ge(ms_ready, 1)
            act.activation(root[:], ms[:], ACT.Sqrt).then_inc(root_ready, 1)
            for k in range(KD):
                act.wait_ge(turned, k + 1)
                act.copy(hT[0][:, k, :], bank[k % 4][:]).then_inc(high, 1)

        @block.tensor
        def _(pe):
            c.there(pe)
            pe.wait_ge(normed, NT)
            for k in range(KD):
                if k >= 4:
                    pe.wait_ge(taken[k % 4], k // 4)
                for i in range(NT):
                    mm = pe.transpose(bank[k % 4][:, i * P:(i + 1) * P], xn[:, i, k * P:(k + 1) * P], c["ident"][:])
                mm.then_inc(turned, 1)


def project(nc, c, tag, lhsT, w, width, step, dst, add=False, shared=None):
    w_view = w.rearrange("(k p) n -> p k n", p=P)
    kk = w_view.shape[1]
    trips = width // (2 * step)
    assert trips * 2 * step == width
    with Tiles(nc, tag, shared) as t:
        raw = [t.sb(f"raw{s}", [P, kk, step]) for s in range(2)]
        halves = [[t.sb(f"w{s}{half}", [P, kk, step], F32R) for half in "hl"] for s in range(2)]
        bank = t.banks("out", 8)
        w_in, high, low = t.sems("w_in", 2), t.sems("high", 2), t.leads("low", 2)
        ready, taken = t.leads("ready", 2), t.leads("taken", 2)
        block = t.block()

        @block.sync
        def _(sp):
            with sp.Fori(0, trips) as i:
                for s in range(2):
                    sp.wait_ge(low[s], LEAD + i)
                    sp.dma_start(raw[s][:], w_view[:, :, ds((i * 2 + s) * step, step)]).then_inc(w_in[s], 16)

        @block.scalar
        def _(act):
            with act.Fori(0, trips) as i:
                for s in range(2):
                    act.wait_ge(w_in[s], i * 16 + 16)
                    act.wait_ge(ready[s], LEAD + i * NT)
                    act.copy(halves[s][0][:], raw[s][:]).then_inc(high[s], 1)

        @block.gpsimd
        def _(pool):
            with pool.Fori(0, trips) as i:
                for s in range(2):
                    pool.wait_ge(high[s], i + 1)
                    pool.tensor_tensor(halves[s][1][:], raw[s][:], halves[s][0][:].bitcast(F32),
                                       ALU.subtract).then_inc(low[s], 1)

        @block.tensor
        def _(pe):
            with pe.Fori(0, trips) as i:
                for s in range(2):
                    pe.wait_ge(low[s], LEAD + i + 1)
                    pe.wait_ge(taken[s], LEAD + i * NT)
                    for m in range(NT):
                        for k in range(kk):
                            mm = passes(pe, bank[s * 4 + m][:, 0:step], [h[:, k, m * P:(m + 1) * P] for h in lhsT],
                                        [h[:, k, :] for h in halves[s]], k == 0, k == kk - 1)
                        mm.then_inc(ready[s], 1)

        @block.vector
        def _(v):
            with v.Fori(0, trips) as i:
                for s in range(2):
                    for m in range(NT):
                        out = dst[:, m, ds((i * 2 + s) * step, step)]
                        v.wait_ge(ready[s], LEAD + i * NT + m + 1)
                        if add:
                            ins = v.tensor_tensor(out, bank[s * 4 + m][:, 0:step], out, ALU.add)
                        else:
                            ins = v.tensor_copy(out, bank[s * 4 + m][:, 0:step])
                        ins.then_inc(taken[s], 1)


def prepare_heads(nc, c, tag, jobs, cos, sin, shared=None):
    with Tiles(nc, tag, shared) as t:
        rows, nt = jobs[0][0].shape[0], jobs[0][0].shape[1]
        widest = max(a.shape[2] for a, _ in jobs)
        ta, tb = t.sb("ta", [rows, nt, widest, HD]), t.sb("tb", [rows, nt, widest, HD])
        ms, root, r = [t.sb(n, [rows, nt, widest]) for n in ("ms", "root", "r")]
        gains = [g for _, g in jobs if g is not None]
        gain = t.sb("gain", [rows, max(len(gains), 1), HD])
        dve, ms_ready, root_ready, gain_in = t.sem("dve"), t.sem("ms_ready"), t.sem("root_ready"), t.sem("gain_in")
        block = t.block()

        @block.sync
        def _(sp):
            for n, g in enumerate(gains):
                sp.dma_start(gain[:, n, :], g.partition_broadcast(rows)).then_inc(gain_in, 16)

        @block.vector
        def _(v):
            ch = Chain(v, dve)
            n = 0
            for a, g in jobs:
                heads = a.shape[2]
                if g is not None:
                    full, few = [rows, nt, heads, HD], slice(0, heads)
                    ch.link(v.tensor_tensor(ta[:, :, few, :], a, a, ALU.mult))
                    ch.link(v.tensor_reduce(ms[:, :, few], ta[:, :, few, :], AX.X, ALU.add))
                    v.tensor_scalar(ms[:, :, few], ms[:, :, few], 1.0 / HD, EPS, ALU.mult,
                                    ALU.add).then_inc(ms_ready, 1)
                    n += 1
                    rstd_steps(v, ch, ms[:, :, few], root[:, :, few], r[:, :, few], root_ready, n)
                    v.wait_ge(gain_in, 16 * len(gains))
                    ch.link(v.tensor_tensor(a, a, r[:, :, few].unsqueeze(3).broadcast_to(full), ALU.mult))
                    ch.link(v.tensor_tensor(a, a, gain[:, n - 1, :].unsqueeze(1).unsqueeze(1).broadcast_to(full),
                                            ALU.mult))
                x1, x2 = a[:, :, :, 0:HD // 2], a[:, :, :, HD // 2:HD]
                cs, sn = [bc(m, 2, heads) for m in (cos, sin)]
                a1, a2 = ta[:, :, 0:heads, 0:HD // 2], ta[:, :, 0:heads, HD // 2:HD]
                b1, b2 = tb[:, :, 0:heads, 0:HD // 2], tb[:, :, 0:heads, HD // 2:HD]
                ch.put(v.tensor_tensor(a1, x1, cs, ALU.mult))
                ch.put(v.tensor_tensor(a2, x2, sn, ALU.mult))
                ch.put(v.tensor_tensor(b1, x1, sn, ALU.mult))
                ch.link(v.tensor_tensor(b2, x2, cs, ALU.mult))
                ch.put(v.tensor_tensor(x1, a1, a2, ALU.subtract))
                ch.link(v.tensor_tensor(x2, b1, b2, ALU.add))

        @block.scalar
        def _(act):
            n = 0
            for a, g in jobs:
                if g is not None:
                    few = slice(0, a.shape[2])
                    n += 1
                    act.wait_ge(ms_ready, n)
                    act.activation(root[:, :, few], ms[:, :, few], ACT.Sqrt).then_inc(root_ready, 1)


def turn(nc, c, tag, blocks, zero=()):
    with Tiles(nc, tag) as t:
        bank = t.banks("turned", 4)
        turned, taken, high = t.sem("turned"), t.sems("taken", 4), t.sem("high")
        block = t.block()
        split = isinstance(blocks[0][0], tuple)

        @block.tensor
        def _(pe):
            c.there(pe)
            for n, (dst, srcs, rows) in enumerate(blocks):
                if n >= 4:
                    pe.wait_ge(taken[n % 4], n // 4)
                at = 0
                for src in srcs:
                    k = src.shape[0]
                    mm = pe.transpose(bank[n % 4][0:rows, at:at + k], src, c["ident"][0:k, 0:k])
                    at += k
                mm.then_inc(turned, 1)

        def turned_block(n):
            _, srcs, rows = blocks[n]
            return bank[n % 4][0:rows, 0:sum(s.shape[0] for s in srcs)]

        @block.gpsimd
        def _(pool):
            for z in zero:
                pool.memset(z, 0.0)

        @block.vector
        def _(v):
            for n, (dst, _, _) in enumerate(blocks):
                if split:
                    v.wait_ge(high, n + 1)
                    v.tensor_tensor(dst[1], turned_block(n), dst[0].bitcast(F32),
                                    ALU.subtract).then_inc(taken[n % 4], 1)
                elif n % 2 == 0:
                    v.wait_ge(turned, n + 1)
                    v.tensor_copy(dst, turned_block(n)).then_inc(taken[n % 4], 1)

        @block.scalar
        def _(act):
            for n, (dst, _, _) in enumerate(blocks):
                if split:
                    act.wait_ge(turned, n + 1)
                    act.copy(dst[0], turned_block(n)).then_inc(high, 1)
                elif n % 2 == 1:
                    act.wait_ge(turned, n + 1)
                    act.copy(dst, turned_block(n)).then_inc(taken[n % 4], 1)


def index_scores(nc, c, tag, iq, iw, ikT, score):
    with Tiles(nc, tag) as t:
        staged = t.sb("staged", [P, NT, P])
        qT = t.sb("qT", [P, SEQ])
        rel = [t.sb(f"rel{m}", [P, (m + 1) * P]) for m in range(1, NT)]
        bank_q = t.banks("q")[0]
        bank = t.banks("s", NT - 1)
        q_staged, q_turned, q_there = t.sem("q_staged"), t.lead("q_turned"), t.sem("q_there")
        s_ready, rel_ready, rel_used, cleared = t.lead("s_ready"), t.lead("rel_ready"), t.lead("rel_used"), t.sem("clr")
        block = t.block()
        M = NT - 1

        @block.gpsimd
        def _(pool):
            pool.memset(score[:], 0.0).then_inc(cleared, 1)
            pool.memset(staged[:], 0.0).then_inc(cleared, 1)
            pool.wait_ge(cleared, 2)
            with pool.Fori(0, NH) as h:
                pool.wait_ge(q_turned, LEAD + h)
                pool.tensor_copy(staged[:, :, 0:HD], iq[:, :, ds(h * HD, HD)]).then_inc(q_staged, 1)

        @block.tensor
        def _(pe):
            c.there(pe)
            with pe.Fori(0, NH) as h:
                pe.wait_ge(q_staged, h + 1)
                for m in range(NT):
                    mm = pe.transpose(bank_q[:, m * P:(m + 1) * P], staged[:, m, :], c["ident"][:])
                mm.then_inc(q_turned, 1)
                pe.wait_ge(q_there, h + 1)
                pe.wait_ge(rel_ready, LEAD + h * M)
                for m in range(1, NT):
                    n = (m + 1) * P
                    pe.matmul(bank[m - 1][:, 0:n], qT[:, m * P:(m + 1) * P], ikT[:, 0:n],
                              start=True, stop=True).then_inc(s_ready, 1)

        @block.scalar
        def _(act):
            with act.Fori(0, NH) as h:
                act.wait_ge(q_turned, LEAD + h + 1)
                act.wait_ge(s_ready, LEAD + h * M)
                act.copy(qT[:], bank_q[:]).then_inc(q_there, 1)
                for m in range(1, NT):
                    act.wait_ge(s_ready, LEAD + h * M + m)
                    act.wait_ge(rel_used, LEAD + h * M)
                    act.activation(rel[m - 1][:], bank[m - 1][:, 0:(m + 1) * P], ACT.Relu,
                                   scale=HD ** -0.5).then_inc(rel_ready, 1)

        @block.vector
        def _(v):
            v.wait_ge(cleared, 2)
            with v.Fori(0, NH) as h:
                for m in range(1, NT):
                    s = score[:, m, 0:(m + 1) * P]
                    v.wait_ge(rel_ready, LEAD + h * M + m)
                    v.wait_ge(rel_used, LEAD + h * M)
                    v.scalar_tensor_tensor(out=s, in0=rel[m - 1][:], scalar=iw[:, m, ds(h, 1)], in1=s,
                                           op0=ALU.mult, op1=ALU.add).then_inc(rel_used, 1)


def select_keys(nc, c, tag, score, bias, shared=None):
    with Tiles(nc, tag, shared) as t:
        best = [t.sb(f"best{m}", [P, 8]) for m in range(NT)]
        dve = t.sem("dve")
        block = t.block()

        @block.vector
        def _(v):
            ch = Chain(v, dve)
            c.there(v)
            for m in range(1, NT):
                diag = score[:, m, m * P:(m + 1) * P]
                ch.put(v.tensor_tensor(diag, diag, c["causal"][:], ALU.add))
            ch.link(v.tensor_copy(bias[:, 0, 0:P], c["causal"][:]))
            for _ in range(TOPK_ATT // 8):
                for m in range(1, NT):
                    ch.put(v.max(best[m][:], score[:, m, 0:(m + 1) * P]))
                v.wait_ge(dve, ch.n)
                for m in range(1, NT):
                    s = score[:, m, 0:(m + 1) * P]
                    ch.put(v.match_replace(s, best[m][:], s, TAKEN))
                v.wait_ge(dve, ch.n)
            for m in range(1, NT):
                n = (m + 1) * P
                ch.put(v.tensor_scalar(bias[:, m, 0:n], score[:, m, 0:n], TAKEN / 2, -NEG, ALU.is_lt, ALU.mult))
            v.wait_ge(dve, ch.n)
            for m in range(1, NT):
                n = (m + 1) * P
                ch.put(v.tensor_scalar(bias[:, m, 0:n], bias[:, m, 0:n], NEG, None, ALU.add))
            v.wait_ge(dve, ch.n)


def causal_bias(nc, c, tag, bias, shared=None):
    with Tiles(nc, tag, shared) as t:
        dve = t.sem("dve")
        block = t.block()

        @block.vector
        def _(v):
            ch = Chain(v, dve)
            c.there(v)
            ch.link(v.memset(bias[:], 0.0))
            for m in range(NT):
                ch.link(v.tensor_copy(bias[:, m, m * P:(m + 1) * P], c["causal"][:]))


def attention(nc, c, tag, qT, kT, vals, bias, out, gate=None, add=False):
    with Tiles(nc, tag) as t:
        q = [t.sb(f"q{g}", [P, SEQ]) for g in range(2)]
        sm = [t.sb(f"sm{m}", [P, (m + 1) * P]) for m in range(NT)]
        pT = [t.sb(f"pT{b}", [P, SEQ]) for b in range(2)]
        mx, nmx, den, rden = [t.sb(n, [P, NT]) for n in ("mx", "nmx", "den", "rden")]
        bank_s, bank_t, bank_o = t.banks("s", NT), t.banks("t", 2), t.banks("o", 2)
        q_there, s_ready, s_taken = t.sem("q_there"), t.lead("s_ready", 2 * NT), t.leads("s_taken", NT)
        m_ready, p_ready = t.sem("m_ready"), t.sem("p_ready")
        t_ready, t_taken = t.lead("t_ready"), t.leads("t_taken", 2)
        o_ready, o_taken, dve = t.sem("o_ready"), t.leads("o_taken", 2), t.sem("dve")
        wait_taker = t.sb("wait_taker", [P, 1])
        block = t.block()
        TRIPS = NH // 2

        def trips(eng, step):
            with eng.Fori(0, TRIPS - 1) as r:
                step(r, 0, (r, 1))
                step(r, 1, (r + 1, 0))
            step(TRIPS - 1, 0, (TRIPS - 1, 1))
            step(TRIPS - 1, 1, None)

        @block.tensor
        def _(pe):
            def scores(r, g, m):
                pe.wait_ge(s_taken[m], LEAD + r * 2 + g)
                n = (m + 1) * P
                pe.matmul(bank_s[m][:, 0:n], q[g][:, m * P:(m + 1) * P], kT[:, g, 0:n], start=True,
                          stop=True).then_inc(s_ready, 1)

            def turn_probs(n, m):
                pe.wait_ge(p_ready, n * NT + m + 1)
                pe.wait_ge(t_taken[m % 2], LEAD + n * 2 + m // 2)
                for s in range(m + 1):
                    mm = pe.transpose(bank_t[m % 2][:, s * P:(s + 1) * P], sm[m][:, s * P:(s + 1) * P], c["ident"][:])
                mm.then_inc(t_ready, 1)

            def weigh(n, g, m):
                pe.wait_ge(t_taken[m % 2], LEAD + n * 2 + m // 2 + 1)
                pe.wait_ge(o_taken[m % 2], LEAD + n * 2 + m // 2)
                for s in range(m + 1):
                    mm = pe.matmul(bank_o[m % 2][:, 0:HD], pT[m % 2][:, s * P:(s + 1) * P],
                                   vals[:, s, g * HD:(g + 1) * HD], start=s == 0, stop=s == m)
                mm.then_inc(o_ready, 1)

            def step(r, g, then):
                n = r * 2 + g
                if then:
                    pe.wait_ge(q_there, n + 2)
                for m in range(NT):
                    turn_probs(n, m)
                    if then:
                        scores(*then, m)
                    if m:
                        weigh(n, g, m - 1)
                weigh(n, g, NT - 1)

            c.there(pe)
            pe.wait_ge(q_there, 1)
            for m in range(NT):
                scores(0, 0, m)
            trips(pe, step)

        @block.scalar
        def _(act):
            def place(r, g):
                act.wait_ge(s_ready, (r * 2 + g + 1) * NT)
                act.copy(q[g][:], qT[:, ds(r + g * TRIPS, 1), :].rearrange("p a n -> p (a n)")).then_inc(q_there, 1)

            def step(r, g, then):
                if then:
                    place(*then)
                for m in range(NT):
                    act.wait_ge(m_ready, (r * 2 + g) * NT + m + 1)
                    act.activation(sm[m][:], sm[m][:], ACT.Exp, bias=nmx[:, m:m + 1],
                                   accum_out=den[:, m:m + 1]).then_inc(p_ready, 1)

            place(0, 0)
            trips(act, step)

        @block.vector
        def _(v):
            ch = Chain(v, dve)

            def add_bias(r, g, m):
                n, keys = r * 2 + g, (m + 1) * P
                v.wait_ge(s_ready, 2 * NT + n * NT + m + 1)
                v.wait_ge(t_ready, LEAD + (n - 1) * NT + m + 1 if not isinstance(n, int) or n else LEAD)
                v.memset(wait_taker[:], 0.0)
                v.tensor_tensor_reduce(out=sm[m][:], in0=bank_s[m][:, 0:keys], in1=bias[:, m, 0:keys],
                                       scale=HD ** -0.5, scalar=TAKEN, op0=ALU.add, op1=ALU.max,
                                       accum_out=mx[:, m:m + 1]).then_inc(s_taken[m], 1)
                v.wait_ge(s_taken[m], LEAD + n + 1)
                v.tensor_scalar(nmx[:, m:m + 1], mx[:, m:m + 1], -1.0, None, ALU.mult).then_inc(m_ready, 1)

            def output(r, g, m):
                o = out[:, m, ds((r + g * TRIPS) * HD, HD)]
                v.wait_ge(o_ready, (r * 2 + g) * NT + m + 1)
                if add:
                    ins = v.scalar_tensor_tensor(out=o, in0=bank_o[m % 2][:, 0:HD], scalar=rden[:, m:m + 1],
                                                 in1=o, op0=ALU.mult, op1=ALU.add)
                else:
                    ins = v.tensor_scalar(o, bank_o[m % 2][:, 0:HD], rden[:, m:m + 1], None, ALU.mult)
                ins.then_inc(o_taken[m % 2], 1)

            def step(r, g, then):
                n = r * 2 + g
                for m in range(NT):
                    keys = (m + 1) * P
                    v.wait_ge(t_ready, LEAD + n * NT + m + 1)
                    v.tensor_copy(pT[m % 2][:, 0:keys], bank_t[m % 2][:, 0:keys]).then_inc(t_taken[m % 2], 1)
                    if m == 0:
                        v.wait_ge(p_ready, n * NT + NT)
                        for b in range(2):
                            v.wait_ge(o_taken[b], LEAD + n * 2)
                        ch.link(v.tensor_scalar(rden[:], den[:], 1e-30, None, ALU.max))
                        ch.link(v.reciprocal(rden[:], rden[:]))
                        if gate is not None:
                            ch.link(v.tensor_tensor(rden[:].unsqueeze(2), rden[:].unsqueeze(2),
                                                    gate[:, :, ds(r + g * TRIPS, 1)], ALU.mult))
                    if then:
                        add_bias(*then, m)
                    if m:
                        output(r, g, m - 1)
                output(r, g, NT - 1)

            for m in range(NT):
                add_bias(0, 0, m)
            per = 2 if gate is None else 3
            with v.Fori(0, TRIPS - 1) as r:
                ch.enter(r, 2 * per)
                step(r, 0, (r, 1))
                step(r, 1, (r + 1, 0))
            ch.leave(TRIPS - 1)
            step(TRIPS - 1, 0, (TRIPS - 1, 1))
            step(TRIPS - 1, 1, None)


def s5_inputs(nc, c, tag, hT, w, U, shared=None):
    off = L0_COLS["u"][0]
    w_view = w.rearrange("(k p) n -> p k n", p=P)[:, :, off:off + WIDTH_B]
    PAIRS, STEP, HALF = S5_L // 2, WIDTH_B // 2, S5_G // 2
    with Tiles(nc, tag, shared) as t:
        raw = [t.sb(f"raw{s}", [P, KD, STEP]) for s in range(2)]
        halves = [[t.sb(f"w{s}{half}", [P, KD, STEP], F32R) for half in "hl"] for s in range(2)]
        u_sb = t.sb("u", [P, S5_G, PAIRS, S5_C])
        bank = t.banks("out", 4)
        bank_t = t.banks("t", 4)
        w_in, high, low = t.sems("w_in", 2), t.sem("high"), t.sem("low")
        ready, taken, turned = t.sem("ready"), t.sem("taken"), t.sem("turned")
        early_moved, moved = t.sem("early_moved"), t.sem("moved")
        block = t.block()

        @block.sync
        def _(sp):
            for s in range(2):
                sp.dma_start(raw[s][:], w_view[:, :, s * STEP:(s + 1) * STEP]).then_inc(w_in[s], 16)

        @block.gpsimd
        def _(pool):
            for s in range(2):
                pool.wait_ge(high, s + 1)
                pool.tensor_tensor(halves[s][1][:], raw[s][:], halves[s][0][:].bitcast(F32),
                                   ALU.subtract).then_inc(low, 1)

        @block.tensor
        def _(pe):
            for s in range(2):
                pe.wait_ge(low, s + 1)
                if s:
                    pe.wait_ge(taken, PAIRS)
                for l in range(PAIRS):
                    for k in range(KD):
                        mm = passes(pe, bank[l][:, 0:STEP],
                                    [h[:, k, l:SEQ:PAIRS] for h in hT],
                                    [h[:, k, :] for h in halves[s]], k == 0, k == KD - 1)
                    mm.then_inc(ready, 1)
            c.there(pe)
            pe.wait_ge(taken, 2 * PAIRS)
            for g in range(S5_G):
                b = g // 4 % 4
                if g % 4 == 0 and g >= 16:
                    pe.wait_ge(moved, g // 4 - 3)
                mm = pe.transpose(bank_t[b][0:64, (g % 4) * P:(g % 4 + 1) * P],
                                  u_sb[:, g, :, :].rearrange("p l c -> p (l c)"), c["ident"][:])
                if g % 4 == 3:
                    mm.then_inc(turned, 1)

        @block.scalar
        def _(act):
            for s in range(2):
                act.wait_ge(w_in[s], 16)
                act.copy(halves[s][0][:], raw[s][:]).then_inc(high, 1)
            for s in range(2):
                for l in range(PAIRS):
                    act.wait_ge(ready, s * PAIRS + l + 1)
                    act.copy(u_sb[:, s * HALF:(s + 1) * HALF, l, :],
                             bank[l][:, 0:STEP].rearrange("p (g c) -> p g c", c=S5_C)).then_inc(taken, 1)
            for n in range(S5_G // 4):
                act.wait_ge(early_moved, n + 1)
                src = bank_t[n % 4][0:64, :].rearrange("p (g n q) -> p g n q", g=4, q=2)
                act.copy(U[64:128, 4 * n:4 * n + 4, :], src[:, :, :, 1]).then_inc(moved, 1)

        @block.vector
        def _(v):
            for n in range(S5_G // 4):
                v.wait_ge(turned, n + 1)
                src = bank_t[n % 4][0:64, :].rearrange("p (g n q) -> p g n q", g=4, q=2)
                v.tensor_copy(U[0:64, 4 * n:4 * n + 4, :], src[:, :, :, 0]).then_inc(early_moved, 1)


def s5_tables(nc, c, tag, ins, vr, vi, car, cai, step, bb, tmp, shared=None):
    with Tiles(nc, tag, shared) as t:
        raw = {n: t.sb(n, [P, S5_GP]) for n in ("log_dt", "a_re", "a_im")}
        raw3 = {n: t.sb(n, [P, S5_GP, S5_C]) for n in ("b_re", "b_im", "c_re", "c_im")}
        dt, dlr, mag, th, nn, red, half, sin_t, sin_h, cos_t, den, u1, u2, fr, fi = [
            t.sb(n, [P, S5_GP]) for n in ("dt", "dlr", "mag", "th", "nn", "red", "half", "sin_t", "sin_h", "cos_t",
                                          "den", "u1", "u2", "fr", "fi")]
        pr, pi = t.sb("pr", [P, S5_GP, S5_L + 1]), t.sb("pi", [P, S5_GP, S5_L + 1])
        qr, qi = t.sb("qr", [P, S5_GP, S5_L]), t.sb("qi", [P, S5_GP, S5_L])
        t3 = t.sb("t3", [P, S5_GP, S5_C])
        loaded, dve, act_in, act_out = t.sem("loaded"), t.sem("dve"), t.sem("act_in"), t.sem("act_out")
        block = t.block()
        every = {**raw, **raw3}

        @block.sync
        def _(sp):
            for n, tile in every.items():
                sp.dma_start(tile[:], ins[n]).then_inc(loaded, 16)

        @block.scalar
        def _(act):
            act.wait_ge(loaded, 16 * len(every))
            act.activation(dt[:], raw["log_dt"][:], ACT.Exp).then_inc(act_out, 1)
            act.wait_ge(act_in, 1)
            act.activation(mag[:], dlr[:], ACT.Exp).then_inc(act_out, 1)
            act.wait_ge(act_in, 2)
            act.activation(sin_t[:], red[:], ACT.Sin).then_inc(act_out, 1)
            act.activation(sin_h[:], half[:], ACT.Sin).then_inc(act_out, 1)

        @block.vector
        def _(v):
            ch = Chain(v, dve)

            def tt(out, a, b, op):
                ch.link(v.tensor_tensor(out, a, b, op))

            lr, li = raw["a_re"][:], raw["a_im"][:]
            v.wait_ge(loaded, 16 * len(every))
            v.wait_ge(act_out, 1)
            v.tensor_tensor(dlr[:], dt[:], lr, ALU.mult).then_inc(act_in, 1)
            tt(th[:], dt[:], li, ALU.mult)
            rnd = 1.5 * 2 ** 23
            ch.link(v.tensor_scalar(nn[:], th[:], 0.15915494309189535, rnd, ALU.mult, ALU.add))
            ch.link(v.tensor_scalar(nn[:], nn[:], -rnd, None, ALU.add))
            c1 = 6.28125
            c2 = 0.0019350051879882812
            c3 = 2 * np.pi - c1 - c2
            src = th
            for cc in (c1, c2, c3):
                ch.link(v.scalar_tensor_tensor(out=red[:], in0=nn[:], scalar=-float(cc), in1=src[:], op0=ALU.mult,
                                               op1=ALU.add))
                src = red
            ch.link(v.tensor_scalar(red[:], red[:], 3.1415925, -3.1415925, ALU.min, ALU.max))
            v.tensor_scalar(half[:], red[:], 0.5, None, ALU.mult).then_inc(act_in, 1)
            v.wait_ge(act_out, 4)
            tt(cos_t[:], sin_h[:], sin_h[:], ALU.mult)
            ch.link(v.tensor_scalar(cos_t[:], cos_t[:], -2.0, 1.0, ALU.mult, ALU.add))
            ch.put(v.memset(pr[:, :, 0], 1.0))
            ch.put(v.memset(pi[:, :, 0], 0.0))
            ch.put(v.tensor_tensor(pr[:, :, 1], mag[:], cos_t[:], ALU.mult))
            ch.link(v.tensor_tensor(pi[:, :, 1], mag[:], sin_t[:], ALU.mult))
            ar, ai = pr[:, :, 1], pi[:, :, 1]
            for l in range(2, S5_L + 1):
                ch.put(v.tensor_tensor(u1[:], pr[:, :, l - 1], ar, ALU.mult))
                ch.put(v.tensor_tensor(u2[:], pi[:, :, l - 1], ai, ALU.mult))
                ch.put(v.tensor_tensor(fr[:], pr[:, :, l - 1], ai, ALU.mult))
                ch.link(v.tensor_tensor(fi[:], pi[:, :, l - 1], ar, ALU.mult))
                ch.put(v.tensor_tensor(pr[:, :, l], u1[:], u2[:], ALU.subtract))
                ch.link(v.tensor_tensor(pi[:, :, l], fr[:], fi[:], ALU.add))
            tt(u1[:], lr, lr, ALU.mult)
            tt(u2[:], li, li, ALU.mult)
            tt(den[:], u1[:], u2[:], ALU.add)
            ch.link(v.reciprocal(den[:], den[:]))
            ch.link(v.tensor_scalar(nn[:], ar, -1.0, None, ALU.add))
            tt(u1[:], nn[:], lr, ALU.mult)
            tt(u2[:], ai, li, ALU.mult)
            tt(fr[:], u1[:], u2[:], ALU.add)
            tt(fr[:], fr[:], den[:], ALU.mult)
            tt(u1[:], ai, lr, ALU.mult)
            tt(u2[:], nn[:], li, ALU.mult)
            tt(fi[:], u1[:], u2[:], ALU.subtract)
            tt(fi[:], fi[:], den[:], ALU.mult)
            br, bi = raw3["b_re"][:], raw3["b_im"][:]
            frb, fib = bc(fr[:], 2, S5_C), bc(fi[:], 2, S5_C)
            tt(bb[:, 0], frb, br, ALU.mult)
            tt(t3[:], fib, bi, ALU.mult)
            tt(bb[:, 0], bb[:, 0], t3[:], ALU.subtract)
            tt(bb[:, 1], frb, bi, ALU.mult)
            tt(t3[:], fib, br, ALU.mult)
            tt(bb[:, 1], bb[:, 1], t3[:], ALU.add)
            for n, part in enumerate((cos_t, sin_t, mag)):
                ch.put(v.tensor_copy(step[:, n, :], part[:]))
            for l in range(S5_L):
                ch.put(v.tensor_copy(qr[:, :, l], pr[:, :, S5_L - 1 - l]))
                ch.put(v.tensor_copy(qi[:, :, l], pi[:, :, S5_L - 1 - l]))
            v.wait_ge(dve, ch.n)
            sh = [P, S5_GP, S5_L, S5_C]
            qrb, qib = bc(qr[:], 3, S5_C), bc(qi[:], 3, S5_C)
            bbr, bbi = bc(bb[:, 0], 2, S5_L), bc(bb[:, 1], 2, S5_L)
            tl = tmp[:, :, 0:S5_L, :]
            tt(vr[:], qrb, bbr, ALU.mult)
            tt(tl, qib, bbi, ALU.mult)
            tt(vr[:], vr[:], tl, ALU.subtract)
            tt(vi[:], qrb, bbi, ALU.mult)
            tt(tl, qib, bbr, ALU.mult)
            tt(vi[:], vi[:], tl, ALU.add)
            prb, pib = bc(pr[:], 3, S5_C), bc(pi[:], 3, S5_C)
            cr, ci = bc(raw3["c_re"][:], 2, S5_L + 1), bc(raw3["c_im"][:], 2, S5_L + 1)
            tt(car[:], prb, cr, ALU.mult)
            tt(tmp, pib, ci, ALU.mult)
            tt(car[:], car[:], tmp, ALU.subtract)
            tt(cai[:], pib, cr, ALU.mult)
            tt(tmp, prb, ci, ALU.mult)
            tt(cai[:], cai[:], tmp, ALU.add)
            ch.link(v.tensor_scalar(cai[:], cai[:], -1.0, None, ALU.mult))


PARTS_OF_PRODUCT = ((0, 0), (1, 1), (1, 0), (0, 1))


def s5_scan(nc, c, tag, ins, U, vT, car, cai, step, bb, y_sb):
    LC = S5_L * S5_C
    with Tiles(nc, tag) as t:
        toep = t.sb("toep", [P, S5_G, LC])
        prod = t.sb("prod", [P, 4, S5_GP, S5_NC])
        kern = prod[0:S5_C].rearrange("p a g m -> p (a g m)").rearrange("p (g n) -> p g n", n=LC)
        skip, dd = t.sb("skip", [S5_C, S5_G]), t.sb("dd", [S5_C, S5_G, S5_C])
        xs = t.sb("xs", [P, 2, S5_GP, S5_NC])
        st = t.sb("st", [P, 2, S5_GP, S5_NC + 1])
        rot, pw = t.sb("rot", [P, 2, S5_GP, S5_NC]), t.sb("pw", [P, 2, S5_GP, 7])
        rho, decay = t.sb("rho", [P, S5_GP, 1]), t.sb("decay", [P, S5_GP, S5_NC])
        zs = t.sb("zs", [P, 2, S5_GP, S5_NC])
        u1, u2 = t.sb("u1", [P, S5_GP, 1]), t.sb("u2", [P, S5_GP, 1])
        bank = t.banks("b", 8)
        skip_in, k_ready, k_there, toep_in = t.sem("skip_in"), t.sem("k_ready"), t.sem("k_there"), t.sem("toep_in")
        cleared, x_ready, x_there, dve = t.sem("cleared"), t.sem("x_ready"), t.sem("x_there"), t.sem("dve")
        scanned, y_ready = t.sem("scanned"), t.sem("y_ready")
        block = t.block()

        @block.gpsimd
        def _(pool):
            pool.memset(toep[:], 0.0).then_inc(cleared, 1)

        @block.sync
        def _(sp):
            sp.dma_start(skip[:], ins["d_skip"]).then_inc(skip_in, 16)
            sp.wait_ge(cleared, 1)
            sp.wait_ge(k_there, 1)
            for l in range(S5_L):
                sp.dma_start(toep[l * S5_C:(l + 1) * S5_C, :, l * S5_C:LC],
                             kern[:, :, 0:LC - l * S5_C]).then_inc(toep_in, 16)

        @block.tensor
        def _(pe):
            for g in range(S5_G):
                lo, gp = 64 * (g % 2), g // 2
                out = bank[4 * (g % 2) + gp // 4][0:S5_C, (gp % 4) * LC:(gp % 4 + 1) * LC]
                pe.matmul(out, bb[lo:lo + 64, 0, gp, :], car[lo:lo + 64, gp, 0:S5_L, :], start=True, stop=False)
                mm = pe.matmul(out, bb[lo:lo + 64, 1, gp, :], cai[lo:lo + 64, gp, 0:S5_L, :], start=False, stop=True)
            mm.then_inc(k_ready, 1)
            pe.wait_ge(k_there, 1)
            for g in range(S5_G):
                lo, gp = 64 * (g % 2), g // 2
                for ri in range(2):
                    out = bank[2 * ri + gp // 8][lo:lo + 64, (gp % 8) * S5_NC:(gp % 8 + 1) * S5_NC]
                    mm = pe.matmul(out, vT[:, ri, gp, lo:lo + 64], U[:, g, :], start=True, stop=True)
            mm.then_inc(x_ready, 1)
            pe.wait_ge(toep_in, 16 * S5_L)
            pe.wait_ge(scanned, 2)
            for g in range(S5_G):
                lo, gp = 64 * (g % 2), g // 2
                out = bank[4 * (g % 2) + gp // 4][0:S5_NC, (gp % 4) * LC:(gp % 4 + 1) * LC]
                pe.matmul(out, U[:, g, :], toep[:, g, :], start=True, stop=False)
                pe.matmul(out, st[lo:lo + 64, 0, gp, 0:S5_NC], car[lo:lo + 64, gp, 1:S5_L + 1, :], start=False,
                          stop=False)
                mm = pe.matmul(out, st[lo:lo + 64, 1, gp, 0:S5_NC], cai[lo:lo + 64, gp, 1:S5_L + 1, :], start=False,
                               stop=True)
                if g % 8 >= 6:
                    mm.then_inc(y_ready, 1)

        @block.vector
        def _(v):
            ch = Chain(v, dve)
            spare = zs[:].rearrange("p a g m -> p (a g m)").rearrange("p (k g m) -> p k g m", k=4, g=S5_GP)

            def rotate(out, a, b):
                n = a[0].shape[2]
                p = [spare[:, k, :, 0:n] for k in range(4)]
                for k, (i, j) in enumerate(PARTS_OF_PRODUCT):
                    ch.put(v.tensor_tensor(p[k], a[i], b[j], ALU.mult))
                v.wait_ge(dve, ch.n)
                ch.put(v.tensor_tensor(out[0], p[0], p[1], ALU.subtract))
                ch.link(v.tensor_tensor(out[1], p[2], p[3], ALU.add))

            def unit(c_, s_):
                ch.put(v.tensor_tensor(u1[:], c_, c_, ALU.mult))
                ch.link(v.tensor_tensor(u2[:], s_, s_, ALU.mult))
                ch.link(v.tensor_tensor(u1[:], u1[:], u2[:], ALU.add))
                ch.link(v.tensor_scalar(u1[:], u1[:], -0.5, 1.5, ALU.mult, ALU.add))
                ch.put(v.tensor_tensor(c_, c_, u1[:], ALU.mult))
                ch.link(v.tensor_tensor(s_, s_, u1[:], ALU.mult))

            angle = [pw[:, n, :, 0:1] for n in range(2)]
            ch.put(v.tensor_copy(rho[:], step[:, 2, :].unsqueeze(2)))
            for n in range(2):
                ch.put(v.tensor_copy(angle[n], step[:, n, :].unsqueeze(2)))
            v.wait_ge(dve, ch.n)
            unit(*angle)
            for _ in range(3):
                ch.put(v.tensor_tensor(rho[:], rho[:], rho[:], ALU.mult))
                rotate(angle, angle, angle)
                unit(*angle)
            for b in range(6):
                low, high = [[pw[:, n, :, k:k + 1] for n in range(2)] for k in (b, b + 1)]
                rotate(high, low, low)
                unit(*high)
            v.wait_ge(k_ready, 1)
            for b in range(8):
                ch.put(v.tensor_copy(kern[:, 8 * (b % 4) + b // 4:8 * (b % 4) + 8:2, :],
                                     bank[b][0:S5_C, :].rearrange("p (g n) -> p g n", g=4)))
            v.wait_ge(dve, ch.n)
            v.wait_ge(skip_in, 16)
            c.there(v)
            ch.link(v.tensor_tensor(dd[:], bc(c["ident"][0:S5_C, 0:S5_C], 1, S5_G), bc(skip[:], 2, S5_C), ALU.mult))
            v.tensor_tensor(kern[:, :, 0:S5_C], kern[:, :, 0:S5_C], dd[:], ALU.add).then_inc(k_there, 1)
            ch.put(v.memset(st[:], 0.0))
            for n in range(2):
                ch.link(v.tensor_copy(rot[:, n, :, 0:1], angle[n]))
            for b in range(6):
                k = 2 ** b
                rotate([rot[:, n, :, k:2 * k] for n in range(2)], [rot[:, n, :, 0:k] for n in range(2)],
                       [pw[:, n, :, b:b + 1].broadcast_to([P, S5_GP, k]) for n in range(2)])
            ch.link(v.tensor_copy(decay[:], rho[:].broadcast_to([P, S5_GP, S5_NC])))
            ch.put(v.memset(decay[:, :, 0:1], 0.0))
            v.wait_ge(x_ready, 1)
            for ri in range(2):
                for b in range(2):
                    ins = v.tensor_copy(xs[:, ri, 8 * b:8 * b + 8, :],
                                        bank[2 * ri + b][:].rearrange("p (g n) -> p g n", g=8))
                    ins.then_inc(x_there, 1)
            v.wait_ge(x_there, 4)
            v.wait_ge(toep_in, 16 * S5_L)
            turns = [rot[:, n] for n in range(2)]
            for n, (i, j) in enumerate(PARTS_OF_PRODUCT):
                ch.put(v.tensor_tensor(prod[:, n], xs[:, i], turns[j], ALU.mult))
            v.wait_ge(dve, ch.n)
            ch.put(v.tensor_tensor(zs[:, 0], prod[:, 0], prod[:, 1], ALU.add))
            ch.link(v.tensor_tensor(zs[:, 1], prod[:, 2], prod[:, 3], ALU.subtract))
            for n in range(2):
                z = zs[:, n].rearrange("p g m -> p (g m)")
                ch.put(v.tensor_tensor_scan(xs[:, n].rearrange("p g m -> p (g m)"),
                                            decay[:].rearrange("p g m -> p (g m)"), z, 0.0, ALU.mult, ALU.add))
            v.wait_ge(dve, ch.n)
            for n, (i, j) in enumerate(PARTS_OF_PRODUCT):
                ch.put(v.tensor_tensor(prod[:, n], xs[:, i], turns[j], ALU.mult))
            v.wait_ge(dve, ch.n)
            for n, op in enumerate((ALU.subtract, ALU.add)):
                v.tensor_tensor(st[:, n, :, 1:S5_NC + 1], prod[:, 2 * n], prod[:, 2 * n + 1],
                                op).then_inc(scanned, 1)

        @block.scalar
        def _(act):
            y_view = y_sb[:].rearrange("p l (g c) -> p g l c", c=S5_C)
            for n in range(8):
                quad, par = n // 2, n % 2
                act.wait_ge(y_ready, n + 1)
                act.activation(y_view[:, 8 * quad + par:8 * quad + 8:2],
                               bank[4 * par + quad][0:S5_NC, :].rearrange("p (g l c) -> p g l c", g=4, l=S5_L),
                               ACT.Gelu_apprx_tanh)


def glu(nc, c, tag, yT, w, b, oT, shared=None):
    K = WIDTH_B // P
    with Tiles(nc, tag, shared) as t:
        wb, bias, sg = t.sb("w", [P, K, WIDTH_B]), t.sb("bias", [P, K]), t.sb("sg", [P, K, SEQ])
        gated, high = t.sem("gated"), t.sem("high")
        bank = t.banks("z", K)
        loaded, z_ready, sg_ready = t.sem("loaded"), t.sem("z_ready"), t.sem("sg_ready")
        block = t.block()

        @block.sync
        def _(sp):
            sp.dma_start(wb[:], w.rearrange("(k p) n -> p k n", p=P)).then_inc(loaded, 16)
            sp.dma_start(bias[:], b).then_inc(loaded, 16)

        @block.tensor
        def _(pe):
            pe.wait_ge(loaded, 32)
            for f in range(K):
                for k in range(K):
                    mm = pe.matmul(bank[f][:], wb[:, k, f * P:(f + 1) * P], yT[:, k, :], start=k == 0, stop=k == K - 1)
                mm.then_inc(z_ready, 1)

        @block.scalar
        def _(act):
            act.wait_ge(loaded, 32)
            for f in range(K):
                act.wait_ge(z_ready, f + 1)
                act.activation(sg[:, f, :], bank[f][:], ACT.Sigmoid, bias=bias[:, f:f + 1]).then_inc(sg_ready, 1)
            for f in range(K):
                act.wait_ge(gated, f + 1)
                act.copy(oT[0][:, f, :], sg[:, f, :]).then_inc(high, 1)

        @block.gpsimd
        def _(pool):
            for f in range(K):
                pool.wait_ge(sg_ready, f + 1)
                pool.tensor_tensor(sg[:, f, :], yT[:, f, :], sg[:, f, :], ALU.mult).then_inc(gated, 1)
            for f in range(K):
                pool.wait_ge(high, f + 1)
                pool.tensor_tensor(oT[1][:, f, :], sg[:, f, :], oT[0][:, f, :].bitcast(F32), ALU.subtract)


def halves(t, name, shape):
    return [t.sb(f"{name}{half}", shape, F32R) for half in "hl"]


def layer0_mixer(nc, c, x, a):
    with Tiles(nc, "l0in") as inner:
        qkv = inner.sb("qkv", [P, NT, L0_WIDTH])
        U, iw = inner.sb("U", [P, S5_G, S5_NC]), inner.sb("iw", [P, NT, 8])
        hT = oT = halves(inner, "hT", [P, KD, SEQ])

        def cols(name, heads=None):
            o, n = L0_COLS[name]
            v = qkv[:, :, o:o + n]
            return v.rearrange("p t (h d) -> p t h d", h=heads) if heads else v

        with Tiles(nc, "l0s") as t:
            car, cai = [t.sb(n, [P, S5_GP, S5_L + 1, S5_C]) for n in ("car", "cai")]
            step, bb = t.sb("step", [P, 3, S5_GP]), t.sb("bb", [P, 2, S5_GP, S5_C])
            vT = t.sb("vT", [P, 2, S5_GP, P])
            with Tiles(nc, "l0v") as tv:
                vr, vi = [tv.sb(n, [P, S5_GP, S5_L, S5_C]) for n in ("vr", "vi")]
                normed_transpose(nc, c, "n0", x, a["l0_mix_norm"], hT)
                tmp = vT[:].rearrange("p r g n -> p (r g n)")[:, 0:S5_GP * (S5_L + 1) * S5_C]\
                    .rearrange("p (g l c) -> p g l c", g=S5_GP, c=S5_C)
                with Tiles(nc, "l0p") as both:
                    both.block()
                    s5_tables(nc, c, "st", a, vr, vi, car, cai, step, bb, tmp, shared=both)
                    project(nc, c, "p0", hT, a["l0_w_in"][:, 0:L0_WIDTH], L0_WIDTH, L0_WIDTH // 4, qkv, shared=both)
                with Tiles(nc, "l0q") as both:
                    both.block()
                    prepare_heads(nc, c, "ph", [(cols("k", 2), a["l0_a_k_gain"]), (cols("q", 8), a["l0_a_q_gain"]),
                                                (cols("iq", 8), None), (cols("ik", 1), None)],
                                  c["cos"][:], c["sin"][:], shared=both)
                    scale_small(nc, c, "iw", iw, cols("iw"), 8 ** -0.5, shared=both)
                    s5_inputs(nc, c, "u0", hT, a["l0_w_in"], U, shared=both)
                turn(nc, c, "tu", [(vT[:, ri, 4 * b:4 * b + 4, :].rearrange("p g n -> p (g n)"),
                                    [s[:, gp, :, :].rearrange("p l c -> p (l c)") for gp in range(4 * b, 4 * b + 4)], P)
                                   for ri, s in enumerate((vr, vi)) for b in range(4)])
            y_sb = t.sb("y", [S5_NC, S5_L, WIDTH_B])
            s5_scan(nc, c, "sc", a, U, vT, car, cai, step, bb, y_sb)
            yT = U[:].rearrange("p g n -> p (g n)").rearrange("p (f t) -> p f t", t=SEQ)
            turn(nc, c, "ty", [(yT[:, f, :].rearrange("p (n l) -> p l n", l=S5_L),
                                [y_sb[:, l, f * P:(f + 1) * P] for l in range(S5_L)], P) for f in range(4)])

        with Tiles(nc, "l0a") as t:
            qT, kT, ikT = t.sb("qT", [P, NH, SEQ]), t.sb("kT", [P, 2, SEQ]), t.sb("ikT", [P, SEQ])
            score, bias = t.sb("score", [P, NT, SEQ]), t.sb("bias", [P, NT, SEQ])
            o_a = t.sb("o", [P, NT, SEQ])
            q, k, ik = cols("q"), cols("k"), cols("ik")
            turn(nc, c, "tk", [(kT[0:HD, g, :], [k[:, m, g * HD:(g + 1) * HD] for m in range(NT)], HD)
                               for g in range(2)] + [(ikT[0:HD, :], [ik[:, m, :] for m in range(NT)], HD)] +
                 [(qT[0:HD, h, :], [q[:, m, h * HD:(h + 1) * HD] for m in range(NT)], HD) for h in range(NH)],
                 zero=[kT[HD:P], ikT[HD:P], qT[HD:P]])
            index_scores(nc, c, "ix", cols("iq"), iw, ikT, score)
            with Tiles(nc, "l0e") as both:
                both.block()
                select_keys(nc, c, "se", score, bias, shared=both)
                glu(nc, c, "gl", yT, a["l0_s5_w_glu"], a["b_glu"], [o[:, 4:8, :] for o in oT], shared=both)
            attention(nc, c, "at", qT, kT, cols("v"), bias, o_a)
            turn(nc, c, "to", [(tuple(o[:, f, :] for o in oT), [o_a[:, m, f * P:(f + 1) * P] for m in range(NT)], P)
                               for f in range(4)])
        project(nc, c, "po", oT, a["l0_w_out"], D, D // 4, x, add=True)


def scale_small(nc, c, tag, out, src, by, shared=None):
    with Tiles(nc, tag, shared) as t:
        block = t.block()

        @block.vector
        def _(v):
            v.tensor_scalar(out[:], src, by, None, ALU.mult)


def compress(nc, c, tag, cols, a, kcT, vc, beside):
    NB, L = 32, CMP_LEN
    with Tiles(nc, tag) as t:
        posT = t.sb("posT", [HD, L])
        flat = [t.sb(f"flat{n}", [HD, 2, SEQ]) for n in range(2)]
        blk = [t.sb(f"blk{n}", [HD, L, 2, NB]) for n in range(2)]
        w1 = [t.sb(f"w1{b}", [HD, L, P]) for b in range(2)]
        w2 = [t.sb(f"w2{n}", [P, CMP_HID // P, HD]) for n in range(2)]
        hid = t.sb("hid", [P, 2, 2, 2 * NB])
        kc = t.sb("kc", [2 * NB, 1, 1, HD])
        srcs = [cols(n) for n in ("kc", "vc")]
        turn(nc, c, tag + "t", [(flat[n][:, g, :], [srcs[n][:, m, g * HD:(g + 1) * HD] for m in range(NT)], HD)
                                for n in range(2) for g in range(2)])
        with Tiles(nc, tag + "h") as t2:
            bank = t2.banks("h", 4)
            bank_v, bank_k = t2.banks("v", 2), t2.banks("k")[0]
            small_in, w1_in, cleared, blocks = t2.sem("small_in"), t2.sems("w1_in", 2), t2.sem("cleared"), t2.sem("blocks")
            h_ready, h_there, o_ready = t2.sem("h_ready"), t2.sem("h_there"), t2.sem("o_ready")
            block = t2.block()
            beside(t2)

            @block.sync
            def _(sp):
                sp.dma_start(posT[:], a["l1_nsa_cmp_pos"]).then_inc(small_in, 16)
                for n, name in enumerate(("l1_nsa_k_w2", "l1_nsa_v_w2")):
                    sp.dma_start(w2[n][:], a[name].rearrange("(m p) d -> p m d", p=P)).then_inc(small_in, 16)
                for n, name in enumerate(("l1_nsa_k_w1", "l1_nsa_v_w1")):
                    for m in range(2):
                        if n:
                            sp.wait_ge(h_ready, m + 1)
                        sp.dma_start(w1[m][:], a[name].rearrange("(l d) h -> d l h", d=HD)[:, :, m * P:(m + 1) * P])\
                          .then_inc(w1_in[m], 16)

            @block.gpsimd
            def _(pool):
                for n in range(2):
                    pool.memset(blk[n][:], 0.0).then_inc(cleared, 1)
                pool.wait_ge(cleared, 2)
                pool.wait_ge(small_in, 48)
                for n in range(2):
                    for g in range(2):
                        for half in range(L // CMP_STRIDE):
                            lo = half * CMP_STRIDE
                            win = flat[n][:, g, lo:lo + NCMP * CMP_STRIDE].rearrange("p (n l) -> p l n", l=CMP_STRIDE)
                            pool.tensor_tensor(blk[n][:, lo:lo + CMP_STRIDE, g, 0:NCMP], win,
                                            bc(posT[:, lo:lo + CMP_STRIDE], 2, NCMP), ALU.add).then_inc(blocks, 1)

            @block.tensor
            def _(pe):
                for n in range(2):
                    pe.wait_ge(blocks, 4 * (n + 1))
                    for m in range(2):
                        pe.wait_ge(w1_in[m], 16 * (n + 1))
                        for l in range(L):
                            mm = pe.matmul(bank[2 * n + m][:, 0:2 * NB], w1[m][:, l, :],
                                           blk[n][:, l, :, :].rearrange("p g n -> p (g n)"), start=l == 0,
                                           stop=l == L - 1)
                        mm.then_inc(h_ready, 1)
                pe.wait_ge(h_there, 4)
                for m in range(2):
                    mm = pe.matmul(bank_k[0:2 * NB, 0:HD], hid[:, 0, m, :], w2[0][:, m, :], start=m == 0, stop=m == 1)
                mm.then_inc(o_ready, 1)
                for g in range(2):
                    for m in range(2):
                        mm = pe.matmul(bank_v[g][0:NB, 0:HD], hid[:, 1, m, g * NB:(g + 1) * NB], w2[1][:, m, :],
                                       start=m == 0, stop=m == 1)
                    mm.then_inc(o_ready, 1)

            @block.scalar
            def _(act):
                for n in range(2):
                    for m in range(2):
                        act.wait_ge(h_ready, 2 * n + m + 1)
                        act.activation(hid[:, n, m, :], bank[2 * n + m][:, 0:2 * NB],
                                       ACT.Gelu_apprx_tanh).then_inc(h_there, 1)
                act.wait_ge(o_ready, 3)
                act.copy(kc[:, 0, 0, :], bank_k[0:2 * NB, 0:HD])
                for g in range(2):
                    act.copy(vc[:, g, :], bank_v[g][0:NB, 0:HD])

        prepare_heads(nc, c, tag + "p", [(kc[:], a["l1_c_k_gain"])], c["ccos"][:], c["csin"][:])
        turn(nc, c, tag + "u", [(kcT[0:HD].rearrange("p g n -> p (g n)"), [kc[:, 0, 0, :]], HD)], zero=[kcT[HD:P]])


def compressed_attention(nc, c, tag, qT, kcT, vc, out, gate):
    NB, SAME = 32, NH // 2
    with Tiles(nc, tag) as t:
        sm = [t.sb(f"sm{g}", [P, NT, SAME, NB]) for g in range(2)]
        pT = [t.sb(f"pT{g}", [P, SEQ]) for g in range(2)]
        vals = t.sb("vals", [P, 2, SAME * HD])
        mx, den = [[t.sb(f"{n}{g}", [P, NT, SAME, 1]) for g in range(2)] for n in ("mx", "den")]
        bank_s, bank_t, bank_o = t.banks("s", 2), t.banks("t", 2), t.banks("o", 4)
        cleared, placed, s_ready, m_ready, e_there, p_ready, t_ready, pT_there, o_ready, dve = [
            t.sem(n) for n in ("cleared", "placed", "s_ready", "m_ready", "e_there", "p_ready", "t_ready", "pT_there",
                               "o_ready", "dve")]
        block = t.block()

        @block.gpsimd
        def _(pool):
            pool.memset(vals[:], 0.0).then_inc(cleared, 1)

        @block.tensor
        def _(pe):
            c.there(pe)
            for g in range(2):
                for m in range(NT):
                    for r in range(SAME):
                        at = (m * SAME + r) * NB
                        mm = pe.matmul(bank_s[g][:, at:at + NB], qT[:, g * SAME + r, m * P:(m + 1) * P],
                                       kcT[:, g, :], start=True, stop=True)
                mm.then_inc(s_ready, 1)
            for g in range(2):
                pe.wait_ge(p_ready, g + 1)
                for m in range(NT):
                    mm = pe.transpose(bank_t[g][:, m * P:(m + 1) * P], sm[g][:, m, :, :].rearrange("p r n -> p (r n)"),
                                      c["ident"][:])
                mm.then_inc(t_ready, 1)
            pe.wait_ge(placed, 2 * SAME)
            for g in range(2):
                pe.wait_ge(pT_there, g + 1)
                for m in range(NT):
                    mm = pe.matmul(bank_o[2 * g + m // 2][:, m % 2 * SAME * HD:(m % 2 + 1) * SAME * HD],
                                   pT[g][:, m * P:(m + 1) * P], vals[:, g, :], start=True, stop=True)
                    if m % 2:
                        mm.then_inc(o_ready, 1)

        @block.scalar
        def _(act):
            act.wait_ge(cleared, 1)
            for g in range(2):
                for r in range(SAME):
                    act.copy(vals[r * NB:(r + 1) * NB, g, r * HD:(r + 1) * HD], vc[:, g, :]).then_inc(placed, 1)
            for g in range(2):
                act.wait_ge(m_ready, g + 1)
                act.activation(sm[g][:], sm[g][:], ACT.Exp).then_inc(e_there, 1)
            for g in range(2):
                act.wait_ge(t_ready, g + 1)
                act.copy(pT[g][:], bank_t[g][:]).then_inc(pT_there, 1)

        @block.vector
        def _(v):
            ch = Chain(v, dve)
            c.there(v)
            full = [P, NT, SAME, NB]
            for g in range(2):
                v.wait_ge(s_ready, g + 1)
                ch.link(v.tensor_scalar(sm[g][:].rearrange("p m r n -> p (m r n)"), bank_s[g][:], HD ** -0.5, None,
                                        ALU.mult))
                ch.link(v.tensor_tensor(sm[g][:], sm[g][:], bc(c["cbias"][:], 2, SAME), ALU.add))
                ch.link(v.tensor_reduce(mx[g][:].rearrange("p m r o -> p m (r o)"), sm[g][:], AX.X, ALU.max))
                v.tensor_tensor(sm[g][:], sm[g][:], mx[g][:].broadcast_to(full), ALU.subtract).then_inc(m_ready, 1)
            for g in range(2):
                v.wait_ge(e_there, g + 1)
                v.tensor_tensor(sm[g][:], sm[g][:], bc(c["cmask"][:], 2, SAME), ALU.mult).then_inc(p_ready, 1)
                v.wait_ge(p_ready, g + 1)
                ch.link(v.tensor_reduce(den[g][:].rearrange("p m r o -> p m (r o)"), sm[g][:], AX.X, ALU.add))
                ch.link(v.tensor_scalar(den[g][:], den[g][:], 1e-30, None, ALU.max))
                ch.link(v.reciprocal(den[g][:], den[g][:]))
                ch.link(v.tensor_tensor(den[g][:], den[g][:], gate[:, :, g * SAME:(g + 1) * SAME].unsqueeze(3),
                                        ALU.mult))
            for g in range(2):
                for b in range(2):
                    v.wait_ge(o_ready, g * 2 + b + 1)
                    v.tensor_tensor(out[:, 2 * b:2 * b + 2, g * SAME * HD:(g + 1) * SAME * HD]
                                    .rearrange("p m (r d) -> p m r d", d=HD),
                                    bank_o[2 * g + b][:].rearrange("p (m r d) -> p m r d", m=2, d=HD),
                                    den[g][:, 2 * b:2 * b + 2].broadcast_to([P, 2, SAME, HD]), ALU.mult)


def gla_decays(nc, c, tag, cols, a, qd, ki, kd, dec, la):
    W = GLA_H * GLA_K
    with Tiles(nc, tag) as t:
        lowT, wg, bg = t.sb("lowT", [16, SEQ]), t.sb("wg", [16, W]), t.sb("bg", [P, W])
        lg, e1 = t.sb("lg", [P, NT, W]), t.sb("e1", [P, NT, W])
        bank = t.banks("b", 8)
        loaded, turned, low_there, l_ready, lg_ready = [
            t.sem(n) for n in ("loaded", "turned", "low_there", "l_ready", "lg_ready")]
        e_there, la_ready, s_ready, x_there, dve = [
            t.sem(n) for n in ("e_there", "la_ready", "s_ready", "x_there", "dve")]
        block = t.block()
        low, gq, gk = cols("glow"), cols("gq"), cols("gk")

        @block.sync
        def _(sp):
            sp.dma_start(wg[:], a["l1_gla_w_gate"]).then_inc(loaded, 16)
            sp.dma_start(bg[:], a["l1_gla_b_gate"].partition_broadcast(P)).then_inc(loaded, 16)

        @block.tensor
        def _(pe):
            c.there(pe)
            for m in range(NT):
                mm = pe.transpose(bank[0][0:16, m * P:(m + 1) * P], low[:, m, :], c["ident"][:])
            mm.then_inc(turned, 1)
            pe.wait_ge(loaded, 32)
            pe.wait_ge(low_there, 1)
            for m in range(NT):
                pe.matmul(bank[1 + m][:, 0:W], lowT[:, m * P:(m + 1) * P], wg[:], start=True,
                          stop=True).then_inc(l_ready, 1)
            pe.wait_ge(la_ready, NT)
            for h in range(GLA_H):
                for m in range(NT):
                    mm = pe.matmul(bank[0][0:GLA_K, (h * NT + m) * 4:(h * NT + m + 1) * 4],
                                   la[:, m, h * GLA_K:(h + 1) * GLA_K], c["chunk"][:], start=True, stop=True)
            mm.then_inc(s_ready, 1)
            for m in range(NT):
                pe.matmul(bank[1 + m][:, 0:W], c["upto"][:], la[:, m, :], start=True, stop=True)
                pe.matmul(bank[1 + m][:, W:2 * W], c["after"][:], la[:, m, :], start=True,
                          stop=True).then_inc(s_ready, 1)

        @block.scalar
        def _(act):
            act.wait_ge(turned, 1)
            act.copy(lowT[:], bank[0][0:16, :]).then_inc(low_there, 1)
            act.wait_ge(lg_ready, NT)
            act.activation(e1[:], lg[:], ACT.Abs).then_inc(e_there, 1)
            act.wait_ge(e_there, 1)
            act.activation(e1[:], e1[:], ACT.Exp, scale=-1.0).then_inc(e_there, 1)
            act.wait_ge(e_there, 2)
            act.activation(e1[:], e1[:], ACT.Ln, bias=1.0).then_inc(e_there, 1)
            act.wait_ge(s_ready, 1)
            act.activation(dec[:].rearrange("p h n -> p (h n)"), bank[0][0:GLA_K, 0:GLA_H * GLA_N], ACT.Exp)
            for m in range(NT):
                act.wait_ge(s_ready, m + 2)
                act.activation(qd[:, m, :], bank[1 + m][:, 0:W], ACT.Exp).then_inc(x_there, 1)
                act.activation(ki[:, m, :], bank[1 + m][:, 0:W], ACT.Exp, scale=-1.0).then_inc(x_there, 1)
                act.activation(kd[:, m, :], bank[1 + m][:, W:2 * W], ACT.Exp).then_inc(x_there, 1)

        @block.vector
        def _(v):
            ch = Chain(v, dve)
            v.wait_ge(loaded, 32)
            for m in range(NT):
                v.wait_ge(l_ready, m + 1)
                v.tensor_tensor(lg[:, m, :], bank[1 + m][:, 0:W], bg[:], ALU.add).then_inc(lg_ready, 1)
            v.wait_ge(e_there, 3)
            ch.link(v.scalar_tensor_tensor(out=lg[:], in0=lg[:], scalar=0.0, in1=e1[:], op0=ALU.min, op1=ALU.subtract))
            for m in range(NT):
                v.tensor_scalar(la[:, m, :], lg[:, m, :], 1.0 / 16.0, None, ALU.mult).then_inc(la_ready, 1)
            for m in range(NT):
                v.wait_ge(x_there, 3 * m + 3)
                v.scalar_tensor_tensor(out=qd[:, m, :], in0=gq[:, m, :], scalar=GLA_K ** -0.5, in1=qd[:, m, :],
                                       op0=ALU.mult, op1=ALU.mult)
                v.tensor_tensor(ki[:, m, :], gk[:, m, :], ki[:, m, :], ALU.mult)
                v.tensor_tensor(kd[:, m, :], gk[:, m, :], kd[:, m, :], ALU.mult)


def gla_mix(nc, c, tag, gv, qdT, kiT, kd, dec, o):
    C4 = P // GLA_C
    with Tiles(nc, tag) as t:
        att = t.sb("att", [P, NT, GLA_H, P])
        state = t.sb("state", [GLA_K, GLA_N + 1, GLA_H, GLA_V])
        bank_a, bank_u, bank_o = t.banks("a", 2), t.banks("u", 4), t.banks("o", 2)
        cleared, a_ready, a_there, u_ready, u_there, o_ready, o_taken, dve = [
            t.sem(n) for n in ("cleared", "a_ready", "a_there", "u_ready", "u_there", "o_ready", "o_taken", "dve")]
        block = t.block()

        @block.gpsimd
        def _(pool):
            pool.memset(att[:], 0.0).then_inc(cleared, 1)
            pool.memset(state[:, 0], 0.0).then_inc(cleared, 1)

        @block.tensor
        def _(pe):
            for m in range(NT):
                if m >= 2:
                    pe.wait_ge(a_there, m - 1)
                for h in range(GLA_H):
                    mm = pe.matmul(bank_a[m % 2][:, h * P:(h + 1) * P], kiT[:, h, m * P:(m + 1) * P],
                                   qdT[:, h, m * P:(m + 1) * P], start=True, stop=True)
                mm.then_inc(a_ready, 1)
                for n in range(C4):
                    lo = n * GLA_C
                    if m:
                        pe.wait_ge(u_there, (m - 1) * C4 + n + 1)
                    for h in range(GLA_H):
                        mm = pe.matmul(bank_u[n][0:GLA_K, h * GLA_V:(h + 1) * GLA_V],
                                       kd[lo:lo + GLA_C, m, h * GLA_K:(h + 1) * GLA_K],
                                       gv[lo:lo + GLA_C, m, h * GLA_V:(h + 1) * GLA_V], start=True, stop=True)
                    mm.then_inc(u_ready, 1)
            for m in range(NT):
                pe.wait_ge(a_there, m + 1)
                pe.wait_ge(u_there, (m + 1) * C4)
                if m >= 2:
                    pe.wait_ge(o_taken, m - 1)
                for h in range(GLA_H):
                    out = bank_o[m % 2][:, h * GLA_V:(h + 1) * GLA_V]
                    pe.matmul(out, att[:, m, h, :], gv[:, m, h * GLA_V:(h + 1) * GLA_V], start=True, stop=False,
                              skip_group_check=True)
                    for n in range(C4):
                        lo = n * GLA_C
                        mm = pe.matmul(out[lo:lo + GLA_C], qdT[:, h, m * P + lo:m * P + lo + GLA_C],
                                       state[:, m * C4 + n, h, :], start=False, stop=True, skip_group_check=True)
                mm.then_inc(o_ready, 1)

        @block.vector
        def _(v):
            ch = Chain(v, dve)
            c.there(v)
            v.wait_ge(cleared, 2)
            for m in range(NT):
                v.wait_ge(a_ready, m + 1)
                for h in range(GLA_H):
                    ins = v.copy_predicated(att[:, m, h, :], c["upto"][:].bitcast(U32), bank_a[m % 2][:, h * P:(h + 1) * P])
                ins.then_inc(a_there, 1)
                for n in range(C4):
                    at = m * C4 + n
                    v.wait_ge(u_ready, at + 1)
                    for h in range(GLA_H):
                        ins = v.scalar_tensor_tensor(out=state[:, at + 1, h, :], in0=state[:, at, h, :],
                                                     scalar=dec[:, h, at:at + 1],
                                                     in1=bank_u[n][0:GLA_K, h * GLA_V:(h + 1) * GLA_V],
                                                     op0=ALU.mult, op1=ALU.add)
                    ins.then_inc(u_there, 1)
                    v.wait_ge(u_there, at + 1)

        @block.scalar
        def _(act):
            for m in range(NT):
                act.wait_ge(o_ready, m + 1)
                act.copy(o[:, m, :], bank_o[m % 2][:]).then_inc(o_taken, 1)


def gla_gate(nc, c, tag, o, gr, gain, shared=None):
    with Tiles(nc, tag, shared) as t:
        sq, sg, gb = t.sb("sq", [P, NT, GLA_H, GLA_V]), t.sb("sg", [P, NT, SEQ]), t.sb("gain", [P, GLA_V])
        ms, root, r = [t.sb(n, [P, NT, GLA_H]) for n in ("ms", "root", "r")]
        gain_in, ms_ready, root_ready, sg_ready, dve = [
            t.sem(n) for n in ("gain_in", "ms_ready", "root_ready", "sg_ready", "dve")]
        block = t.block()
        o4 = o[:].rearrange("p m (h e) -> p m h e", h=GLA_H)
        full = [P, NT, GLA_H, GLA_V]

        @block.sync
        def _(sp):
            sp.dma_start(gb[:], gain.partition_broadcast(P)).then_inc(gain_in, 16)

        @block.scalar
        def _(act):
            act.activation(sg[:], gr, ACT.Sigmoid).then_inc(sg_ready, 1)
            act.wait_ge(ms_ready, 1)
            act.activation(root[:], ms[:], ACT.Sqrt).then_inc(root_ready, 1)

        @block.vector
        def _(v):
            ch = Chain(v, dve)
            ch.link(v.tensor_tensor(sq[:], o4, o4, ALU.mult))
            ch.link(v.tensor_reduce(ms[:], sq[:], AX.X, ALU.add))
            v.tensor_scalar(ms[:], ms[:], 1.0 / GLA_V, EPS, ALU.mult, ALU.add).then_inc(ms_ready, 1)
            rstd_steps(v, ch, ms[:], root[:], r[:], root_ready, 1)
            ch.link(v.tensor_tensor(o4, o4, r[:].unsqueeze(3).broadcast_to(full), ALU.mult))
            v.wait_ge(gain_in, 16)
            ch.link(v.tensor_tensor(o4, o4, gb[:].unsqueeze(1).unsqueeze(1).broadcast_to(full), ALU.mult))
            v.wait_ge(sg_ready, 1)
            ch.link(v.tensor_tensor(sg[:], sg[:], gr, ALU.mult))
            ch.link(v.tensor_tensor(o[:], o[:], sg[:], ALU.mult))


def sigmoid_gates(nc, c, tag, gates, src, shared=None):
    with Tiles(nc, tag, shared) as t:
        block = t.block()

        @block.scalar
        def _(act):
            act.activation(gates[:], src.rearrange("p m (h b) -> p m b h", b=3), ACT.Sigmoid)


def layer1_mixer(nc, c, x, a):
    with Tiles(nc, "l1in") as inner:
        qkv = inner.sb("qkv", [P, NT, L1_WIDTH])
        with Tiles(nc, "l1h") as t:
            hT = halves(t, "hT", [P, KD, SEQ])
            normed_transpose(nc, c, "n1", x, a["l1_mix_norm"], hT)
            project(nc, c, "p1", hT, a["l1_w_in"], L1_WIDTH, L1_WIDTH // 6, qkv)
        oT, o_d = halves(inner, "oT", [P, KD, SEQ]), inner.sb("o_d", [P, NT, SEQ])

        def cols(name, heads=None):
            o, n = L1_COLS[name]
            v = qkv[:, :, o:o + n]
            return v.rearrange("p t (h d) -> p t h d", h=heads) if heads else v

        with Tiles(nc, "l1g") as t:
            kd, dec = t.sb("kd", [P, NT, 256]), t.sb("dec", [GLA_K, GLA_H, GLA_N])
            qdT, kiT = [t.sb(n, [GLA_K, GLA_H, SEQ]) for n in ("qdT", "kiT")]
            with Tiles(nc, "l1gd") as t2:
                qd, ki, la = [t2.sb(n, [P, NT, 256]) for n in ("qd", "ki", "la")]
                gla_decays(nc, c, "gd", cols, a, qd, ki, kd, dec, la)
                turn(nc, c, "gt", [(d[:, h, :], [s[:, m, h * GLA_K:(h + 1) * GLA_K] for m in range(NT)], GLA_K)
                                   for d, s in ((qdT, qd), (kiT, ki)) for h in range(GLA_H)])
            gla_mix(nc, c, "gm", cols("gv"), qdT, kiT, kd, dec, o_d)

        with Tiles(nc, "l1a") as t:
            kcT, vc = t.sb("kcT", [P, 2, 32]), t.sb("vc", [32, 2, HD])
            gates, bias = t.sb("gates", [P, NT, 3, NH]), t.sb("bias", [P, NT, SEQ])

            def beside(shared):
                prepare_heads(nc, c, "pq", [(cols("q", 8), a["l1_c_q_gain"]), (cols("ks", 2), a["l1_c_k_gain"]),
                                            (cols("kw", 2), a["l1_c_k_gain"])], c["cos"][:], c["sin"][:],
                              shared=shared)
                gla_gate(nc, c, "gg", o_d, cols("gr"), a["l1_gla_o_gain"], shared=shared)
                sigmoid_gates(nc, c, "sg", gates, cols("gl"), shared=shared)
                causal_bias(nc, c, "cb", bias, shared=shared)

            compress(nc, c, "cm", cols, a, kcT, vc, beside)
            turn(nc, c, "go", [(tuple(o[:, 4 + f, :] for o in oT), [o_d[:, m, f * P:(f + 1) * P] for m in range(NT)], P)
                               for f in range(4)])
            kT, qT, q = [t.sb(f"kT{n}", [P, 2, SEQ]) for n in range(2)], t.sb("qT", [P, NH, SEQ]), cols("q")
            o_c = t.sb("o", [P, NT, SEQ])
            ks = [cols("ks"), cols("kw")]
            turn(nc, c, "tk1", [(kT[n][0:HD, g, :], [ks[n][:, m, g * HD:(g + 1) * HD] for m in range(NT)], HD)
                                for n in range(2) for g in range(2)] +
                 [(qT[0:HD, h, :], [q[:, m, h * HD:(h + 1) * HD] for m in range(NT)], HD) for h in range(NH)],
                 zero=[k[HD:P] for k in kT] + [qT[HD:P]])
            compressed_attention(nc, c, "ca", qT, kcT, vc, o_c, gates[:, :, 0, :])
            attention(nc, c, "as", qT, kT[0], cols("vs"), bias, o_c, gate=gates[:, :, 1, :], add=True)
            attention(nc, c, "aw", qT, kT[1], cols("vw"), bias, o_c, gate=gates[:, :, 2, :], add=True)
            turn(nc, c, "to1", [(tuple(o[:, f, :] for o in oT), [o_c[:, m, f * P:(f + 1) * P] for m in range(NT)], P)
                                for f in range(4)])
        project(nc, c, "po1", oT, a["l1_w_out"], D, D // 4, x, add=True)


def retrieve(nc, c, tag, xs, wq, subkeysT, gates, rows, cols, uT, hmat):
    with Tiles(nc, tag) as t:
        raw = [t.sb(f"raw{s}", [P, KD, P]) for s in range(2)]
        wb = [halves(t, f"wq{s}", [P, KD, P]) for s in range(2)]
        keys = t.sb("keys", [P, NLIST, PEER_K])
        qT = [t.sb(f"qT{s}", [P, SEQ]) for s in range(2)]
        T = PEER_TOP
        val = [t.sb(f"val{s}", [P, NT, T]) for s in range(2)]
        idx = [t.sb(f"idx{s}", [P, NT, T], U32) for s in range(2)]
        idf = [t.sb(f"idf{s}", [P, NT, T]) for s in range(2)]
        work = t.sb("work", [P, NT, P])
        cand, rest = t.sb("cand", [P, NT, T * T]), t.sb("rest", [P, NT, T * T])
        top, pos = t.sb("top", [P, NT, T]), t.sb("pos", [P, NT, T], U32)
        place = [t.sb(f"place{s}", [P, NT, T], U32) for s in range(2)]
        placef = [t.sb(f"placef{s}", [P, NT, T]) for s in range(2)]
        onehot = t.sb("onehot", [P, NT, T, T])
        peak = t.sb("peak", [P, NT, PEER_H, 1])
        wait_taker = t.sb("wait_taker", [P, 1])
        u_raw, hid = [[t.sb(f"{n}{b}", [P, w]) for b in range(2)] for n, w in (("u", D), ("hid", SEQ))]
        u_half = [halves(t, f"uh{b}", [P, D]) for b in range(2)]
        bank_q, bank_s, bank_h = t.banks("q", 2), t.banks("s", 2), t.banks("h", 2)
        keys_in, wq_in = t.sem("keys_in"), t.sems("wq_in", 2)
        high, low = t.sems("high", 2), t.leads("low", 2)
        q_ready, q_there = t.leads("q_ready", 2), t.leads("q_there", 2)
        s_ready, s_taken = t.leads("s_ready", 2), t.leads("s_taken", 2)
        dve, e_ready, e_there = t.sem("dve"), t.sem("e_ready"), t.sem("e_there")
        u_in, u_high = t.sems("u_in", 2), t.sems("u_high", 2)
        u_low, h_done, h_taken, h_stored = [t.leads(n, 2) for n in ("u_low", "h_done", "h_taken", "h_stored")]
        block = t.block()
        wq_view = wq.rearrange("(k p) n -> p k n", p=P)

        def trips(eng, head, first=lambda: None):
            first()
            with eng.Fori(0, PEER_H - 1) as h:
                head(h, True)
            head(PEER_H - 1, False)

        def used(h, q):
            return h * 2 + q // 2

        @block.sync
        def _(sp):
            def columns(h):
                for s in range(2):
                    sp.wait_ge(low[s], LEAD + h)
                    sp.dma_start(raw[s][:], wq_view[:, :, ds((h * 2 + s) * P, P)]).then_inc(wq_in[s], 16)

            def head(h, more):
                for q in range(4):
                    if q == 2 and more:
                        columns(h + 1)
                    sp.wait_ge(u_low[q % 2], LEAD + used(h, q))
                    sp.dma_start(u_raw[q % 2][:], uT[ds(h * 8 + 2 * q + 1, 1)].rearrange("o a d -> a (o d)"))\
                      .then_inc(u_in[q % 2], 16)

            sp.dma_start(keys[:], subkeysT).then_inc(keys_in, 16)
            trips(sp, head, lambda: columns(0))

        @block.tensor
        def _(pe):
            pe.wait_ge(keys_in, 16)
            with pe.Fori(0, PEER_H) as h:
                for s in range(2):
                    pe.wait_ge(low[s], LEAD + h + 1)
                    pe.wait_ge(q_there[s], LEAD + h)
                    for k in range(KD):
                        mm = passes(pe, bank_q[s][:], [w[:, k, :] for w in wb[s]], [m[:, k, :] for m in xs], k == 0,
                                    k == KD - 1)
                    mm.then_inc(q_ready[s], 1)
                for s in range(2):
                    pe.wait_ge(q_there[s], LEAD + h + 1)
                    pe.wait_ge(s_taken[s], LEAD + h)
                    for m in range(NT):
                        mm = pe.matmul(bank_s[s][:, m * P:(m + 1) * P], qT[s][:, m * P:(m + 1) * P],
                                       keys[:, ds(h * 2 + s, 1), :].rearrange("p a n -> p (a n)"),
                                       start=True, stop=True)
                    mm.then_inc(s_ready[s], 1)
                for q in range(4):
                    b = q % 2
                    pe.wait_ge(u_low[b], LEAD + used(h, q) + 1)
                    pe.wait_ge(h_taken[b], LEAD + used(h, q))
                    for k in range(KD):
                        mm = passes(pe, bank_h[b][:], [u[:, k * P:(k + 1) * P] for u in u_half[b]],
                                    [m[:, k, :] for m in xs], k == 0, k == KD - 1)
                    mm.then_inc(h_done[b], 1)

        @block.gpsimd
        def _(pool):
            def columns(h):
                for s in range(2):
                    pool.wait_ge(high[s], h + 1)
                    pool.tensor_tensor(wb[s][1][:], raw[s][:], wb[s][0][:].bitcast(F32),
                                       ALU.subtract).then_inc(low[s], 1)

            def head(h, more):
                for q in range(4):
                    b = q % 2
                    pool.wait_ge(u_high[b], used(h, q) + 1)
                    pool.tensor_tensor(u_half[b][1][:], u_raw[b][:], u_half[b][0][:].bitcast(F32),
                                       ALU.subtract).then_inc(u_low[b], 1)
                if more:
                    columns(h + 1)

            trips(pool, head, lambda: columns(0))

        @block.scalar
        def _(act):
            def columns(h):
                for s in range(2):
                    act.wait_ge(wq_in[s], h * 16 + 16)
                    act.wait_ge(q_ready[s], LEAD + h)
                    act.copy(wb[s][0][:], raw[s][:]).then_inc(high[s], 1)

            def split(h, q):
                b = q % 2
                act.wait_ge(u_in[b], used(h, q) * 16 + 16)
                act.wait_ge(h_done[b], LEAD + used(h, q))
                act.copy(u_half[b][0][:], u_raw[b][:]).then_inc(u_high[b], 1)

            def gelu(h, q):
                b = q % 2
                act.wait_ge(h_done[b], LEAD + used(h, q) + 1)
                act.wait_ge(h_stored[b], LEAD + used(h, q) * 16)
                act.activation(hid[b][:], bank_h[b][:], ACT.Gelu_apprx_tanh).then_inc(h_taken[b], 1)
                act.wait_ge(h_taken[b], LEAD + used(h, q) + 1)
                act.dma_start(hmat[ds(h * 4 + q, 1)].rearrange("o a t -> a (o t)"), hid[b][:])\
                   .then_inc(h_stored[b], 16)

            def head(h, more):
                split(h, 0)
                split(h, 1)
                for s in range(2):
                    act.wait_ge(q_ready[s], LEAD + h + 1)
                    act.wait_ge(s_ready[s], LEAD + h)
                    act.copy(qT[s][:], bank_q[s][:]).then_inc(q_there[s], 1)
                for q in range(4):
                    if q == 2 and more:
                        columns(h + 1)
                    gelu(h, q)
                    if q < 2:
                        split(h, q + 2)

            trips(act, head, lambda: columns(0))
            act.wait_ge(e_ready, 1)
            act.activation(gates[:], gates[:], ACT.Exp).then_inc(e_there, 1)
            for b in range(2):
                act.wait_ge(h_stored[b], LEAD + PEER_H * 2 * 16)

        @block.vector
        def _(v):
            ch = Chain(v, dve)
            c.there(v)

            def sync():
                v.wait_ge(dve, ch.n + ch.off)
                v.memset(wait_taker[:], 0.0)

            def best16(src, spare, values, indices, done=None):
                for m in range(NT):
                    ch.put(v.max(values[:, m, 0:8], src(m)))
                sync()
                for m in range(NT):
                    ch.put(v.max_index(indices[:, m, 0:8], values[:, m, 0:8], src(m)))
                for m in range(NT):
                    ins = v.match_replace(spare(m), values[:, m, 0:8], src(m), TAKEN)
                    if m < NT - 1 or done is None:
                        ch.put(ins)
                    else:
                        ins.then_inc(done[0], 1)
                        v.wait_ge(done[0], done[1])
                sync()
                for m in range(NT):
                    ch.put(v.max(values[:, m, 8:T], spare(m)))
                sync()
                for m in range(NT):
                    ch.put(v.max_index(indices[:, m, 8:T], values[:, m, 8:T], spare(m)))
                v.wait_ge(dve, ch.n + ch.off)

            with v.Fori(0, PEER_H) as h:
                ch.enter(h, 2 * (5 * NT - 1 + 1) + NT + 5 * NT + 2 + 4 * 2 + 1)
                for s in range(2):
                    v.wait_ge(s_ready[s], LEAD + h + 1)
                    v.memset(wait_taker[:], 0.0)
                    best16(lambda m: bank_s[s][:, m * P:(m + 1) * P], lambda m: work[:, m, :], val[s], idx[s],
                           (s_taken[s], LEAD + h + 1))
                    ch.put(v.tensor_copy(idf[s][:], idx[s][:]))
                for m in range(NT):
                    ch.put(v.tensor_tensor(cand[:, m, :].rearrange("p (a b) -> p a b", b=T),
                                           bc(val[0][:, m, :], 2, T), bc(val[1][:, m, :], 1, T), ALU.add))
                sync()
                best16(lambda m: cand[:, m, :], lambda m: rest[:, m, :], top, pos)
                ch.put(v.tensor_scalar(place[0][:], pos[:], 4, None, ALU.logical_shift_right))
                ch.link(v.tensor_scalar(place[1][:], pos[:], T - 1, None, ALU.bitwise_and))
                for s, e in ((0, rows), (1, cols)):
                    ch.link(v.tensor_copy(placef[s][:], place[s][:]))
                    ch.link(v.tensor_tensor(onehot[:], bc(placef[s][:], 3, T),
                                            c["iota"][:, 0:T].unsqueeze(1).unsqueeze(1).broadcast_to([P, NT, T, T]),
                                            ALU.is_equal))
                    ch.link(v.tensor_tensor(onehot[:], onehot[:], bc(idf[s][:], 2, T), ALU.mult))
                    ch.link(v.tensor_reduce(e[:, :, ds(h * T, T)], onehot[:], AX.X, ALU.add))
                ch.put(v.tensor_copy(gates[:, :, ds(h * T, T)], top[:]))
                v.wait_ge(dve, ch.n + ch.off)
            ch.leave(PEER_H)
            g4 = gates[:].rearrange("p m (h k) -> p m h k", k=T)
            full = [P, NT, PEER_H, T]
            ch.link(v.tensor_copy(peak[:], g4[:, :, :, 0:1]))
            v.tensor_tensor(g4, g4, peak[:].broadcast_to(full), ALU.subtract).then_inc(e_ready, 1)
            v.wait_ge(e_there, 1)
            ch.link(v.tensor_reduce(peak[:].rearrange("p m h o -> p m (h o)"), g4, AX.X, ALU.add))
            ch.link(v.reciprocal(peak[:], peak[:]))
            ch.link(v.tensor_tensor(g4, g4, peak[:].broadcast_to(full), ALU.mult))


def spread_gates(nc, c, tag, gT, rT, cT, gmat, xs, uT, hmat):
    FEW, GROUPS = 4, 4
    STEP = FEW * GROUPS
    trips = PART_T // STEP
    with Tiles(nc, tag) as t:
        wide = [t.sb(f"wide{s}", [P, PEER_K, PART_T]) for s in range(2)]
        left, right = [[t.sb(f"{n}{g}", [P, FEW, P]) for g in range(GROUPS)] for n in ("left", "right")]
        bank = t.banks("g", GROUPS)
        made, gated, spread, taken, stored = [
            t.leads(n, GROUPS) for n in ("made", "gated", "spread", "taken", "stored")]
        u_raw, hid = [[t.sb(f"{n}{b}", [P, w]) for b in range(m)] for n, w, m in (("u", D, trips), ("hid", SEQ, 2))]
        u_half = [halves(t, f"uh{b}", [P, D]) for b in range(2)]
        bank_h = t.banks("h", 2)
        u_in, u_high, u_low = t.sems("u_in", trips), t.sems("u_high", 2), [t.lead(f"u_low{b}", 2) for b in range(2)]
        h_done, h_taken, h_stored = [t.leads(n, 2) for n in ("h_done", "h_taken", "h_stored")]
        block = t.block()
        EARLY = SEQ // STEP

        def walk(eng, body, before=lambda *now: None, after=lambda *now: None):
            with eng.Fori(0, PARTS // 2) as o:
                for s in range(2):
                    part = o * 2 + s
                    for j in range(trips):
                        n = part * trips + j
                        now = n, part, j, part * (trips // 2) + j // 2, j % 2
                        before(*now)
                        for g in range(GROUPS):
                            at = j * STEP + g * FEW
                            body(part * PART_T + at, at, n, o, s, g)
                        after(*now)

        @block.vector
        def _(v):
            c.there(v)
            iota = bc(c["iota"][:], 1, FEW)

            def body(tok, at, n, o, s, g):
                v.wait_ge(spread[g], LEAD + n)
                v.tensor_tensor(left[g][:], iota, bc(rT[:, ds(tok, FEW)], 2, P), ALU.is_equal).then_inc(made[g], 1)
                v.tensor_tensor(right[g][:], iota, bc(cT[:, ds(tok, FEW)], 2, P), ALU.is_equal).then_inc(made[g], 1)

            def split(n, part, j, used, b):
                v.wait_ge(u_in[j], part * 16 + 16)
                v.wait_ge(h_done[b], LEAD + used)
                v.tensor_copy(u_half[b][0][:], u_raw[j][:]).then_inc(u_high[b], 1)
                v.wait_ge(u_high[b], used + 1)
                v.tensor_tensor(u_half[b][1][:], u_raw[j][:], u_half[b][0][:].bitcast(F32),
                                ALU.subtract).then_inc(u_low[b], 1)

            walk(v, body, before=split)

        @block.gpsimd
        def _(pool):
            def body(tok, at, n, o, s, g):
                pool.wait_ge(made[g], LEAD + n * 2 + 1)
                pool.tensor_tensor(left[g][:], left[g][:], bc(gT[:, ds(tok, FEW)], 2, P),
                                   ALU.mult).then_inc(gated[g], 1)
            walk(pool, body)

        @block.tensor
        def _(pe):
            def body(tok, at, n, o, s, g):
                pe.wait_ge(gated[g], LEAD + n + 1)
                pe.wait_ge(made[g], LEAD + n * 2 + 2)
                pe.wait_ge(taken[g], LEAD + n)
                for q in range(FEW):
                    mm = pe.matmul(bank[g][:, q * P:(q + 1) * P], left[g][:, q, :], right[g][:, q, :], start=True,
                                   stop=True)
                mm.then_inc(spread[g], 1)

            def early(n, part, j, used, b):
                pe.wait_ge(u_low[b], 2 + used + 1)
                pe.wait_ge(h_taken[b], LEAD + used)
                for k in range(KD):
                    mm = passes(pe, bank_h[b][:], [u[:, k * P:(k + 1) * P] for u in u_half[b]],
                                [m[:, k, :] for m in xs], k == 0, k == KD - 1)
                mm.then_inc(h_done[b], 1)

            walk(pe, body, after=early)

        @block.scalar
        def _(act):
            def body(tok, at, n, o, s, g):
                act.wait_ge(spread[g], LEAD + n + 1)
                act.wait_ge(stored[s], LEAD + o * 16)
                act.copy(wide[s][:, :, ds(at, FEW)],
                         bank[g][:].rearrange("p (q b) -> p b q", q=FEW)).then_inc(taken[g], 1)
                if at == PART_T - FEW:
                    for k in range(GROUPS):
                        act.wait_ge(taken[k], LEAD + n + 1)
                    act.dma_start(gmat[ds(o * 2 + s, 1)].rearrange("o a b t -> a (o b t)"),
                                  wide[s][:].rearrange("a b t -> a (b t)")).then_inc(stored[s], 16)

            def gelu(n, part, j, used, b):
                act.wait_ge(h_done[b], LEAD + used + 1)
                act.wait_ge(h_stored[b], LEAD + used * 16)
                act.activation(hid[b][:], bank_h[b][:], ACT.Gelu_apprx_tanh).then_inc(h_taken[b], 1)
                act.wait_ge(h_taken[b], LEAD + used + 1)
                act.dma_start(hmat[ds(n + EARLY, 1)].rearrange("o a t -> a (o t)"), hid[b][:])\
                   .then_inc(h_stored[b], 16)

            walk(act, body, after=gelu)
            for b in range(2):
                act.wait_ge(h_stored[b], LEAD + EARLY // 2 * 16)

        @block.sync
        def _(sp):
            with sp.Fori(0, PARTS // 2) as o:
                for s in range(2):
                    part = o * 2 + s
                    for j in range(trips):
                        used, b = part * (trips // 2) + j // 2, j % 2
                        sp.wait_ge(u_low[b], 2 + used - 1)
                        sp.dma_start(u_raw[j][:], uT[ds((part * trips + j + EARLY) * 2 + 1, 1)]
                                     .rearrange("o a d -> a (o d)")).then_inc(u_in[j], 16)
            for s in range(2):
                sp.wait_ge(stored[s], LEAD + 16 * (PARTS // 2))


class Set:

    def __init__(self, n, quad, j):
        self.n, self.quad, self.j = n, quad, j
        self.early, self.order, self.place = j % 2 == 1, quad * 2 + j % 4 // 2, j // 2 % 2

    def __add__(self, k):
        return Set(self.n + k, self.quad + (self.j % 4 + k) // 4, (self.j + k) % 8)

    def from_(self, k):
        return not isinstance(self.n, int) or self.n >= k


def all_experts(nc, c, tag, xs, uT, v_tab, gmat, hmat, x):
    SETS, PART, OUTS = PEER_K, 4, NT * 2
    BODY = 2 * PART
    trips = (SETS - BODY) // BODY
    last = PART + trips * BODY
    v_view = v_tab.rearrange("(a b) d -> b a d", b=PEER_K)
    with Tiles(nc, tag) as t:
        u_raw, v_raw = [[t.sb(f"{n}{j}", [P, D]) for j in range(m)] for n, m in (("ur", 2), ("vr", PART))]
        u_half = [[t.sb(f"u{j}{half}", [P, D], F32R) for half in "hl"] for j in range(2)]
        v_half = [[t.sb(f"v{j}{half}", [P, D], F32R) for half in "hl"] for j in range(PART)]
        g_raw = [t.sb(f"g{j}", [P, SEQ]) for j in range(PART)]
        hid, hid_early = [[t.sb(f"{n}{j}", [P, SEQ]) for j in range(2)] for n in ("hid", "early")]
        prod = [t.sb(f"prod{j}", [P, SEQ]) for j in range(2)]
        p_half = [[t.sb(f"p{j}{half}", [P, SEQ], F32R) for half in "hl"] for j in range(BODY)]
        y = t.sb("y", [P, NT, D])
        bank_h, bank_y = t.banks("hb", 2), t.banks("yb", 4)
        u_in, v_in, g_in, early_in = t.sems("u_in", 2), t.sems("v_in", PART), t.sems("g_in", PART), t.sems("early_in", 2)
        uh_made, ul_made, vh_made, ph_made, pl_made = [
            t.sem(n) for n in ("uh_made", "ul_made", "vh_made", "ph_made", "pl_made")]
        h_ready, hid_made, prod_made, cleared = [t.sem(n) for n in ("h_ready", "hid_made", "prod_made", "cleared")]
        vl_made, y_ready, y_taken = t.lead("vl_made", PART), t.lead("y_ready", OUTS), t.lead("y_taken", OUTS)
        block = t.block()

        def goes_on(s):
            return not isinstance(s.n, int) or s.n < SETS - PART

        def walk(eng, hidden, output, behind=lambda s: None):
            def all_behind(s):
                if s.j % PART == 0:
                    for k in range(PART):
                        behind(s + k)

            for k in range(PART):
                hidden(Set(k, 0, k))
            with eng.Fori(0, trips) as i:
                for j in range(BODY):
                    s = Set(i * BODY + j, i * 2 + j // PART, j)
                    all_behind(s)
                    hidden(s + PART)
                    if j % PART == PART - 1:
                        output(s)
            for k in range(BODY):
                s = Set(last - PART + k, last // PART - 1 + k // PART, k)
                all_behind(s)
                if k < PART:
                    hidden(s + PART)
                if k % PART == PART - 1:
                    output(s)

        @block.gpsimd
        def _(pool):
            pool.memset(y[:], 0.0).then_inc(cleared, 1)

        @block.sync
        def _(sp):
            def load(buf, src, done, at, row):
                sp.dma_start(buf[at][:], src[ds(row, 1)].rearrange("o a d -> a (o d)")).then_inc(done[at], 16)

            def ahead(s):
                if not s.early and goes_on(s):
                    sp.wait_ge(ul_made, s.order + 1)
                    load(u_raw, uT, u_in, s.place, s.n + PART)
                if s.from_(PART):
                    sp.wait_ge(prod_made, s.n - PART + 1)
                sp.dma_start(g_raw[s.j % PART][:].rearrange("a (o t) -> a o t", t=PART_T),
                             gmat[:, :, ds(s.n, 1), :].rearrange("o a b t -> a o (b t)"))\
                  .then_inc(g_in[s.j % PART], 16)
                if s.early:
                    load(hid_early, hmat, early_in, s.place, s.order)

            def values(s):
                sp.wait_ge(vl_made, s.n + 1)
                load(v_raw, v_view, v_in, s.j % PART, s.n)

            for k in range(2):
                load(u_raw, uT, u_in, k, 2 * k)
            for k in range(PART):
                ahead(Set(k, 0, k))
            walk(sp, lambda s: ahead(s) if s.from_(PART) else None, lambda s: None, values)

        @block.tensor
        def _(pe):
            def hidden(s):
                if s.early:
                    return
                pe.wait_ge(ul_made, s.order + 1)
                if s.from_(PART):
                    pe.wait_ge(hid_made, s.order - 1)
                for k in range(KD):
                    mm = passes(pe, bank_h[s.place][:], [h[:, k * P:(k + 1) * P] for h in u_half[s.place]],
                                [h[:, k, :] for h in xs], k == 0, k == KD - 1)
                mm.then_inc(h_ready, 1)

            def output(s):
                pe.wait_ge(pl_made, s.n + 1)
                pe.wait_ge(vl_made, PART + s.n + 1)
                for o in range(OUTS):
                    m, half = o // 2, o % 2
                    pe.wait_ge(y_taken, OUTS + s.quad * OUTS + o - 3)
                    for k in range(PART):
                        mm = passes(pe, bank_y[o % 4][:],
                                    [h[:, m * P:(m + 1) * P] for h in p_half[s.j // PART * PART + k]],
                                    [h[:, half * 512:(half + 1) * 512] for h in v_half[k]], k == 0, k == PART - 1)
                    mm.then_inc(y_ready, 1)

            walk(pe, hidden, output)

        @block.scalar
        def _(act):
            def split_u(s):
                act.wait_ge(u_in[s.place], s.quad * 16 + 16)
                if s.from_(PART):
                    act.wait_ge(h_ready, s.order - 1)
                act.copy(u_half[s.place][0][:], u_raw[s.place][:]).then_inc(uh_made, 1)

            def hidden(s):
                if not s.early:
                    if goes_on(s):
                        split_u(s + PART)
                    act.wait_ge(h_ready, s.order + 1)
                    if s.from_(PART):
                        act.wait_ge(prod_made, s.n - PART + 1)
                    act.activation(hid[s.place][:], bank_h[s.place][:],
                                   ACT.Gelu_apprx_tanh).then_inc(hid_made, 1)
                act.wait_ge(prod_made, s.n + 1)
                if s.from_(BODY):
                    act.wait_ge(y_ready, s.quad * OUTS)
                act.copy(p_half[s.j][0][:], prod[s.j % 2][:]).then_inc(ph_made, 1)

            def behind(s):
                act.wait_ge(v_in[s.j % PART], s.quad * 16 + 16)
                act.wait_ge(y_ready, OUTS + s.quad * OUTS)
                act.copy(v_half[s.j % PART][0][:], v_raw[s.j % PART][:]).then_inc(vh_made, 1)

            split_u(Set(0, 0, 0))
            split_u(Set(2, 0, 2))
            walk(act, hidden, lambda s: None, behind)

        @block.vector
        def _(v):
            def low(halves, raw, n, made, done):
                v.wait_ge(made, n + 1)
                v.tensor_tensor(halves[1][:], raw[:], halves[0][:].bitcast(F32), ALU.subtract).then_inc(done, 1)

            def hidden(s):
                if s.early:
                    v.wait_ge(early_in[s.place], s.quad * 16 + 16)
                else:
                    if goes_on(s):
                        u = s + PART
                        low(u_half[u.place], u_raw[u.place], u.order, uh_made, ul_made)
                    v.wait_ge(hid_made, s.order + 1)
                v.wait_ge(g_in[s.j % PART], s.quad * 16 + 16)
                v.tensor_tensor(prod[s.j % 2][:], (hid_early if s.early else hid)[s.place][:], g_raw[s.j % PART][:],
                                ALU.mult).then_inc(prod_made, 1)
                low(p_half[s.j], prod[s.j % 2], s.n, ph_made, pl_made)

            def output(s):
                for o in range(OUTS):
                    part = y[:, o // 2, (o % 2) * 512:(o % 2 + 1) * 512]
                    v.wait_ge(y_ready, OUTS + s.quad * OUTS + o + 1)
                    v.wait_ge(y_taken, s.quad * OUTS + o + 1)
                    v.tensor_tensor(part, bank_y[o % 4][:], part, ALU.add).then_inc(y_taken, 1)

            v.wait_ge(cleared, 1)
            for k in range(2):
                low(u_half[k], u_raw[k], k, uh_made, ul_made)
            walk(v, hidden, output,
                 lambda s: low(v_half[s.j % PART], v_raw[s.j % PART], s.n, vh_made, vl_made))
            v.wait_ge(y_taken, OUTS + SETS // PART * OUTS)
            v.tensor_tensor(x[:], x[:], y[:], ALU.add)


def peer(nc, c, tag, x, a, l):
    gmat = nc.dram_tensor(f"{tag}_gmat", (PARTS, PEER_K, PEER_K, PART_T), F32, kind="Internal").ap()
    hmat = nc.dram_tensor(f"{tag}_hmat", (PEER_K // 2, PEER_K, SEQ), F32, kind="Internal").ap()
    with Tiles(nc, tag) as keep:
        xs = halves(keep, "xs", [P, KD, SEQ])
        normed_transpose(nc, c, tag + "n", x, a[f"{l}_ffn_norm"], xs)
        with Tiles(nc, tag + "g") as t:
            turned = [t.sb(n, [P, SEQ]) for n in ("gT", "rT", "cT")]
            with Tiles(nc, tag + "r") as t2:
                parts = [t2.sb(n, [P, NT, P]) for n in ("gates", "rows", "cols")]
                retrieve(nc, c, tag + "q", xs, a[f"{l}_peer_wq"], a[f"{l}_peer_subkeysT"], *parts,
                         a[f"{l}_peer_uT"], hmat)
                turn(nc, c, tag + "t", [(d[:], [p[:, m, :] for m in range(NT)], P) for d, p in zip(turned, parts)])
            spread_gates(nc, c, tag + "s", *turned, gmat, xs, a[f"{l}_peer_uT"], hmat)
        all_experts(nc, c, tag + "e", xs, a[f"{l}_peer_uT"], a[f"{l}_peer_v"], gmat, hmat, x)


def store(nc, c, tag, x, out):
    with Tiles(nc, tag) as t:
        stored = t.sem("stored")
        block = t.block()

        @block.sync
        def _(sp):
            sp.dma_start(out.rearrange("(t p) d -> p t d", p=P), x[:]).then_inc(stored, 16)
            sp.wait_ge(stored, 16)


def trunk(nc, a, tables, out):
    with Tiles(nc, "all") as t:
        c = Consts(nc, t, tables)
        x = t.sb("x", [P, NT, D])
        load_all(nc, t, c, a["x"], x)
        layer0_mixer(nc, c, x, a)
        end_half(nc)
        peer(nc, c, "f0", x, a, "l0")
        end_half(nc)
        layer1_mixer(nc, c, x, a)
        end_half(nc)
        peer(nc, c, "f1", x, a, "l1")
        store(nc, c, "out", x, out)


def host_tables():
    f = np.float32
    half = HD // 2
    inv = (f(10000.0) ** (-np.arange(half, dtype=f) / f(half))).astype(f)

    def rope(pos):
        ang = pos.astype(f)[:, None] * inv[None, :]
        return np.cos(ang).astype(f), np.sin(ang).astype(f)

    cos, sin = rope(np.arange(SEQ))
    tiles = lambda m: np.ascontiguousarray(m.reshape(NT, P, half).transpose(1, 0, 2))
    pos = np.tile(np.arange(32) * CMP_STRIDE + CMP_LEN - 1, 2)
    ccos, csin = rope(pos)
    i = np.arange(P)
    same = (i[:, None] // GLA_C) == (i[None, :] // GLA_C)
    tq = np.arange(SEQ).reshape(NT, P).T
    cmask = ((np.arange(32) * CMP_STRIDE + CMP_LEN - 1)[None, None, :] <= tq[:, :, None]).astype(f)
    return {
        "ident": np.eye(P, dtype=f),
        "causal": np.where(i[None, :] <= i[:, None], 0.0, NEG).astype(f),
        "cos": tiles(cos), "sin": tiles(sin),
        "ccos": ccos[:, None, :], "csin": csin[:, None, :],
        "cmask": cmask, "cbias": np.where(cmask > 0, 0.0, NEG).astype(f),
        "upto": (same & (i[:, None] <= i[None, :])).astype(f),
        "after": (same & (i[:, None] > i[None, :])).astype(f),
        "chunk": ((i[:, None] // GLA_C) == np.arange(4)[None, :]).astype(f),
        "iota": np.tile(np.arange(P, dtype=f), (P, 1)),
    }


def lay_out(inputs):
    f = {k: np.asarray(v) for k, v in inputs.items()}
    out = {k: np.ascontiguousarray(v) for k, v in f.items() if not k.startswith("l0_s5") and not k.endswith("_peer_u")
           and not k.endswith("_peer_subkeys")}
    out["x"] = f["x"].reshape(SEQ, D)
    out["l0_s5_w_glu"] = f["l0_s5_w_glu"]

    def states(m):
        m = m.reshape(S5_GP, 2, *m.shape[1:])
        m = np.moveaxis(m, 0, 2)
        return np.ascontiguousarray(m.reshape(P, *m.shape[2:]))

    out["log_dt"] = states(np.repeat(f["l0_s5_log_dt"][:, None], S5_P, axis=1))
    out["a_re"], out["a_im"] = states(f["l0_s5_a_re"]), states(f["l0_s5_a_im"])
    out["b_re"], out["b_im"] = states(f["l0_s5_b_re"]), states(f["l0_s5_b_im"])
    out["c_re"] = states(np.swapaxes(f["l0_s5_c_re"], 1, 2))
    out["c_im"] = states(np.swapaxes(f["l0_s5_c_im"], 1, 2))
    out["d_skip"] = np.ascontiguousarray(f["l0_s5_d"].T)
    out["b_glu"] = np.ascontiguousarray(f["l0_s5_b_glu"].reshape(4, P).T)
    out["l1_nsa_cmp_pos"] = np.ascontiguousarray(f["l1_nsa_cmp_pos"].T)
    for l in ("l0", "l1"):
        u = f[f"{l}_peer_u"].reshape(PEER_K, PEER_K, KD, P)
        out[f"{l}_peer_uT"] = np.ascontiguousarray(u.transpose(1, 3, 2, 0)).reshape(PEER_K, P, D)
        sk = f[f"{l}_peer_subkeys"].reshape(NLIST, PEER_K, P)
        out[f"{l}_peer_subkeysT"] = np.ascontiguousarray(sk.transpose(2, 0, 1))
    return out


def kernel(**inputs):
    import concourse.bacc as bacc
    from concourse.bass_utils import run_bass_kernel_spmd as run

    nc = bacc.Bacc("TRN2", target_bir_lowering=False, num_devices=1)
    arrays = lay_out(inputs)
    tables = host_tables()
    aps = {k: nc.dram_tensor(k, v.shape, mybir.dt.from_np(v.dtype), kind="ExternalInput").ap()
           for k, v in arrays.items()}
    taps = {k: nc.dram_tensor(f"table_{k}", v.shape, F32, kind="ExternalInput").ap() for k, v in tables.items()}
    out = nc.dram_tensor("out", (SEQ, D), F32, kind="ExternalOutput").ap()
    trunk(nc, aps, taps, out)
    r = run(nc, [{**arrays, **{f"table_{k}": v for k, v in tables.items()}}], core_ids=[0])
    return r.results[0]["out"].reshape(1, SEQ, D)
```
